# Optimizing a Trainium2 kernel written in Bass

```python
import math
import jax, jax.numpy as jnp
from jax import lax
import numpy as np

D_MODEL = 2048
BATCH = 1
SEQ = 256
DEPTH = 1

ALPHA = (2.0 * DEPTH) ** 0.25
BETA = (8.0 * DEPTH) ** -0.25
LN_EPS = 1e-5
RMS_EPS = 1e-5

SSD_D_INNER = 2 * D_MODEL
SSD_HEAD_DIM = 64
SSD_N_HEADS = SSD_D_INNER // SSD_HEAD_DIM
SSD_N_GROUPS = 8
SSD_HEADS_PER_GROUP = SSD_N_HEADS // SSD_N_GROUPS
SSD_D_STATE = 128
SSD_CONV_W = 4
SSD_CONV_DIM = SSD_D_INNER + 2 * SSD_N_GROUPS * SSD_D_STATE
SSD_CHUNK = 128

GLA_N_HEADS = 4
GLA_D_KEY = D_MODEL // 2
GLA_D_VALUE = D_MODEL
GLA_HEAD_K = GLA_D_KEY // GLA_N_HEADS
GLA_HEAD_V = GLA_D_VALUE // GLA_N_HEADS
GLA_GATE_RANK = 16
GLA_GATE_NORMALIZER = 16.0
GLA_CHUNK = 64

D_FF = 4 * D_MODEL

IN_SPLIT_SIZES = (SSD_D_INNER, SSD_CONV_DIM, SSD_N_HEADS, GLA_D_KEY, GLA_D_KEY, GLA_D_VALUE, GLA_D_VALUE, GLA_GATE_RANK, D_MODEL, D_MODEL)
D_IN_PROJ = SSD_D_INNER + SSD_CONV_DIM + SSD_N_HEADS + 2 * GLA_D_KEY + 2 * GLA_D_VALUE + GLA_GATE_RANK + 2 * D_MODEL


def _split_cols(a, sizes):
    idx = np.cumsum(np.array(sizes))[:-1].tolist()
    return jnp.split(a, idx, axis=-1)

def layer_norm(x, g, b):
    xf = x.astype(jnp.float32)
    mu = jnp.mean(xf, axis=-1, keepdims=True)
    xc = xf - mu
    var = jnp.mean(xc * xc, axis=-1, keepdims=True)
    y = xc * lax.rsqrt(var + LN_EPS) * g.astype(jnp.float32) + b.astype(jnp.float32)
    return y.astype(x.dtype)

def grouped_rms_norm(y, w, n_groups):
    shp = y.shape
    yf = y.astype(jnp.float32).reshape(shp[:-1] + (n_groups, shp[-1] // n_groups))
    yf = yf * lax.rsqrt(jnp.mean(yf * yf, axis=-1, keepdims=True) + RMS_EPS)
    return (yf.reshape(shp) * w.astype(jnp.float32)).astype(y.dtype)

def causal_depthwise_conv(u, w, b):
    out = lax.conv_general_dilated(
        u, w[:, None, :].astype(u.dtype), window_strides=(1,),
        padding=[(SSD_CONV_W - 1, 0)], dimension_numbers=('NWC', 'WIO', 'NWC'),
        feature_group_count=u.shape[-1])
    return out + b.astype(u.dtype)

def ssd_chunked(xh, dt, A, Bm, Cm):
    Bsz, L = xh.shape[0], xh.shape[1]
    Q = SSD_CHUNK
    nc = L // Q
    G, Hg, P, N = SSD_N_GROUPS, SSD_HEADS_PER_GROUP, SSD_HEAD_DIM, SSD_D_STATE
    x = xh.reshape(Bsz, nc, Q, G, Hg, P)
    dtc = dt.reshape(Bsz, nc, Q, G, Hg)
    Bc = Bm.reshape(Bsz, nc, Q, G, N)
    Cc = Cm.reshape(Bsz, nc, Q, G, N)
    a_cs = jnp.cumsum(dtc * A.reshape(G, Hg), axis=2)
    xdt = x * dtc[..., None]
    mask = jnp.tril(jnp.ones((Q, Q), dtype=bool))[:, :, None, None]
    seg = a_cs[:, :, :, None] - a_cs[:, :, None, :]
    decay = jnp.exp(jnp.where(mask, seg, -jnp.inf))
    cb = jnp.einsum('bcign,bcjgn->bcijg', Cc, Bc)
    y_diag = jnp.einsum('bcijgh,bcjghp->bcighp', cb[..., None] * decay, xdt)
    a_last = a_cs[:, :, -1]
    xw = xdt * jnp.exp(a_last[:, :, None] - a_cs)[..., None]
    states = jnp.einsum('bcjgn,bcjghp->bcghpn', Bc, xw)

    def step(carry, inp):
        st, al = inp
        new = carry * jnp.exp(al)[..., None, None] + st
        return new, carry

    init = jnp.zeros((Bsz, G, Hg, P, N), dtype=states.dtype)
    _, prev = lax.scan(step, init, (jnp.moveaxis(states, 1, 0), jnp.moveaxis(a_last, 1, 0)))
    prev = jnp.moveaxis(prev, 0, 1)
    y_off = jnp.einsum('bcign,bcghpn->bcighp', Cc, prev) * jnp.exp(a_cs)[..., None]
    return (y_diag + y_off).reshape(Bsz, L, SSD_N_HEADS, P)

def gla_chunked(q, k, v, gk):
    Bsz, L = q.shape[0], q.shape[1]
    C = GLA_CHUNK
    nc = L // C
    H, K, V = GLA_N_HEADS, GLA_HEAD_K, GLA_HEAD_V
    scale = K ** -0.5
    qc = q.reshape(Bsz, nc, C, H, K)
    kc = k.reshape(Bsz, nc, C, H, K)
    vc = v.reshape(Bsz, nc, C, H, V)
    G = jnp.cumsum(gk.reshape(Bsz, nc, C, H, K), axis=2)
    G_last = G[:, :, -1:]
    qg = qc * scale * jnp.exp(G)
    kg = kc * jnp.exp(-G)
    kd = kc * jnp.exp(G_last - G)
    att = jnp.einsum('bcihk,bcjhk->bchij', qg, kg)
    att = jnp.where(jnp.tril(jnp.ones((C, C), dtype=bool)), att, 0.0)
    o_intra = jnp.einsum('bchij,bcjhv->bcihv', att, vc)

    def step(S, inp):
        q_i, k_i, v_i, d_i = inp
        o = jnp.einsum('bihk,bhkv->bihv', q_i, S)
        S = S * d_i[..., None] + jnp.einsum('bjhk,bjhv->bhkv', k_i, v_i)
        return S, o

    init = jnp.zeros((Bsz, H, K, V), dtype=q.dtype)
    xs = (jnp.moveaxis(qg, 1, 0), jnp.moveaxis(kd, 1, 0), jnp.moveaxis(vc, 1, 0),
          jnp.moveaxis(jnp.exp(G_last[:, :, 0]), 1, 0))
    _, o_inter = lax.scan(step, init, xs)
    o_inter = jnp.moveaxis(o_inter, 0, 1)
    return (o_intra + o_inter).reshape(Bsz, L, H, V)

def hybrid_mixer(h, w_in, ssd_conv_w, ssd_conv_b, ssd_dt_bias, ssd_A_log, ssd_D, ssd_norm_w,
                 gla_gk_w, gla_gk_b, gla_norm_w, w_ssd_branch, w_gla_branch, gate_bias, w_out):
    f32 = jnp.float32
    Bsz, L, _ = h.shape
    proj = h @ w_in
    z, xbc, dt_raw, q, k, v, g, gk_lr, gate_ssd, gate_gla = _split_cols(proj, IN_SPLIT_SIZES)

    xbc = jax.nn.silu(causal_depthwise_conv(xbc, ssd_conv_w, ssd_conv_b))
    xs, Bm, Cm = _split_cols(xbc, (SSD_D_INNER, SSD_N_GROUPS * SSD_D_STATE, SSD_N_GROUPS * SSD_D_STATE))
    xh = xs.reshape(Bsz, L, SSD_N_HEADS, SSD_HEAD_DIM).astype(f32)
    dt = jax.nn.softplus(dt_raw.astype(f32) + ssd_dt_bias.astype(f32))
    A = -jnp.exp(ssd_A_log.astype(f32))
    y = ssd_chunked(xh, dt, A,
                    Bm.reshape(Bsz, L, SSD_N_GROUPS, SSD_D_STATE).astype(f32),
                    Cm.reshape(Bsz, L, SSD_N_GROUPS, SSD_D_STATE).astype(f32))
    y = y + ssd_D.astype(f32)[:, None] * xh
    y = y.reshape(Bsz, L, SSD_D_INNER).astype(h.dtype)
    y = grouped_rms_norm(y * jax.nn.silu(z), ssd_norm_w, SSD_N_GROUPS)

    gk = jax.nn.log_sigmoid((gk_lr @ gla_gk_w + gla_gk_b).astype(f32)) / GLA_GATE_NORMALIZER
    o = gla_chunked(q.reshape(Bsz, L, GLA_N_HEADS, GLA_HEAD_K).astype(f32),
                    k.reshape(Bsz, L, GLA_N_HEADS, GLA_HEAD_K).astype(f32),
                    v.reshape(Bsz, L, GLA_N_HEADS, GLA_HEAD_V).astype(f32),
                    gk.reshape(Bsz, L, GLA_N_HEADS, GLA_HEAD_K))
    o = grouped_rms_norm(o.astype(h.dtype), gla_norm_w, 1) * jax.nn.silu(g).reshape(Bsz, L, GLA_N_HEADS, GLA_HEAD_V)
    o = o.reshape(Bsz, L, GLA_D_VALUE)

    branch_ssd = y @ w_ssd_branch
    branch_gla = o @ w_gla_branch
    merged = (jax.nn.sigmoid(gate_ssd + gate_bias[0]) * branch_ssd
              + jax.nn.sigmoid(gate_gla + gate_bias[1]) * branch_gla)
    return merged @ w_out

def squared_relu_mlp(h, w_up, w_down):
    return jnp.square(jax.nn.relu(h @ w_up)) @ w_down

def first_inputs(seed: int = 0) -> dict:
    key = jax.random.key(seed)
    ks = jax.random.split(key, 21)
    nrm = jax.random.normal
    H = SSD_N_HEADS
    x = nrm(ks[0], (BATCH, SEQ, D_MODEL), jnp.float32)
    w_in = nrm(ks[1], (DEPTH, D_MODEL, D_IN_PROJ), jnp.float32) * D_MODEL ** -0.5
    ssd_conv_w = nrm(ks[2], (DEPTH, SSD_CONV_W, SSD_CONV_DIM), jnp.float32) * SSD_CONV_W ** -0.5
    ssd_conv_b = 0.02 * nrm(ks[3], (DEPTH, SSD_CONV_DIM), jnp.float32)
    dt0 = jnp.exp(jax.random.uniform(ks[4], (DEPTH, H), jnp.float32, minval=math.log(1e-3), maxval=math.log(1e-1)))
    ssd_dt_bias = dt0 + jnp.log(-jnp.expm1(-dt0))
    ssd_A_log = jnp.log(jax.random.uniform(ks[5], (DEPTH, H), jnp.float32, minval=1.0, maxval=16.0))
    ssd_D = 1.0 + 0.1 * nrm(ks[6], (DEPTH, H), jnp.float32)
    ssd_norm_w = 1.0 + 0.02 * nrm(ks[7], (DEPTH, SSD_D_INNER), jnp.float32)
    gla_gk_w = nrm(ks[8], (DEPTH, GLA_GATE_RANK, GLA_D_KEY), jnp.float32) * GLA_GATE_RANK ** -0.5
    gla_gk_b = 0.02 * nrm(ks[9], (DEPTH, GLA_D_KEY), jnp.float32)
    gla_norm_w = 1.0 + 0.02 * nrm(ks[10], (DEPTH, GLA_HEAD_V), jnp.float32)
    w_ssd_branch = nrm(ks[11], (DEPTH, SSD_D_INNER, D_MODEL), jnp.float32) * SSD_D_INNER ** -0.5
    w_gla_branch = nrm(ks[12], (DEPTH, GLA_D_VALUE, D_MODEL), jnp.float32) * GLA_D_VALUE ** -0.5
    gate_bias = 0.02 * nrm(ks[13], (DEPTH, 2, D_MODEL), jnp.float32)
    w_out = nrm(ks[14], (DEPTH, D_MODEL, D_MODEL), jnp.float32) * (D_MODEL ** -0.5 * BETA)
    ln1_g = 1.0 + 0.02 * nrm(ks[15], (DEPTH, D_MODEL), jnp.float32)
    ln1_b = 0.02 * nrm(ks[16], (DEPTH, D_MODEL), jnp.float32)
    w_up = nrm(ks[17], (DEPTH, D_MODEL, D_FF), jnp.float32) * D_MODEL ** -0.5
    w_down = nrm(ks[18], (DEPTH, D_FF, D_MODEL), jnp.float32) * (D_FF ** -0.5 * BETA)
    ln2_g = 1.0 + 0.02 * nrm(ks[19], (DEPTH, D_MODEL), jnp.float32)
    ln2_b = 0.02 * nrm(ks[20], (DEPTH, D_MODEL), jnp.float32)
    return {'x': x, 'w_in': w_in, 'ssd_conv_w': ssd_conv_w, 'ssd_conv_b': ssd_conv_b,
            'ssd_dt_bias': ssd_dt_bias, 'ssd_A_log': ssd_A_log, 'ssd_D': ssd_D, 'ssd_norm_w': ssd_norm_w,
            'gla_gk_w': gla_gk_w, 'gla_gk_b': gla_gk_b, 'gla_norm_w': gla_norm_w,
            'w_ssd_branch': w_ssd_branch, 'w_gla_branch': w_gla_branch, 'gate_bias': gate_bias,
            'w_out': w_out, 'ln1_g': ln1_g, 'ln1_b': ln1_b, 'w_up': w_up, 'w_down': w_down,
            'ln2_g': ln2_g, 'ln2_b': ln2_b}

def first_block(x, w_in, ssd_conv_w, ssd_conv_b, ssd_dt_bias, ssd_A_log, ssd_D, ssd_norm_w,
              gla_gk_w, gla_gk_b, gla_norm_w, w_ssd_branch, w_gla_branch, gate_bias,
              w_out, ln1_g, ln1_b, w_up, w_down, ln2_g, ln2_b):
    for l in range(DEPTH):
        mix = hybrid_mixer(x, w_in[l], ssd_conv_w[l], ssd_conv_b[l], ssd_dt_bias[l], ssd_A_log[l],
                           ssd_D[l], ssd_norm_w[l], gla_gk_w[l], gla_gk_b[l], gla_norm_w[l],
                           w_ssd_branch[l], w_gla_branch[l], gate_bias[l], w_out[l])
        x = layer_norm(ALPHA * x + mix, ln1_g[l], ln1_b[l])
        x = layer_norm(ALPHA * x + squared_relu_mlp(x, w_up[l], w_down[l]), ln2_g[l], ln2_b[l])
    return x


_first_inputs = first_inputs


def first_inputs(seed=0):
    import zlib

    import numpy as np

    out = dict(_first_inputs(seed))
    spreads = {}
    factors = {'ssd_conv_b': 7.584,
     'ssd_norm_w': 27.322,
     'gla_gk_w': 3.492,
     'gla_gk_b': 22.771,
     'gla_norm_w': 43.863,
     'gate_bias': 8.0,
     'ln1_b': 2.786,
     'ln2_g': 8.54,
     'ln2_b': 8.38}
    for name, (base, spread) in spreads.items():
        noise = np.random.default_rng([zlib.crc32(name.encode()), seed]).standard_normal(out[name].shape)
        drawn = base * np.exp(spread * noise) if base else spread * noise
        out[name] = __import__('jax').numpy.asarray(drawn.astype(out[name].dtype))
    for name, factor in factors.items():
        out[name] = (out[name] * factor).astype(out[name].dtype)
    return out


_narrow_inputs = first_inputs


def first_inputs(seed=0):

    out = dict(_narrow_inputs(seed))
    wider = {'ssd_norm_w': 4.26, 'gla_norm_w': 4.28, 'ln2_g': 3.29, 'ln2_b': 3.29}
    for name, times in wider.items():
        mean = out[name].mean()
        out[name] = (mean + times * (out[name] - mean)).astype(out[name].dtype)
    return out


DEPTH_2 = 2

GRID_W = 64
HEAD_DIM = 128
A_HEADS = 8
A_KV_HEADS = 2
B_HEADS = 4
B_Q_LORA = 512
B_KV_LORA = 256
B_NOPE = 128
B_ROPE = 64
B_V = 128
C_HEADS = 4
WIN_ROWS = 8
WIN_COLS = 16
D_MIX = A_HEADS * HEAD_DIM + B_HEADS * B_V + C_HEADS * HEAD_DIM
Q_BLOCK = 128
ROPE_THETA = 10000.0
NORM_EPS = 1e-6
IN_SPLITS = (
    A_HEADS * HEAD_DIM,
    A_KV_HEADS * HEAD_DIM,
    A_KV_HEADS * HEAD_DIM,
    A_HEADS * HEAD_DIM,
    B_Q_LORA,
    B_KV_LORA,
    B_ROPE,
    B_HEADS * B_V,
    C_HEADS * HEAD_DIM,
    C_HEADS * HEAD_DIM,
    C_HEADS * HEAD_DIM,
    C_HEADS * HEAD_DIM,
)
D_IN = sum(IN_SPLITS)


def _rms_norm(x, g):
    xf = x.astype(jnp.float32)
    y = xf * lax.rsqrt(jnp.mean(xf * xf, axis=-1, keepdims=True) + NORM_EPS)
    return (y * g.astype(jnp.float32)).astype(x.dtype)

def _rope_half(x, pos):
    n = x.shape[-1]
    inv_freq = 1.0 / (ROPE_THETA ** (jnp.arange(0, n, 2, dtype=jnp.float32) / n))
    ang = pos.astype(jnp.float32)[:, None] * inv_freq[None, :]
    cos = jnp.cos(ang)[:, None, :]
    sin = jnp.sin(ang)[:, None, :]
    xf = x.astype(jnp.float32)
    x1, x2 = xf[..., : n // 2], xf[..., n // 2:]
    out = jnp.concatenate([x1 * cos - x2 * sin, x2 * cos + x1 * sin], axis=-1)
    return out.astype(x.dtype)

def _rope_axial(x, row, col):
    h = x.shape[-1] // 2
    return jnp.concatenate([_rope_half(x[..., :h], row), _rope_half(x[..., h:], col)], axis=-1)

def _dense_block_attention(q, k, v):
    B, S, H, dq = q.shape
    Hk = k.shape[2]
    G = H // Hk
    dv = v.shape[-1]
    nb = S // Q_BLOCK
    scale = dq ** -0.5
    qb = q.reshape(B, nb, Q_BLOCK, Hk, G, dq).transpose(1, 0, 2, 3, 4, 5)

    def one(qblk):
        s = jnp.einsum('bqkgd,bskd->bkgqs', qblk, k).astype(jnp.float32) * scale
        p = jax.nn.softmax(s, axis=-1).astype(v.dtype)
        return jnp.einsum('bkgqs,bskd->bqkgd', p, v)

    o = lax.map(one, qb)
    return o.transpose(1, 0, 2, 3, 4, 5).reshape(B, S, H, dv)

def _neighbourhood_attention(q, k, v, rpb):
    B, S, H, d = q.shape
    rows = S // GRID_W
    kr = min(WIN_ROWS, rows)
    nk = kr * WIN_COLS
    t = jnp.arange(S)
    r = t // GRID_W
    c = t % GRID_W
    r0 = jnp.clip(r - kr // 2, 0, rows - kr)
    c0 = jnp.clip(c - WIN_COLS // 2, 0, GRID_W - WIN_COLS)
    key_r = r0[:, None, None] + jnp.arange(kr)[None, :, None]
    key_c = c0[:, None, None] + jnp.arange(WIN_COLS)[None, None, :]
    idx = (key_r * GRID_W + key_c).reshape(S, nk)
    dr = key_r - r[:, None, None] + (WIN_ROWS - 1)
    dc = key_c - c[:, None, None] + (WIN_COLS - 1)
    bias = rpb[:, dr, dc].reshape(H, S, nk)
    nb = S // Q_BLOCK
    scale = d ** -0.5
    qb = q.reshape(B, nb, Q_BLOCK, H, d).transpose(1, 0, 2, 3, 4)
    idxb = idx.reshape(nb, Q_BLOCK, nk)
    biasb = bias.reshape(H, nb, Q_BLOCK, nk).transpose(1, 0, 2, 3)

    def one(args):
        qblk, iblk, bblk = args
        kg = jnp.take(k, iblk, axis=1)
        vg = jnp.take(v, iblk, axis=1)
        s = jnp.einsum('bqhd,bqnhd->bhqn', qblk, kg).astype(jnp.float32) * scale
        s = s + bblk[None].astype(jnp.float32)
        p = jax.nn.softmax(s, axis=-1).astype(v.dtype)
        return jnp.einsum('bhqn,bqnhd->bqhd', p, vg)

    o = lax.map(one, (qb, idxb, biasb))
    return o.transpose(1, 0, 2, 3, 4).reshape(B, S, H, d)

def _layer(x, g_pre, g_post, w_in, a_qn, a_kn, b_qn, b_kvn, w_uq, w_ukv, rpb, w_out, row, col):
    B, S, _ = x.shape
    h = _rms_norm(x, g_pre)
    proj = jnp.einsum('bsd,de->bse', h, w_in)
    split_points = [int(p) for p in np.cumsum(IN_SPLITS)[:-1]]
    (a_q, a_k, a_v, a_g, b_cq, b_ckv, b_kr, b_g,
     c_q, c_k, c_v, c_g) = jnp.split(proj, split_points, axis=-1)

    qa = _rms_norm(a_q.reshape(B, S, A_HEADS, HEAD_DIM), a_qn)
    ka = _rms_norm(a_k.reshape(B, S, A_KV_HEADS, HEAD_DIM), a_kn)
    va = a_v.reshape(B, S, A_KV_HEADS, HEAD_DIM)
    qa = _rope_axial(qa, row, col)
    ka = _rope_axial(ka, row, col)
    o_a = _dense_block_attention(qa, ka, va).reshape(B, S, A_HEADS * HEAD_DIM) * jax.nn.silu(a_g)

    cq = _rms_norm(b_cq, b_qn)
    qb = jnp.einsum('bsr,re->bse', cq, w_uq).reshape(B, S, B_HEADS, B_NOPE + B_ROPE)
    q_nope, q_pe = qb[..., :B_NOPE], qb[..., B_NOPE:]
    q_pe = _rope_axial(q_pe, row, col)
    ckv = _rms_norm(b_ckv, b_kvn)
    kv = jnp.einsum('bsr,re->bse', ckv, w_ukv).reshape(B, S, B_HEADS, B_NOPE + B_V)
    k_nope, vb = kv[..., :B_NOPE], kv[..., B_NOPE:]
    k_pe = _rope_axial(b_kr.reshape(B, S, 1, B_ROPE), row, col)
    k_pe = jnp.broadcast_to(k_pe, (B, S, B_HEADS, B_ROPE))
    q_full = jnp.concatenate([q_nope, q_pe], axis=-1)
    k_full = jnp.concatenate([k_nope, k_pe], axis=-1)
    o_b = _dense_block_attention(q_full, k_full, vb).reshape(B, S, B_HEADS * B_V) * jax.nn.silu(b_g)

    qc = c_q.reshape(B, S, C_HEADS, HEAD_DIM)
    kc = c_k.reshape(B, S, C_HEADS, HEAD_DIM)
    vc = c_v.reshape(B, S, C_HEADS, HEAD_DIM)
    o_c = _neighbourhood_attention(qc, kc, vc, rpb).reshape(B, S, C_HEADS * HEAD_DIM) * jax.nn.silu(c_g)

    y = jnp.einsum('bse,ed->bsd', jnp.concatenate([o_a, o_b, o_c], axis=-1), w_out)
    return x + _rms_norm(y, g_post)

def second_inputs(seed: int = 0) -> dict:
    key = jax.random.key(seed)
    ks = jax.random.split(key, 13)
    f32 = jnp.float32

    def gain(k, n):
        return 1.0 + 0.05 * jax.random.normal(k, (DEPTH_2, n), f32)

    x = jax.random.normal(ks[0], (BATCH, SEQ, D_MODEL), f32)
    norm_pre = gain(ks[1], D_MODEL)
    norm_post = gain(ks[2], D_MODEL)
    w_in = jax.random.normal(ks[3], (DEPTH_2, D_MODEL, D_IN), f32) * D_MODEL ** -0.5
    a_q_norm = gain(ks[4], HEAD_DIM)
    a_k_norm = gain(ks[5], HEAD_DIM)
    b_q_norm = gain(ks[6], B_Q_LORA)
    b_kv_norm = gain(ks[7], B_KV_LORA)
    b_w_uq = jax.random.normal(ks[8], (DEPTH_2, B_Q_LORA, B_HEADS * (B_NOPE + B_ROPE)), f32) * B_Q_LORA ** -0.5
    b_w_ukv = jax.random.normal(ks[9], (DEPTH_2, B_KV_LORA, B_HEADS * (B_NOPE + B_V)), f32) * B_KV_LORA ** -0.5
    c_rpb = 0.1 * jax.random.normal(ks[10], (DEPTH_2, C_HEADS, 2 * WIN_ROWS - 1, 2 * WIN_COLS - 1), f32)
    w_out = jax.random.normal(ks[11], (DEPTH_2, D_MIX, D_MODEL), f32) * D_MIX ** -0.5
    return {"x": x, "norm_pre": norm_pre, "norm_post": norm_post, "w_in": w_in,
            "a_q_norm": a_q_norm, "a_k_norm": a_k_norm, "b_q_norm": b_q_norm,
            "b_kv_norm": b_kv_norm, "b_w_uq": b_w_uq, "b_w_ukv": b_w_ukv,
            "c_rpb": c_rpb, "w_out": w_out}

def second_block(x, norm_pre, norm_post, w_in, a_q_norm, a_k_norm, b_q_norm, b_kv_norm,
              b_w_uq, b_w_ukv, c_rpb, w_out):
    S = x.shape[1]
    t = jnp.arange(S)
    row = t // GRID_W
    col = t % GRID_W
    h = x
    for l in range(DEPTH_2):
        h = _layer(h, norm_pre[l], norm_post[l], w_in[l], a_q_norm[l], a_k_norm[l],
                   b_q_norm[l], b_kv_norm[l], b_w_uq[l], b_w_ukv[l], c_rpb[l], w_out[l],
                   row, col)
    return h


def setup_inputs(seed=0):
    out = dict(first_inputs(seed))
    for name, value in second_inputs(seed + 1).items():
        if name != "x":
            out[name + "_2"] = value
    return out


def reference(
    x, w_in, ssd_conv_w, ssd_conv_b, ssd_dt_bias, ssd_A_log, ssd_D, ssd_norm_w, gla_gk_w,
    gla_gk_b, gla_norm_w, w_ssd_branch, w_gla_branch, gate_bias, w_out, ln1_g, ln1_b, w_up,
    w_down, ln2_g, ln2_b, norm_pre_2, norm_post_2, w_in_2, a_q_norm_2, a_k_norm_2, b_q_norm_2,
    b_kv_norm_2, b_w_uq_2, b_w_ukv_2, c_rpb_2, w_out_2,
):
    x = first_block(
        x, w_in, ssd_conv_w, ssd_conv_b, ssd_dt_bias, ssd_A_log, ssd_D, ssd_norm_w, gla_gk_w,
        gla_gk_b, gla_norm_w, w_ssd_branch, w_gla_branch, gate_bias, w_out, ln1_g, ln1_b, w_up,
        w_down, ln2_g, ln2_b,
    )
    return second_block(
        x, norm_pre_2, norm_post_2, w_in_2, a_q_norm_2, a_k_norm_2, b_q_norm_2, b_kv_norm_2,
        b_w_uq_2, b_w_ukv_2, c_rpb_2, w_out_2,
    )


_drawn_inputs = setup_inputs


def setup_inputs(seed=0):
    import zlib

    import numpy as np

    out = dict(_drawn_inputs(seed))
    spreads = {}
    factors = {'norm_pre_2': 4.485,
     'norm_post_2': 6.879,
     'a_q_norm_2': 8.0,
     'a_k_norm_2': 8.0,
     'b_q_norm_2': 8.0,
     'b_kv_norm_2': 8.0,
     'c_rpb_2': 8.0}
    for name, (base, spread) in spreads.items():
        noise = np.random.default_rng([zlib.crc32(name.encode()), seed]).standard_normal(out[name].shape)
        drawn = base * np.exp(spread * noise) if base else spread * noise
        out[name] = __import__('jax').numpy.asarray(drawn.astype(out[name].dtype))
    for name, factor in factors.items():
        out[name] = (out[name] * factor).astype(out[name].dtype)
    return out
```

```python
from contextlib import ExitStack, contextmanager

import numpy as np

import concourse.bass as bass
import concourse.mybir as mybir

F32 = mybir.dt.float32
F32R = mybir.dt.float32r
ALU = mybir.AluOpType
ACT = mybir.ActivationFunctionType
AX = mybir.AxisListType.X
ds = bass.ds

P = 128
S = 256
NT = S // P
D = 2048
KT = D // P
QK = 4
BLK = 512
RAW_RING = 4
SPLIT_RING = 2

SSD_IN = 2 * D
SSD_G, SSD_HG, SSD_P, SSD_N = 8, 8, 64, 128
SSD_H = SSD_G * SSD_HG
CONV_W = 4
CONV_T = 6
GLA_H, GLA_K, GLA_V, GLA_C, GLA_R = 4, 256, 512, 64, 16
FF = 4 * D
ALPHA = 2.0 ** 0.25
COL_Z = 0
COL_XBC = SSD_IN
COL_DT = COL_XBC + SSD_IN + 2 * SSD_G * SSD_N
COL_Q = COL_DT + SSD_H
COL_K = COL_Q + GLA_H * GLA_K
COL_V = COL_K + GLA_H * GLA_K
COL_G = COL_V + D
COL_GK = COL_G + D
COL_GATE = COL_GK + GLA_R
N_IN = COL_GATE + 2 * D

LAYERS = 2
HD = 128
A_H, A_KV, B_H, C_H = 8, 2, 4, 4
B_QL, B_KVL, B_ROPE = 512, 256, 64
GRID = 64
ROWS = S // GRID
WIN_R, WIN_C = 8, 16
UNIT_H = 4
C2_AQ = 0
C2_AK = C2_AQ + A_H * HD
C2_AV = C2_AK + A_KV * HD
C2_AG = C2_AV + A_KV * HD
C2_CQ = C2_AG + A_H * HD
C2_CKV = C2_CQ + B_QL
C2_KR = C2_CKV + B_KVL
C2_BG = C2_KR + B_ROPE
C2_Q = C2_BG + B_H * HD
C2_K = C2_Q + C_H * HD
C2_V = C2_K + C_H * HD
C2_G = C2_V + C_H * HD
N_IN2 = C2_G + C_H * HD
MASKED = -1.0e30

INPUTS = ["x", "w_in", "conv", "ssd_dt_bias", "ssd_A_log", "ssd_D", "ssd_norm_w", "gla_gk_w", "gla_gk_b",
          "gla_norm_w", "w_ssd_branch", "w_gla_branch", "gate_bias", "w_out", "ln1_g", "ln1_b", "w_up",
          "w_down", "ln2_g", "ln2_b", "norm_pre_2", "norm_post_2", "w_in_2", "a_q_norm_2", "a_k_norm_2",
          "b_q_norm_2", "b_kv_norm_2", "b_w_uq_2", "b_w_ukv_2", "c_rpb_2", "w_out_2"]


class Count:

    def __init__(self, prog, name, step=1):
        self.prog, self.name, self.step, self.n = prog, name, step, 0
        self.sem = prog.ctx.enter_context(prog.nc.semaphore(name))

    def up(self, instruction):
        instruction.then_inc(self.sem, self.step)
        self.n += self.step
        return self.now()

    def now(self, back=0):
        return Mark(self, self.n - back * self.step, tuple(self.prog.loops))


class Mark:
    def __init__(self, count, n, loops):
        self.count, self.n, self.loops = count, n, loops


class Loop:
    def __init__(self, prog, key, index, trips):
        self.key, self.index, self.trips = key, index, trips
        self.gain = prog.gains.get(key, {})


class Prog:

    def __init__(self, nc, ctx, gains):
        self.nc, self.ctx, self.gains, self.found = nc, ctx, gains, {}
        self.loops, self.counts, self.held, self.seen = [], {}, {}, {}
        self.n_loops = 0
        self.pe = self.count("pe")
        self.act = self.count("act")
        self.dve = self.count("dve")
        self.pool = self.count("pool")

    def count(self, name, step=1):
        self.counts[name] = Count(self, name, step)
        return self.counts[name]

    def wait(self, engine, *marks):
        for m in marks:
            if m is None:
                continue
            open_at = tuple(x for x in m.loops if x in self.loops)
            known = self.seen.get((engine, m.count.name))
            if m.loops == open_at and known and known[0] == m.loops and known[1] >= m.n:
                continue
            if m.loops == open_at:
                self.seen[engine, m.count.name] = (m.loops, m.n)
            value, index = m.n, None
            for loop in m.loops:
                gain = loop.gain.get(m.count.name, 0)
                if not gain:
                    continue
                if loop in self.loops:
                    term = loop.index * gain
                    index = term if index is None else index + term
                else:
                    value += (loop.trips - 1) * gain
            if index is None:
                if value > 0:
                    engine.wait_ge(m.count.sem, value)
            else:
                assert value > 0, m.count.name
                engine.wait_ge(m.count.sem, index + value)

    @contextmanager
    def loop(self, trips, apart=True):
        if apart:
            self.meet()
        key = self.n_loops
        self.n_loops += 1
        before = {k: c.n for k, c in self.counts.items()}
        self.seen = {}
        with self.nc.Fori(0, trips) as index:
            loop = Loop(self, key, index, trips)
            self.loops.append(loop)
            yield index
            if apart:
                self.meet()
            self.loops.pop()
        self.seen = {}
        self.found[key] = {}
        for k, c in self.counts.items():
            gain = c.n - before.get(k, 0)
            if gain:
                self.found[key][k] = gain
                c.n += (trips - 1) * gain
        if self.gains:
            assert self.found[key] == loop.gain, (key, self.found[key], loop.gain)

    def meet(self):
        nc = self.nc
        mine = [(nc.tensor, self.pe), (nc.scalar, self.act), (nc.vector, self.dve), (nc.gpsimd, self.pool)]
        for engine, _ in mine:
            for _, other in mine:
                self.wait(engine, other.now())
        self.held = {}

    def hold(self, what, *marks):
        self.held[what] = marks

    def free(self, engine, what):
        self.wait(engine, *self.held.get(what, ()))

    def T(self, f, *args, after=(), **kw):
        self.wait(self.nc.tensor, *after)
        return self.pe.up(f(*args, **kw))

    def A(self, f, *args, after=(), **kw):
        self.wait(self.nc.scalar, *after)
        return self.act.up(f(*args, **kw))

    def V(self, f, *args, after=(), **kw):
        self.wait(self.nc.vector, *after)
        return self.dve.up(f(*args, **kw))

    def G(self, f, *args, after=(), **kw):
        self.wait(self.nc.gpsimd, *after)
        return self.pool.up(f(*args, **kw))


def wide(ap, shape):
    return ap.to_broadcast(list(shape))


def emit(nc, ctx, gains, i, out, debug=None):
    pr = Prog(nc, ctx, gains)
    T, A, V, G, wait, hold, free = pr.T, pr.A, pr.V, pr.G, pr.wait, pr.hold, pr.free
    pe, act, dve, pool, sp = nc.tensor, nc.scalar, nc.vector, nc.gpsimd, nc.sync

    def sb(name, shape, dt=F32):
        return ctx.enter_context(nc.sbuf_tensor(name, shape, dt))

    def scratch(name, shape):
        kind = "ExternalOutput" if debug is not None and name in debug else "Internal"
        return nc.dram_tensor(name, shape, F32, kind=kind).ap()

    raw = sb("raw", [P, RAW_RING, QK, BLK])
    w_hi = sb("w_hi", [P, SPLIT_RING, QK, BLK], F32R)
    w_lo = sb("w_lo", [P, SPLIT_RING, QK, BLK], F32R)
    x_hi = sb("x_hi", [P, 2 * KT, S], F32R)
    x_lo = sb("x_lo", [P, 2 * KT, S], F32R)
    stage = sb("stage", [P, 2, NT, BLK])
    arena = sb("arena", [P, 14080])
    ident = sb("ident", [P, P])
    bank = [ctx.enter_context(nc.psum_tensor(f"bank{b}", [P, BLK], F32)) for b in range(8)]

    class Room:

        def __init__(self, at=0):
            self.at = at

        def __call__(self, *shape):
            n = int(np.prod(shape))
            a = arena[:, self.at:self.at + n]
            self.at += n
            assert self.at <= arena.shape[1], self.at
            if len(shape) == 2:
                a = a.rearrange("p (a b) -> p a b", a=shape[0])
            if len(shape) == 3:
                a = a.rearrange("p (a b c) -> p a b c", a=shape[0], b=shape[1])
            return a

    proj = scratch("proj", [S, N_IN])
    proj2 = scratch("proj2", [S, N_IN2])
    latent = scratch("latent", [S, 2048])
    residual = scratch("residual", [S, D])
    gated = scratch("gated", [S, D])
    skew = scratch("skew", [C_H * (2 * ROWS - 1), GRID, P])

    def rows(ap):
        return ap.rearrange("(t p) n -> p t n", p=P)

    s_raw = [pr.count(f"s_raw{n}", 16) for n in range(RAW_RING)]
    s_hi = pr.count("s_hi")
    s_lo = pr.count("s_lo")
    s_mm = pr.count("s_mm")
    s_dra = pr.count("s_dra")
    s_drv = pr.count("s_drv")
    s_st = [pr.count(f"s_st{n}", 16) for n in range(2)]
    d_in = pr.count("d_in", 16)
    d_late = pr.count("d_late", 16)
    d_out = pr.count("d_out", 16)
    at = {"quad": 0, "block": 0, "drain": None, "save": None, "turn": 0, "since": 0}

    def summed():
        return s_mm.now(at["since"])

    def load(to, source, *after, count=d_in):
        wait(act, *after)
        return count.up(act.dma_start(to, source))

    def store(to, source, *after):
        wait(act, *after)
        return d_out.up(act.dma_start(to, source))

    def quad(weight, x0, kts, n, banks, first, last):
        slot, half = at["quad"] % RAW_RING, at["quad"] % SPLIT_RING
        source = weight()
        wait(sp, s_lo.now(RAW_RING - 1))
        landed = s_raw[slot].up(sp.dma_start(raw[:, slot, 0:kts, 0:n], source))
        wait(act, landed, s_mm.now(SPLIT_RING - 1))
        hi = s_hi.up(act.activation(w_hi[:, half, 0:kts, 0:n], raw[:, slot, 0:kts, 0:n], ACT.Copy))
        wait(dve, hi)
        lo = s_lo.up(dve.tensor_tensor(w_lo[:, half, 0:kts, 0:n], raw[:, slot, 0:kts, 0:n],
                                       w_hi[:, half, 0:kts, 0:n].bitcast(F32), ALU.subtract))
        wait(pe, lo)
        for k in range(kts):
            for t in range(NT):
                tok = slice(t * P, t * P + P)
                a, b = first and k == 0, last and k == kts - 1
                o = bank[banks + t][:, 0:n]
                pe.matmul(o, x_hi[:, x0 + k, tok], w_lo[:, half, k, 0:n], start=a, stop=False)
                pe.matmul(o, x_hi[:, x0 + k, tok], w_hi[:, half, k, 0:n], start=False, stop=False)
                mm = pe.matmul(o, x_lo[:, x0 + k, tok], w_hi[:, half, k, 0:n], start=False, stop=b)
        s_mm.up(mm)
        at["quad"] += 1

    def drained(late=False):
        if at["drain"] is not None:
            at["save"] = at["drain"]()
            at["drain"] = None
        if not late:
            saved()

    def saved():
        if at["save"] is not None:
            at["save"]()
            at["save"] = None

    def block(weight, x0, kts, n, drain):
        half = at["block"] % 2
        wait(pe, s_drv.now())
        quads = max(1, kts // QK)
        for q in range(quads):
            quad(lambda: weight(q), x0 + q * QK, min(QK, kts), n, 2 * half, q == 0, q == quads - 1)
            if q == min(1, quads - 1):
                at["since"] = q + 1
                drained(late=True)
            elif q == 2:
                saved()
        saved()
        at["since"] = 0
        at["block"] += 1
        at["drain"] = lambda: drain(half, n)

    def weight_at(w, col, n):
        w = w.rearrange("(k p) n -> p k n", p=P)
        kts = min(QK, w.shape[1])

        def get(q):
            c = col
            if not isinstance(col, int):
                c = sp.snap(col)
            return w[:, q * kts:(q + 1) * kts, ds(c, n)]
        return get

    def segment(w, col, blocks, x0, drain, n=BLK):
        def one(j):
            block(weight_at(w, j * n + col, n), x0, KT, n, drain(j))

        def again(j):
            at["drain"] = lambda h=(at["block"] - 1) % 2: drain(j)(h, n)
        one(0)
        done = 1
        if blocks > 5:
            turns = (blocks - 1) // 2
            with pr.loop(turns, apart=False) as turn:
                again(turn * 2)
                one(turn * 2 + 1)
                one(turn * 2 + 2)
            again(2 * turns)
            done += 2 * turns
        for j in range(done, blocks):
            one(j)

    def to_dram(dest, col):
        def drain_of(j):
            def drain(half, n):
                wait(act, summed(), s_st[half].now())
                s_dra.up(act.activation(stage[:, half, 0, 0:n], bank[2 * half][:, 0:n], ACT.Copy))
                wait(dve, summed(), s_st[half].now(), s_dra.now())
                s_drv.up(dve.tensor_copy(stage[:, half, 1, 0:n], bank[2 * half + 1][:, 0:n]))
                full = s_drv.now()

                def save():
                    wait(act, full)
                    s_st[half].up(act.dma_start(rows(dest)[:, :, ds(j * BLK + col, n)], stage[:, half, :, 0:n]))
                return save
            return drain
        return drain_of

    def to_sum(total, add):
        def drain_of(j):
            def drain(half, n):
                wait(dve, summed())
                for t in range(NT):
                    to = total[:, t, j * BLK:j * BLK + n]
                    b = bank[2 * half + t][:, 0:n]
                    if add:
                        wait(dve, total_marks.get(j))
                        last = dve.tensor_tensor(to, b, to, ALU.add)
                    else:
                        last = dve.tensor_copy(to, b)
                total_marks[j] = s_drv.up(last)
            return drain
        return drain_of
    total_marks = {}

    TP = (6, 7)

    def transpose4(source, x0, t, *after, tiles=4):
        b = TP[at["turn"] % 2]
        at["turn"] += 1
        free(pe, b)
        wait(pe, *after)
        for k in range(tiles):
            last = pe.transpose(bank[b][:, k * P:(k + 1) * P], source[:, k * P:(k + 1) * P], ident[:, :])
        turned = pr.pe.up(last)
        full = bank[b][:, 0:tiles * P].rearrange("p (k n) -> p k n", k=tiles)
        hi, lo = x_hi[:, ds(x0, tiles), t * P:(t + 1) * P], x_lo[:, ds(x0, tiles), t * P:(t + 1) * P]
        free_set = s_mm.now()
        rounded = A(act.activation, hi, full, ACT.Copy, after=(turned, free_set))
        rest = V(dve.tensor_tensor, lo, full, hi.bitcast(F32), ALU.subtract, after=(rounded,))
        hold(b, rest)
        return rest

    def transpose_all(source, x0, *after):
        for t in range(NT):
            for k in range(0, KT, 4):
                last = transpose4(source[:, t, k * P:(k + 4) * P], x0 + k, t, *after)
        wait(pe, last)

    def row_of(w, n):
        return w.rearrange("(a n) -> a n", a=1).partition_broadcast(P) if len(w.shape) == 1 else w

    def inverse_root(to, sums, n, eps, *after):
        m = V(dve.tensor_scalar, to, sums, 1.0 / n, eps, ALU.mult, ALU.add, after=after)
        m = V(dve.reciprocal, to, to, after=(m,))
        return A(act.activation, to, to, ACT.Sqrt, after=(m,))

    def log1p_exp(to, x, e, u, *after):
        m = V(dve.scalar_tensor_tensor, e, x, -1.0, x, ALU.mult, ALU.max, after=after)
        m = A(act.activation, e, e, ACT.Exp, scale=-1.0, after=(m,))
        mu = V(dve.tensor_scalar, u, e, 1.0, None, ALU.add, after=(m,))
        ml = A(act.activation, to, u, ACT.Ln, after=(mu,))
        m = V(dve.scalar_tensor_tensor, e, u, -1.0, e, ALU.add, ALU.subtract, after=(mu,))
        m = V(dve.reciprocal, u, u, after=(m, ml))
        m = V(dve.tensor_tensor, e, e, u, ALU.mult, after=(m,))
        return V(dve.tensor_tensor, to, to, e, ALU.subtract, after=(m,))

    room = Room()
    xin = room(NT, D)
    loaded = load(ident[:, :], i["identity"])
    loaded = load(xin, rows(i["x"][0]))
    transpose_all(xin, 0, loaded)

    w_in = i["w_in"][0]

    def small(q):
        return w_in.rearrange("(k p) n -> p k n", p=P)[:, q * QK:(q + 1) * QK, ds(COL_DT, SSD_H)]

    block(small, 0, KT, SSD_H, to_dram(proj, COL_DT)(0))
    block(weight_at(w_in, COL_GK, GLA_R), 0, KT, GLA_R, to_dram(proj, COL_GK)(0))
    segment(w_in, COL_Z, (COL_DT - COL_Z) // BLK, 0, to_dram(proj, COL_Z))
    segment(w_in, COL_Q, (COL_GK - COL_Q) // BLK, 0, to_dram(proj, COL_Q))
    segment(w_in, COL_GATE, 2 * D // BLK, 0, to_dram(proj, COL_GATE))
    drained()
    if debug and "stop0" in debug:
        return finish(pr, out, xin, pr.pe.now())

    from_proj = lambda: wait(act, s_st[0].now(), s_st[1].now())
    from_proj()

    pr.meet()
    room = Room()
    TAB = 10
    tab = room(TAB, SSD_H)
    DT, AA, CS, EC, DW, DD = 0, 2, 4, 6, 8, 9
    tri = room(P)
    ones = room(P)
    t_a, t_b, t_c = room(NT, SSD_H), room(NT, SSD_H), room(NT, SSD_H)
    alog, bias = room(SSD_H), room(SSD_H)
    load(tri, i["causal"])
    load(t_a, rows(proj)[:, :, COL_DT:COL_DT + SSD_H])
    load(bias, row_of(i["ssd_dt_bias"][0], SSD_H))
    load(alog, row_of(i["ssd_A_log"][0], SSD_H))
    loaded = load(tab[:, DD, :], row_of(i["ssd_D"][0], SSD_H))
    m_ones = V(dve.memset, ones, 1.0)
    for t in range(NT):
        m = V(dve.tensor_tensor, t_a[:, t, :], t_a[:, t, :], bias, ALU.add, after=(loaded,))
    flat = lambda ap: ap.rearrange("p a b -> p (a b)")
    m = log1p_exp(flat(tab[:, DT:DT + 2, :]), flat(t_a), flat(t_b), flat(t_c), m)
    m = V(dve.scalar_tensor_tensor, flat(tab[:, DT:DT + 2, :]), flat(t_a), 0.0, flat(tab[:, DT:DT + 2, :]),
          ALU.max, ALU.add, after=(m,))
    me = A(act.activation, alog, alog, ACT.Exp, after=(loaded,))
    for t in range(NT):
        m = V(dve.scalar_tensor_tensor, tab[:, AA + t, :], tab[:, DT + t, :], -1.0, alog, ALU.mult, ALU.mult,
              after=(m, me))
    n2 = NT * SSD_H
    m = T(pe.matmul, bank[0][:, 0:n2], tri, flat(tab[:, AA:AA + 2, :]), start=True, stop=True, after=(m,))
    m2 = T(pe.matmul, bank[1][:, 0:n2], ones, flat(tab[:, AA:AA + 2, :]), start=True, stop=True, after=(m_ones,))
    mc = V(dve.tensor_copy, flat(tab[:, CS:CS + 2, :]), bank[0][:, 0:n2], after=(m2,))
    A(act.activation, flat(tab[:, EC:EC + 2, :]), flat(tab[:, CS:CS + 2, :]), ACT.Exp, after=(mc,))
    m = V(dve.tensor_tensor, alog, bank[1][:, 0:SSD_H], tab[:, CS, :], ALU.subtract, after=(mc,))
    m = A(act.activation, alog, alog, ACT.Exp, after=(m,))
    V(dve.tensor_tensor, tab[:, DW, :], tab[:, DT, :], alog, ALU.mult, after=(m,))

    CH = SSD_HG * SSD_P
    room_g = Room(room.at)
    gt = room_g(TAB, SSD_HG)
    xin = room_g(NT, CONV_T * P)
    z = room_g(NT, CH)
    cw = room_g(CONV_T, CONV_W + 1)
    nw = room_g(CH)
    ut = room_g(CONV_T, S + CONV_W - 1)
    cv = room_g(CONV_T, S)
    xt = room_g(NT, CH)
    xdt = room_g(NT, CH)
    xw = room_g(CH)
    btok = room_g(P)
    cbm = room_g(NT, P)
    dec = room_g(NT, SSD_HG, P)
    prev = xin[:, 0, 0:CH]
    ysum = room_g(2, 1)
    pr.meet()
    V(dve.memset, ut[:, :, 0:CONV_W - 1], 0.0)
    with pr.loop(SSD_G) as g:
        pp = rows(proj)
        load(xin[:, :, 0:CH], pp[:, :, ds(g * CH + COL_XBC, CH)])
        load(xin[:, :, CH:CH + P], pp[:, :, ds(g * P + (COL_XBC + SSD_IN), P)])
        load(xin[:, :, CH + P:CH + 2 * P], pp[:, :, ds(g * P + (COL_XBC + SSD_IN + SSD_G * SSD_N), P)])
        m_in = load(flat(cw), i["conv"][ds(g, 1)].rearrange("a p n -> (a p) n"))
        load(z, pp[:, :, ds(g * CH + COL_Z, CH)], count=d_late)
        m_z = load(nw, row_of(i["ssd_norm_w"][0][ds(g * CH, CH)], CH), count=d_late)
        m_gt = V(dve.tensor_copy, gt, tab[:, :, ds(g * SSD_HG, SSD_HG)])
        for c in range(CONV_T):
            for t in range(NT):
                m = T(pe.transpose, bank[c // 2][:, (c % 2) * S + t * P:(c % 2) * S + (t + 1) * P],
                      xin[:, t, c * P:(c + 1) * P], ident[:, :], after=(m_in,))
            if c % 2:
                mu = A(act.activation, ut[:, c - 1:c + 1, CONV_W - 1:],
                       bank[c // 2][:, :].rearrange("p (a b) -> p a b", a=2), ACT.Copy, after=(m,))
        m_cv = [mu] * CONV_T
        for w in range(CONV_W):
            for c in range(CONV_T):
                src, s = ut[:, c, w:w + S], cw[:, c, w:w + 1]
                if w == 0:
                    m_cv[c] = V(dve.tensor_scalar, cv[:, c, :], src, s, None, ALU.mult, after=(mu, m_in))
                else:
                    m_cv[c] = V(dve.scalar_tensor_tensor, cv[:, c, :], src, s, cv[:, c, :], ALU.mult, ALU.add,
                                after=(m_cv[c],))
        for c in (4, 5, 0, 1, 2, 3):
            m_s = A(act.activation, cv[:, c, :], cv[:, c, :], ACT.Silu, bias=cw[:, c, CONV_W:CONV_W + 1],
                    after=(m_cv[c],))
        for t in range(NT):
            m_sz = A(act.activation, z[:, t, :], z[:, t, :], ACT.Silu, after=(m_z,))
        for t in range(NT):
            tok = slice(t * P, t * P + P)
            m_cb = T(pe.matmul, bank[3][:, tok], cv[:, 4, tok], cv[:, 5, tok], start=True, stop=True,
                     after=(m_s,))
        m_bt = T(pe.transpose, bank[3][:, S:S + P], cv[:, 4, 0:P], ident[:, :])
        for t in range(NT):
            m_cbm = V(dve.tensor_tensor, cbm[:, t, :], bank[3][:, t * P:(t + 1) * P], tri, ALU.mult, after=(m_bt,))
        m_bt = A(act.activation, btok, bank[3][:, S:S + P], ACT.Copy, after=(m_bt, m_cbm))
        for t in range(NT):
            for c in range(4):
                m = T(pe.transpose, bank[4 + t][:, c * P:(c + 1) * P], cv[:, c, t * P:(t + 1) * P], ident[:, :])
            xh = bank[4 + t][:, :].rearrange("p (h e) -> p h e", h=SSD_HG)
            m_xt = A(act.activation, xt[:, t, :], bank[4 + t][:, :], ACT.Copy, after=(m,))
            m_xd = V(dve.tensor_tensor, xdt[:, t, :].rearrange("p (h e) -> p h e", h=SSD_HG), xh,
                     wide(gt[:, DT + t, :].unsqueeze(2), [P, SSD_HG, SSD_P]), ALU.mult, after=(m, m_gt, m_xt))
        m_xw = V(dve.tensor_tensor, xw.rearrange("p (h e) -> p h e", h=SSD_HG),
                 bank[4][:, :].rearrange("p (h e) -> p h e", h=SSD_HG),
                 wide(gt[:, DW, :].unsqueeze(2), [P, SSD_HG, SSD_P]), ALU.mult)
        HB = SSD_HG // 2
        m_dec = {}
        for t in range(NT):
            for hb in range(2):
                b = 2 * t + hb if t == 0 else (2, 6)[hb]
                for h in range(HB):
                    hh = hb * HB + h
                    m = T(pe.matmul, bank[b][:, h * P:(h + 1) * P],
                          wide(gt[:, AA + t, hh:hh + 1], [P, P]), tri, start=True, stop=True, after=(m_gt, mu))
                for h in range(HB):
                    hh = hb * HB + h
                    ms = V(dve.tensor_scalar, dec[:, t, hh, :], bank[b][:, h * P:(h + 1) * P],
                           gt[:, CS + t, hh:hh + 1], 0.0, ALU.subtract, ALU.min, after=(m,))
                me = A(act.activation, dec[:, t, hb * HB:(hb + 1) * HB, :], dec[:, t, hb * HB:(hb + 1) * HB, :],
                       ACT.Exp, after=(ms,))
                m_dec[t, hb] = G(pool.tensor_tensor, dec[:, t, hb * HB:(hb + 1) * HB, :],
                                 dec[:, t, hb * HB:(hb + 1) * HB, :],
                                 wide(cbm[:, t, :].unsqueeze(1), [P, HB, P]), ALU.mult, after=(me, m_cbm))
        m = T(pe.matmul, bank[7][:, :], btok, xw, start=True, stop=True, after=(m_bt, m_xw))
        m = A(act.activation, prev, bank[7][:, :], ACT.Copy, after=(m,))
        m_off = T(pe.matmul, bank[7][:, :], cv[:, 5, P:2 * P], prev, start=True, stop=True, after=(m,))
        by_head = lambda ap: ap.rearrange("p (h e) -> p h e", h=SSD_HG)
        hold(TP[0], *m_dec.values())
        at["turn"] = 0
        for t in range(NT):
            for h in range(SSD_HG):
                m = T(pe.matmul, bank[4 + t][:, h * SSD_P:(h + 1) * SSD_P], dec[:, t, h, :],
                      xdt[:, t, h * SSD_P:(h + 1) * SSD_P], start=True, stop=True,
                      after=(m_dec[t, h // HB], m_xt, m_xw))
            yt = xt[:, t, :]
            mx = V(dve.tensor_tensor, by_head(yt), by_head(yt),
                   wide(gt[:, DD, :].unsqueeze(2), [P, SSD_HG, SSD_P]), ALU.mult, after=(m_xt,))
            mx = V(dve.tensor_tensor, yt, yt, bank[4 + t][:, :], ALU.add, after=(mx, m))
            if t == 1:
                mo = V(dve.tensor_tensor, by_head(xdt[:, 0, :]), by_head(bank[7][:, :]),
                       wide(gt[:, EC + 1, :].unsqueeze(2), [P, SSD_HG, SSD_P]), ALU.mult, after=(m_off, m))
                mx = V(dve.tensor_tensor, yt, yt, xdt[:, 0, :], ALU.add, after=(mx, mo))
            mx = V(dve.tensor_tensor, yt, yt, z[:, t, :], ALU.mult, after=(mx, m_sz))
            ms = V(dve.tensor_tensor_reduce, xin[:, t, 0:CH], yt, yt, 1.0, 0.0, ALU.mult, ALU.add,
                   ysum[:, t, :], after=(mx, m_off))
            ms = inverse_root(ysum[:, t, :], ysum[:, t, :], CH, 1e-5, ms)
            ms = V(dve.scalar_tensor_tensor, yt, yt, ysum[:, t, :], nw, ALU.mult, ALU.mult, after=(ms, m_z))
            if t == 1:
                hold(TP[1], mo)
            transpose4(yt, g * 4, t, ms)

    room = Room()
    total = room(NT, D)
    gate = room(NT, D)
    grow = room(D)

    def branch_sum(w, parts):
        wait(dve, pr.act.now())
        for k in range(parts):
            segment(w[k * D:(k + 1) * D], 0, D // BLK, k * KT, to_sum(total, k > 0))
        drained()

    wait(pe, pr.dve.now())
    wait(dve, pr.act.now(), pr.pe.now(), pr.pool.now())
    branch_sum(i["w_ssd_branch"][0], 2)
    load(gate, rows(proj)[:, :, COL_GATE:COL_GATE + D], pr.pe.now(), pr.act.now(), pr.dve.now())
    loaded = load(grow, row_of(i["gate_bias"][0, 0], D))

    def gated_total(*after):
        for t in range(NT):
            m = V(dve.tensor_tensor, gate[:, t, :], gate[:, t, :], grow, ALU.add, after=after)
            m = A(act.activation, gate[:, t, :], gate[:, t, :], ACT.Sigmoid, after=(m,))
            m = V(dve.tensor_tensor, total[:, t, :], total[:, t, :], gate[:, t, :], ALU.mult,
                  after=(m, s_drv.now()))
        return m
    m = gated_total(loaded)
    stored = store(rows(gated), total, m)

    pr.meet()
    for e in (pe, act, dve):
        wait(e, stored)
    wait(act, stored)
    room = Room()
    low = room(NT, GLA_R)
    lowt = room(S)
    tri64, sum64, last64 = room(P), room(P), room(2)
    most, least = room(GLA_C), room(GLA_C)
    gnw = room(GLA_V)
    load(low, rows(proj)[:, :, COL_GK:COL_GK + GLA_R])
    load(tri64, i["causal64"])
    load(most, i["most64"])
    load(least, i["least64"])
    load(sum64, i["blocks64"])
    load(last64, i["columns64"])
    loaded = load(gnw, row_of(i["gla_norm_w"][0], GLA_V))
    m1 = V(dve.memset, lowt[0:GLA_R + 1, :], 1.0)
    for t in range(NT):
        m = T(pe.transpose, bank[0][0:GLA_R, t * P:(t + 1) * P], low[:, t, :], ident[:, :], after=(loaded,))
    V(dve.tensor_copy, lowt[0:GLA_R, :], bank[0][0:GLA_R, 0:S], after=(m, m1))
    q, k, v, gg = room(NT, GLA_K), room(NT, GLA_K), room(NT, GLA_V), room(NT, GLA_V)
    gkw = room(GLA_K)
    gk, e1, e2, e3 = room(NT, GLA_K), room(NT, GLA_K), room(NT, GLA_K), room(NT, GLA_K)
    qt, kt = room(2, S), room(2, S)
    dk = room(2, NT * 2)
    state = [room(2, GLA_V), room(2, GLA_V)]
    att = room(NT, P)
    osum = room(2, 1)
    o = room(NT, GLA_V)
    G(pool.memset, att, 0.0)
    with pr.loop(GLA_H) as h:
        pp = rows(proj)
        load(gkw[0:GLA_R, :], i["gla_gk_w"][0][:, ds(h * GLA_K, GLA_K)])
        load(gkw[GLA_R:GLA_R + 1, :], i["gla_gk_b"][:, ds(h * GLA_K, GLA_K)])
        load(q, pp[:, :, ds(h * GLA_K + COL_Q, GLA_K)])
        load(k, pp[:, :, ds(h * GLA_K + COL_K, GLA_K)])
        m_in = load(v, pp[:, :, ds(h * GLA_V + COL_V, GLA_V)])
        m_g = load(gg, pp[:, :, ds(h * GLA_V + COL_G, GLA_V)], count=d_late)
        for t in range(NT):
            m = T(pe.matmul, bank[0][:, t * GLA_K:(t + 1) * GLA_K], lowt[0:GLA_R + 1, t * P:(t + 1) * P],
                  gkw[0:GLA_R + 1, :], start=True, stop=True, after=(m_in,))
        m = V(dve.tensor_copy, flat(e1), bank[0][:, :], after=(m,))
        m = log1p_exp(flat(gk), flat(e1), flat(e2), flat(e3), m)
        m = V(dve.scalar_tensor_tensor, flat(gk), flat(e1), 0.0, flat(gk), ALU.min, ALU.subtract, after=(m,))
        m_gk = V(dve.tensor_scalar, flat(gk), flat(gk), 1.0 / 16.0, None, ALU.mult, after=(m,))
        m_G = T(pe.matmul, bank[1][:, :], tri64, flat(gk), start=True, stop=True, after=(m_gk,))
        m_L = T(pe.matmul, bank[2][:, :], sum64, flat(gk), start=True, stop=True)
        for kk in range(2):
            for t in range(NT):
                m = T(pe.matmul, bank[3][:, kk * 4 + 2 * t:kk * 4 + 2 * t + 2], gk[:, t, kk * P:(kk + 1) * P],
                      last64, start=True, stop=True)
        m_dk = A(act.activation, flat(dk), bank[3][:, 0:8], ACT.Exp, after=(m,))
        m_e2 = A(act.activation, flat(e2), bank[1][:, :], ACT.Exp)
        m_e3 = A(act.activation, flat(e3), bank[1][:, :], ACT.Exp, scale=-1.0)
        m_e1 = A(act.activation, flat(e1), bank[1][:, :], ACT.Copy)
        m = V(dve.tensor_tensor, flat(e1), bank[2][:, :], flat(e1), ALU.subtract, after=(m_e1,))
        m_e1 = A(act.activation, flat(e1), flat(e1), ACT.Exp, after=(m,))
        m_q = V(dve.scalar_tensor_tensor, flat(e2), flat(q), GLA_K ** -0.5, flat(e2), ALU.mult, ALU.mult,
                after=(m_e2, m_in))
        m_k = V(dve.tensor_tensor, flat(e3), flat(k), flat(e3), ALU.mult, after=(m_e3,))
        m_kd = V(dve.tensor_tensor, flat(e1), flat(k), flat(e1), ALU.mult, after=(m_e1,))
        for src, b, to, ms in ((e2, 4, qt, m_q), (e3, 5, kt, m_k)):
            for kk in range(2):
                for t in range(NT):
                    m = T(pe.transpose, bank[b][:, kk * S + t * P:kk * S + (t + 1) * P],
                          src[:, t, kk * P:(kk + 1) * P], ident[:, :], after=(ms,))
            m_t = A(act.activation, flat(to), bank[b][:, :], ACT.Copy, after=(m,))
        for c in range(2 * NT):
            t, half = c // 2, c % 2
            tok = slice(c * GLA_C, (c + 1) * GLA_C)
            part = slice(half * GLA_C, (half + 1) * GLA_C)
            for kk in range(2):
                m = T(pe.matmul, bank[6][part, t * GLA_C:(t + 1) * GLA_C], kt[:, kk, tok], qt[:, kk, tok],
                      start=(kk == 0), stop=(kk == 1), after=(m_t,))
        for half in range(2):
            part = slice(half * GLA_C, (half + 1) * GLA_C)
            inner = att[part, :, part]
            ma = V(dve.tensor_tensor, inner, bank[6][part, 0:NT * GLA_C].rearrange("p (t n) -> p t n", t=NT),
                   wide(most[part, :].unsqueeze(1), [GLA_C, NT, GLA_C]), ALU.min, after=(m,))
            m_att = V(dve.tensor_tensor, inner, inner, wide(least[part, :].unsqueeze(1), [GLA_C, NT, GLA_C]),
                      ALU.max, after=(ma,))
        for t in range(NT):
            T(pe.matmul, bank[t][:, :], att[:, t, :], v[:, t, :], start=True, stop=True, after=(m_att, m_e1))
        m_s = None
        for c in range(2 * NT):
            t, half = c // 2, c % 2
            tok = slice(c * GLA_C, (c + 1) * GLA_C)
            part = slice(half * GLA_C, (half + 1) * GLA_C)
            now, nxt = state[c % 2], state[(c + 1) % 2]
            m_o = None
            if c:
                for kk in range(2):
                    m_o = T(pe.matmul, bank[t][part, :], qt[:, kk, tok], now[:, kk, :], start=False,
                            stop=True, skip_group_check=True, after=(m_s,))
            if c < 2 * NT - 1:
                for kk in range(2):
                    b = 2 + kk + 2 * (c % 2)
                    m = T(pe.matmul, bank[b][:, :], e1[part, t, kk * P:(kk + 1) * P], v[part, t, :],
                          start=True, stop=True, after=(m_kd, m_s))
                    if c:
                        m_s = V(dve.scalar_tensor_tensor, nxt[:, kk, :], now[:, kk, :], dk[:, kk, c:c + 1],
                                bank[b][:, :], ALU.mult, ALU.add, after=(m, m_dk, m_o, m_s))
                    else:
                        m_s = V(dve.tensor_copy, nxt[:, kk, :], bank[b][:, :], after=(m,))
        for t in range(NT):
            m_sg = A(act.activation, gg[:, t, :], gg[:, t, :], ACT.Silu, after=(m_g,))
        hold(TP[0], m_att)
        at["turn"] = 1
        for t in range(NT):
            mo = A(act.activation, o[:, t, :], bank[t][:, :], ACT.Copy, after=(m_o,))
            ms = V(dve.tensor_tensor_reduce, v[:, t, :], o[:, t, :], o[:, t, :], 1.0, 0.0, ALU.mult, ALU.add,
                   osum[:, t, :], after=(mo,))
            ms = inverse_root(osum[:, t, :], osum[:, t, :], GLA_V, 1e-5, ms)
            ms = V(dve.scalar_tensor_tensor, o[:, t, :], o[:, t, :], osum[:, t, :], gnw, ALU.mult, ALU.mult,
                   after=(ms,))
            ms = V(dve.tensor_tensor, o[:, t, :], o[:, t, :], gg[:, t, :], ALU.mult, after=(ms, m_sg))
            transpose4(o[:, t, :], h * 4, t, ms)

    room = Room()
    total, gate, grow = room(NT, D), room(NT, D), room(D)
    wait(pe, pr.dve.now())
    branch_sum(i["w_gla_branch"][0], 1)
    load(gate, rows(proj)[:, :, COL_GATE + D:COL_GATE + 2 * D])
    loaded = load(grow, row_of(i["gate_bias"][0, 1], D))
    m = gated_total(loaded)
    loaded = load(gate, rows(gated), m)
    for t in range(NT):
        m = V(dve.tensor_tensor, total[:, t, :], total[:, t, :], gate[:, t, :], ALU.add, after=(loaded, m))
    transpose_all(total, 0, m)
    wait(dve, pr.pe.now())
    segment(i["w_out"][0], 0, D // BLK, 0, to_sum(total, False))
    drained()

    def residual_norm(source, g_row, b_row, dest, *after):
        big = room_n(NT, D)
        grow, brow, mean, var = room_n(D), room_n(D), room_n(2, 1), room_n(2, 1)
        load(big, source, *after)
        load(grow, row_of(g_row, D))
        loaded = load(brow, row_of(b_row, D))
        for t in range(NT):
            m = V(dve.scalar_tensor_tensor, total[:, t, :], big[:, t, :], ALPHA, total[:, t, :], ALU.mult, ALU.add,
                  after=(loaded, s_drv.now()))
            m = V(dve.tensor_reduce, mean[:, t, :], total[:, t, :], AX, ALU.add, after=(m,))
            m = V(dve.tensor_scalar, mean[:, t, :], mean[:, t, :], 1.0 / D, None, ALU.mult, after=(m,))
            m = V(dve.tensor_scalar, total[:, t, :], total[:, t, :], mean[:, t, :], None, ALU.subtract, after=(m,))
            ma = A(act.activation, big[:, t, :], total[:, t, :], ACT.Square, accum_out=var[:, t, :], after=(m,))
            m = inverse_root(var[:, t, :], var[:, t, :], D, 1e-5, ma)
            m = V(dve.scalar_tensor_tensor, total[:, t, :], total[:, t, :], var[:, t, :], grow, ALU.mult, ALU.mult,
                  after=(m,))
            m = V(dve.tensor_tensor, total[:, t, :], total[:, t, :], brow, ALU.add, after=(m,))
        return m, store(rows(dest), total, m)

    room_n = Room(room.at - 3 * D)
    m, stored = residual_norm(rows(i["x"][0]), i["ln1_g"][0], i["ln1_b"][0], residual, pr.dve.now())
    transpose_all(total, 0, m)
    wait(dve, pr.pe.now(), stored)

    hid = Room(NT * D)(2, NT, BLK)
    m0 = V(dve.memset, total, 0.0)
    wait(dve, m0)
    with pr.loop(FF // D) as f:
        total_marks.clear()
        wait(dve, s_drv.now())

        def to_hidden(j):
            def drain(half, n):
                free(dve, ("hid", half))
                wait(dve, summed())
                for t in range(NT):
                    b = bank[2 * half + t][:, 0:n]
                    m1 = V(dve.tensor_scalar, hid[:, half, t, :], b, 0.0, None, ALU.max)
                    wait(dve, m1)
                    last = dve.tensor_tensor(hid[:, half, t, :], hid[:, half, t, :], b, ALU.mult)
                full = s_drv.up(last)
                for t in range(NT):
                    m = transpose4(hid[:, half, t, :], KT + 4 * j, t, full)
                hold(("hid", half), pr.pe.now())
            return drain
        for j in range(D // BLK):
            block(weight_at(i["w_up"][0], f * D + j * BLK, BLK), 0, KT, BLK, to_hidden(j))
        drained()

        def down(q, j):
            w = i["w_down"][0].rearrange("(f k p) n -> f p k n", p=P, k=KT)
            return w[ds(f_sp, 1), :, q * QK:(q + 1) * QK, j * BLK:(j + 1) * BLK].rearrange("a p k n -> (a p) k n")
        wait(pe, pr.dve.now())
        for j in range(D // BLK):
            f_sp = sp.snap(f)
            block(lambda q, j=j: down(q, j), KT, KT, BLK, to_sum(total, True)(j))
        drained()
        m_down = s_drv.now()
    room_n = Room(NT * D)
    m, stored = residual_norm(rows(residual), i["ln2_g"][0], i["ln2_b"][0], residual, m_down, stored)

    if debug and "stop1" in debug:
        return finish(pr, out, total, m)

    pr.meet()
    wait(act, stored)
    with pr.loop(LAYERS) as l:
        def row2(w, n):
            return w.rearrange("(a l) n -> a (l n)", a=1)[:, ds(l * n, n)].partition_broadcast(P)

        def weight2(w, row_tiles, col, n):
            w = w.rearrange("l (k p) n -> p (l k) n", p=P)
            kts = min(QK, row_tiles)

            def get(q):
                first = sp.snap(l * row_tiles + q * kts)
                c = col if isinstance(col, int) else sp.snap(col)
                return w[:, ds(first, kts), ds(c, n)]
            return get

        def segment2(w, blocks, drain):
            def one(j):
                block(weight2(w, KT, j * BLK, BLK), 0, KT, BLK, drain(j))
            for j in range(blocks):
                one(j)

        room = Room()
        xr, hn, grow, ssq = room(NT, D), room(NT, D), room(D), room(2, 1)
        load(xr, rows(residual))
        loaded = load(grow, row2(i["norm_pre_2"], D))
        for t in range(NT):
            m = A(act.activation, hn[:, t, :], xr[:, t, :], ACT.Square, accum_out=ssq[:, t, :], after=(loaded,))
            m = inverse_root(ssq[:, t, :], ssq[:, t, :], D, 1e-6, m)
            m = V(dve.scalar_tensor_tensor, hn[:, t, :], xr[:, t, :], ssq[:, t, :], grow, ALU.mult, ALU.mult,
                  after=(m,))
        transpose_all(hn, 0, m)
        segment2(i["w_in_2"], N_IN2 // BLK, to_dram(proj2, 0))
        rest = N_IN2 % BLK
        block(weight2(i["w_in_2"], KT, N_IN2 - rest, rest), 0, KT, rest, to_dram(proj2, N_IN2 - rest)(0))
        drained()

        pr.meet()
        room = Room()
        DR = 2 * ROWS - 1
        DC = 2 * WIN_C - 1
        osum = room(NT, D)
        edge = room(P)
        m = V(dve.memset, edge, 0.0)
        rpb = i["c_rpb_2"].rearrange("l h a b -> (l h) a b")
        for hh in range(C_H):
            loaded = load(edge[hh * DR:(hh + 1) * DR, GRID - WIN_C:GRID - WIN_C + DC],
                          rpb[ds(l * C_H + hh, 1), WIN_R - ROWS:WIN_R - ROWS + DR, :].rearrange("a r c -> (a r) c"), m)
        skewed = store(skew, wide(edge[0:C_H * DR, :].unsqueeze(1), [C_H * DR, GRID, P]), loaded)

        cq, ckv = room(NT, B_QL), room(NT, B_KVL)
        gq, gkv, sq = room(B_QL), room(B_KVL), room(4, 1)
        junk = room(B_QL)
        wait(act, s_st[0].now(), s_st[1].now())
        load(cq, rows(proj2)[:, :, C2_CQ:C2_CQ + B_QL])
        load(ckv, rows(proj2)[:, :, C2_CKV:C2_CKV + B_KVL])
        load(gq, row2(i["b_q_norm_2"], B_QL))
        loaded = load(gkv, row2(i["b_kv_norm_2"], B_KVL))
        ma = None
        for n, (x, g, w, tiles) in enumerate(((cq, gq, B_QL, 4), (ckv, gkv, B_KVL, 2))):
            for t in range(NT):
                s = sq[:, 2 * n + t, :]
                ma = A(act.activation, junk[:, 0:w], x[:, t, :], ACT.Square, accum_out=s, after=(loaded, ma))
                m = inverse_root(s, s, w, 1e-6, ma)
                m = V(dve.scalar_tensor_tensor, x[:, t, :], x[:, t, :], s, g, ALU.mult, ALU.mult, after=(m,))
                m = transpose4(x[:, t, :], KT + 4 * n, t, m, tiles=tiles)
        wait(pe, m)
        for col, n in ((0, BLK), (BLK, B_H * (HD + B_ROPE) - BLK)):
            block(weight2(i["b_w_uq_2"], B_QL // P, col, n), KT, B_QL // P, n, to_dram(latent, col)(0))
        for col in (0, BLK):
            block(weight2(i["b_w_ukv_2"], B_KVL // P, col, BLK), KT + 4, B_KVL // P, BLK,
                  to_dram(latent, 2 * BLK + col)(0))
        drained()
        wait(act, s_st[0].now(), s_st[1].now())

        UW = UNIT_H * HD
        pr.meet()
        room = Room(NT * D)
        small = room(6, 8)
        work_at = room.at

        def rope(x, heads, n, cos, sin, tmp, *after):
            q4 = n // 4
            split = lambda a: a.rearrange("p h (b s e) -> p h b s e", b=2, s=2)
            xs, ts = split(x), split(tmp)
            ss = sin.rearrange("p (b s e) -> p b s e", b=2, s=2)
            for s in range(2):
                for hh in range(heads):
                    m = V(dve.tensor_tensor, ts[:, hh, :, s, :], xs[:, hh, :, 1 - s, :], ss[:, :, s, :], ALU.mult,
                          after=after)
            m2 = V(dve.tensor_tensor, x, x, wide(cos.unsqueeze(1), [P, heads, n]), ALU.mult, after=(m,))
            return V(dve.tensor_tensor, x, x, tmp, ALU.add, after=(m2,))

        def head_norm(x, n, g, stat, tmp, *after):
            m = V(dve.tensor_tensor, tmp, x, x, ALU.mult, after=after)
            m = V(dve.tensor_reduce, stat, tmp, AX, ALU.add, after=(m,))
            m = inverse_root(stat, stat, HD, 1e-6, m)
            m = V(dve.tensor_tensor, x, x, wide(stat.unsqueeze(2), [P, n, HD]), ALU.mult, after=(m,))
            return V(dve.tensor_tensor, x, x, wide(g.unsqueeze(1), [P, n, HD]), ALU.mult, after=(m,))

        def turn_heads(to, source, banks, width, *after):
            heads = to.shape[1]
            for hh in range(heads):
                b = bank[banks[hh // 2 % len(banks)]]
                for t in range(NT):
                    m = T(pe.transpose, b[0:width, (hh % 2) * S + t * P:(hh % 2) * S + (t + 1) * P],
                          source(hh, t), ident[:, :], after=after)
                if hh % 2 or hh == heads - 1:
                    n = hh % 2 + 1
                    m = A(act.activation, to[0:width, hh - n + 1:hh + 1, :],
                          b[0:width, 0:n * S].rearrange("p (h n) -> p h n", h=n), ACT.Copy, after=(m,))
            return m

        def attend(parts, value, probs, pt, scale, bias, out_col, gate, m_gate, *after):
            m_p = []
            for t in range(NT):
                tok = slice(t * P, (t + 1) * P)
                for hh in range(UNIT_H):
                    o_ = bank[2 * t + hh // 2][:, (hh % 2) * S:(hh % 2 + 1) * S]
                    for n, (qf, kf) in enumerate(parts):
                        m = T(pe.matmul, o_, qf(hh)[:, tok], kf(hh), start=(n == 0), stop=(n == len(parts) - 1),
                              after=after)
                pb = probs[t]
                top, tot = small[:, t, 0:4], small[:, 2 + t, 0:4]
                mm = []
                for n in range(2):
                    sc = bank[2 * t + n][:, :].rearrange("p (h n) -> p h n", h=2)
                    if bias is not None:
                        ms = V(dve.scalar_tensor_tensor, pb[:, 2 * n:2 * n + 2, :], sc, scale,
                               bias[:, t, 2 * n:2 * n + 2, :], ALU.mult, ALU.add, after=(m,))
                        ms = V(dve.tensor_reduce, top[:, 2 * n:2 * n + 2], pb[:, 2 * n:2 * n + 2, :], AX, ALU.max,
                               after=(ms,))
                    else:
                        ms = V(dve.tensor_reduce, top[:, 2 * n:2 * n + 2], sc, AX, ALU.max, after=(m,))
                sf = 1.0 if bias is not None else scale
                ms = V(dve.tensor_scalar, top, top, -sf, None, ALU.mult, after=(ms,))
                for hh in range(UNIT_H):
                    src = pb[:, hh, :] if bias is not None else bank[2 * t + hh // 2][:, (hh % 2) * S:(hh % 2 + 1) * S]
                    me = A(act.activation, pb[:, hh, :], src, ACT.Exp, bias=top[:, hh:hh + 1], scale=sf,
                           accum_out=tot[:, hh:hh + 1], after=(ms,))
                V(dve.reciprocal, tot, tot, after=(me,))
                m_p.append(me)
            m_v = None
            for t in range(NT):
                for hh in range(UNIT_H):
                    b = bank[4 + hh // 2]
                    for kt in range(NT):
                        m = T(pe.transpose, b[:, ((hh % 2) * NT + kt) * P:((hh % 2) * NT + kt + 1) * P],
                              probs[t][:, hh, kt * P:(kt + 1) * P], ident[:, :], after=(m_p[t],))
                    if hh % 2:
                        m = A(act.activation, pt[:, hh - 1:hh + 1, :], b[:, :].rearrange("p (h n) -> p h n", h=2),
                              ACT.Copy, after=(m, m_v))
                o_ = bank[6 + t]
                for hh in range(UNIT_H):
                    for kt in range(NT):
                        m_v = T(pe.matmul, o_[:, hh * HD:(hh + 1) * HD], pt[:, hh, kt * P:(kt + 1) * P],
                                value(hh, kt), start=(kt == 0), stop=(kt == NT - 1), after=(m,))
                to = osum[:, t, out_col:out_col + UW]
                m = V(dve.tensor_tensor, to.rearrange("p (h n) -> p h n", h=UNIT_H),
                      o_[:, :].rearrange("p (h n) -> p h n", h=UNIT_H),
                      wide(small[:, 2 + t, 0:4].unsqueeze(2), [P, UNIT_H, HD]), ALU.mult, after=(m_v, pr.dve.now()))
                ms = A(act.activation, gate[:, t, :], gate[:, t, :], ACT.Silu, after=(m_gate,))
                V(dve.tensor_tensor, to, to, gate[:, t, :], ALU.mult, after=(m, ms))

        heads_of = lambda a: a.rearrange("p t (h n) -> p (t h) n", n=HD)
        p2 = rows(proj2)
        for unit in range(A_KV):
            pr.meet()
            room = Room(work_at)
            q, k, v, gt2 = room(NT, UW), room(NT, HD), room(NT, HD), room(NT, UW)
            qt, kt_, pt = room(UNIT_H, S), room(1, S), room(UNIT_H, S)
            tmp, tmp2 = room(NT, UW), room(NT, UW)
            gq, gk2, cos, sin = room(HD), room(HD), room(NT, HD), room(NT, HD)
            load(q, p2[:, :, C2_AQ + unit * UW:C2_AQ + (unit + 1) * UW])
            load(k, p2[:, :, C2_AK + unit * HD:C2_AK + (unit + 1) * HD])
            load(v, p2[:, :, C2_AV + unit * HD:C2_AV + (unit + 1) * HD])
            load(gq, row2(i["a_q_norm_2"], HD))
            load(gk2, row2(i["a_k_norm_2"], HD))
            load(cos, rows(i["cos128"]))
            m_in = load(sin, rows(i["sin128"]))
            m_gate = load(gt2, p2[:, :, C2_AG + unit * UW:C2_AG + (unit + 1) * UW], count=d_late)
            mq = head_norm(heads_of(q), NT * UNIT_H, gq, small[:, 4, :], heads_of(tmp), m_in)
            mk = head_norm(k, NT, gk2, small[:, 5, 0:2], tmp2[:, :, 0:HD], m_in)
            for t in range(NT):
                mq = rope(q[:, t, :].rearrange("p (h n) -> p h n", n=HD), UNIT_H, HD, cos[:, t, :], sin[:, t, :],
                          tmp[:, t, :].rearrange("p (h n) -> p h n", n=HD), mq)
                mk = rope(k[:, t:t + 1, :], 1, HD, cos[:, t, :], sin[:, t, :], tmp2[:, t:t + 1, 0:HD], mk)
            m1 = turn_heads(qt, lambda h, t: q[:, t, h * HD:(h + 1) * HD], (4, 5), HD, mq)
            m2 = turn_heads(kt_, lambda h, t: k[:, t, :], (6,), HD, mk)
            attend([(lambda h: qt[:, h, :], lambda h: kt_[:, 0, :])], lambda h, kt: v[:, kt, :],
                   [a.rearrange("p t n -> p (t n)").rearrange("p (h n) -> p h n", h=UNIT_H) for a in (tmp, tmp2)],
                   pt, HD ** -0.5, None, unit * UW, gt2, m_gate, m1, m2)

        pr.meet()
        room = Room(work_at)
        QW = HD + B_ROPE
        q, kv, kr = room(NT, B_H * QW), room(NT, B_H * 2 * HD), room(NT, B_ROPE)
        cos, sin = room(NT, B_ROPE), room(NT, B_ROPE)
        qt, kt_, pt = room(B_H, S), room(B_H, S), room(UNIT_H, S)
        qpe, kpe = room(B_H, S), room(1, S)
        tmp = room(B_H, B_ROPE)
        gt2 = room(NT, UW)
        lat = rows(latent)
        load(q, lat[:, :, 0:B_H * QW])
        load(kv, lat[:, :, 2 * BLK:4 * BLK])
        load(kr, p2[:, :, C2_KR:C2_KR + B_ROPE])
        load(cos, rows(i["cos64"]))
        m_in = load(sin, rows(i["sin64"]))
        m_gate = load(gt2, p2[:, :, C2_BG:C2_BG + UW], count=d_late)
        m = m_in
        for t in range(NT):
            m = rope(q[:, t, :].rearrange("p (h n) -> p h n", n=QW)[:, :, HD:QW], B_H, B_ROPE, cos[:, t, :],
                     sin[:, t, :], tmp, m)
            m = rope(kr[:, t:t + 1, :], 1, B_ROPE, cos[:, t, :], sin[:, t, :], tmp[:, 0:1, :], m)
        turn_heads(qt, lambda h, t: q[:, t, h * QW:h * QW + HD], (0, 1), HD, m)
        turn_heads(kt_, lambda h, t: kv[:, t, h * 2 * HD:h * 2 * HD + HD], (2, 3), HD, m)
        turn_heads(qpe, lambda h, t: q[:, t, h * QW + HD:(h + 1) * QW], (4, 5), B_ROPE, m)
        m = turn_heads(kpe, lambda h, t: kr[:, t, :], (6,), B_ROPE, m)
        flat_q = q.rearrange("p t n -> p (t n)")
        attend([(lambda h: qt[:, h, :], lambda h: kt_[:, h, :]),
                (lambda h: qpe[0:B_ROPE, h, :], lambda h: kpe[0:B_ROPE, 0, :])],
               lambda h, kt: kv[:, kt, h * 2 * HD + HD:(h + 1) * 2 * HD],
               [probs_b(stage, t) for t in range(NT)], pt, QW ** -0.5, None, A_H * HD, gt2, m_gate, m)

        pr.meet()
        room = Room(work_at)
        q, k, v, gt2 = room(NT, UW), room(NT, UW), room(NT, UW), room(NT, UW)
        qt, kt_, pt = room(C_H, S), room(C_H, S), room(UNIT_H, S)
        bias, mask = room(NT, C_H * S), room(NT, S)
        for to, c in ((q, C2_Q), (k, C2_K), (v, C2_V)):
            load(to, p2[:, :, c:c + UW])
        wait(act, skewed)
        load(mask, rows(i["window"]))
        for r in range(ROWS):
            part = slice((r % 2) * GRID, (r % 2 + 1) * GRID)
            for hh in range(C_H):
                m_in = load(bias[part, r // 2, hh * S:(hh + 1) * S].rearrange("p (a b) -> p a b", a=ROWS),
                            bass.AP(skew.tensor, (hh * DR + ROWS - 1 - r) * GRID * P + GRID - 1,
                                    [[P - 1, GRID], [GRID * P, ROWS], [1, GRID]]))
        m_gate = load(gt2, p2[:, :, C2_G:C2_G + UW], count=d_late)
        for t in range(NT):
            bt = bias[:, t, :].rearrange("p (h n) -> p h n", h=C_H)
            mb = V(dve.tensor_tensor, bt, bt, wide(mask[:, t, :].unsqueeze(1), [P, C_H, S]), ALU.add, after=(m_in,))
        turn_heads(qt, lambda h, t: q[:, t, h * HD:(h + 1) * HD], (0, 1), HD, m_in)
        m = turn_heads(kt_, lambda h, t: k[:, t, h * HD:(h + 1) * HD], (2, 3), HD, m_in)
        attend([(lambda h: qt[:, h, :], lambda h: kt_[:, h, :])], lambda h, kt: v[:, kt, h * HD:(h + 1) * HD],
               [a.rearrange("p t n -> p (t n)").rearrange("p (h n) -> p h n", h=UNIT_H) for a in (q, k)],
               pt, HD ** -0.5, bias.rearrange("p t (h n) -> p t h n", h=C_H), (A_H + B_H) * HD, gt2, m_gate, m, mb)

        pr.meet()
        transpose_all(osum, 0, pr.dve.now())
        total = osum
        total_marks.clear()
        wait(dve, pr.pe.now())
        segment2(i["w_out_2"], D // BLK, to_sum(total, False))
        drained()
        room = Room(NT * D)
        xr, grow, junk2, sq2 = room(NT, D), room(D), room(D), room(2, 1)
        load(xr, rows(residual), pr.pe.now(), pr.dve.now())
        loaded = load(grow, row2(i["norm_post_2"], D))
        wait(act, s_drv.now(), pr.dve.now())
        ma = None
        for t in range(NT):
            ma = A(act.activation, junk2, total[:, t, :], ACT.Square, accum_out=sq2[:, t, :], after=(ma,))
            m = inverse_root(sq2[:, t, :], sq2[:, t, :], D, 1e-6, ma)
            m = V(dve.scalar_tensor_tensor, total[:, t, :], total[:, t, :], sq2[:, t, :], grow, ALU.mult, ALU.mult,
                  after=(m, loaded))
            m = V(dve.tensor_tensor, total[:, t, :], total[:, t, :], xr[:, t, :], ALU.add, after=(m,))
        stored = store(rows(residual), total, m)
        wait(act, stored)

    return finish(pr, out, total, pr.dve.now())


def probs_b(stage, t):
    return stage[:, t, :, :].rearrange("p a n -> p (a n)").rearrange("p (h n) -> p h n", h=UNIT_H)


def finish(pr, out, value, *after):
    act = pr.nc.scalar
    pr.wait(act, *after)
    d_out = pr.counts["d_out"]
    d_out.up(act.dma_start(out[0].rearrange("(t p) n -> p t n", p=P), value))
    pr.wait(act, d_out.now(), pr.counts["s_st0"].now(), pr.counts["s_st1"].now())
    return pr.found


def constants():
    j, t = np.arange(P)[:, None], np.arange(P)[None, :]
    same = (j // GLA_C) == (t // GLA_C)
    most = np.where((j % GLA_C) <= np.arange(GLA_C)[None, :], np.finfo(np.float32).max, 0.0)
    c = {"most64": most, "least64": -most, "identity": j == t, "causal": j <= t, "causal64": (j <= t) & same, "blocks64": same,
         "columns64": (np.arange(P)[:, None] // GLA_C) == np.arange(2)[None, :]}
    tok = np.arange(S)
    for n, name in ((HD, "128"), (B_ROPE, "64")):
        half = n // 2
        freq = (np.float32(1.0) / (np.float32(10000.0) ** (np.arange(0, half, 2, dtype=np.float32) / np.float32(half)))).astype(np.float32)
        parts_c, parts_s = [], []
        for pos in (tok // GRID, tok % GRID):
            ang = pos.astype(np.float32)[:, None] * freq[None, :]
            parts_c += [np.cos(ang), np.cos(ang)]
            parts_s += [-np.sin(ang), np.sin(ang)]
        c["cos" + name], c["sin" + name] = np.concatenate(parts_c, 1), np.concatenate(parts_s, 1)
    col = tok % GRID
    first = np.clip(col - WIN_C // 2, 0, GRID - WIN_C)[:, None]
    c["window"] = np.where((col[None, :] >= first) & (col[None, :] < first + WIN_C), 0.0, MASKED)
    return {k: np.ascontiguousarray(v, dtype=np.float32) for k, v in c.items()}


def conv_layout(w, b):
    both = np.concatenate([w[0], b], axis=0)
    x, bc = both[:, :SSD_IN], both[:, SSD_IN:]
    x = x.reshape(CONV_W + 1, SSD_G, CONV_T - 2, P)
    bc = bc.reshape(CONV_W + 1, 2, SSD_G, P).transpose(0, 2, 1, 3)
    both = np.concatenate([x, bc], axis=2)
    return np.ascontiguousarray(both.transpose(1, 3, 2, 0).reshape(SSD_G, P, CONV_T * (CONV_W + 1)))


def build(nc, shapes, out_shape, debug=None):
    def one(nc, gains):
        i = {n: nc.dram_tensor(f"in_{n}", s, F32, kind="ExternalInput").ap() for n, s in shapes.items()}
        out = nc.dram_tensor("out", out_shape, F32, kind="ExternalOutput").ap()
        with ExitStack() as ctx:
            return emit(nc, ctx, gains, i, out, debug)
    return one


def kernel(**inputs):
    import concourse.bacc as bacc
    from concourse.bass_utils import run_bass_kernel_spmd

    arrays = {n: np.ascontiguousarray(a) for n, a in inputs.items() if n not in ("ssd_conv_w", "ssd_conv_b")}
    arrays["conv"] = conv_layout(np.asarray(inputs["ssd_conv_w"]), np.asarray(inputs["ssd_conv_b"]))
    arrays.update(constants())
    shapes = {n: a.shape for n, a in arrays.items()}
    one = build(None, shapes, (1, S, D))
    gains = one(bacc.Bacc("TRN2", target_bir_lowering=False, num_devices=1), {})
    nc = bacc.Bacc("TRN2", target_bir_lowering=False, num_devices=1)
    one(nc, gains)
    r = run_bass_kernel_spmd(nc, [{f"in_{n}": a for n, a in arrays.items()}], core_ids=[0])
    return r.results[0]["out"]
```

```python
from contextlib import ExitStack, contextmanager

import numpy as np

import concourse.bass as bass
import concourse.mybir as mybir

F32 = mybir.dt.float32
F32R = mybir.dt.float32r
ALU = mybir.AluOpType
ACT = mybir.ActivationFunctionType
AX = mybir.AxisListType.X
ds = bass.ds

P = 128
S = 256
NT = S // P
D = 2048
KT = D // P
QK = 2
BLK = 512
RAW_RING = 4
SPLIT_RING = 8
AHEAD = 4
PIECES = KT // QK

SSD_IN = 2 * D
SSD_G, SSD_HG, SSD_P, SSD_N = 8, 8, 64, 128
SSD_H = SSD_G * SSD_HG
CONV_W = 4
CONV_T = 6
GLA_H, GLA_K, GLA_V, GLA_C, GLA_R = 4, 256, 512, 64, 16
FF = 4 * D
ALPHA = 2.0 ** 0.25
COL_Z = 0
COL_XBC = SSD_IN
COL_DT = COL_XBC + SSD_IN + 2 * SSD_G * SSD_N
COL_Q = COL_DT + SSD_H
COL_K = COL_Q + GLA_H * GLA_K
COL_V = COL_K + GLA_H * GLA_K
COL_G = COL_V + D
COL_GK = COL_G + D
COL_GATE = COL_GK + GLA_R
N_IN = COL_GATE + 2 * D

LAYERS = 2
HD = 128
A_H, A_KV, B_H, C_H = 8, 2, 4, 4
B_QL, B_KVL, B_ROPE = 512, 256, 64
GRID = 64
ROWS = S // GRID
WIN_R, WIN_C = 8, 16
UNIT_H = 4
C2_AQ = 0
C2_AK = C2_AQ + A_H * HD
C2_AV = C2_AK + A_KV * HD
C2_AG = C2_AV + A_KV * HD
C2_CQ = C2_AG + A_H * HD
C2_CKV = C2_CQ + B_QL
C2_KR = C2_CKV + B_KVL
C2_BG = C2_KR + B_ROPE
C2_Q = C2_BG + B_H * HD
C2_K = C2_Q + C_H * HD
C2_V = C2_K + C_H * HD
C2_G = C2_V + C_H * HD
N_IN2 = C2_G + C_H * HD
MASKED = -1.0e30

INPUTS = ["x", "w_in", "conv", "ssd_dt_bias", "ssd_A_log", "ssd_D", "ssd_norm_w", "gla_gk_w", "gla_gk_b",
          "gla_norm_w", "w_ssd_branch", "w_gla_branch", "gate_bias", "w_out", "ln1_g", "ln1_b", "w_up",
          "w_down", "ln2_g", "ln2_b", "norm_pre_2", "norm_post_2", "w_in_2", "a_q_norm_2", "a_k_norm_2",
          "b_q_norm_2", "b_kv_norm_2", "b_w_uq_2", "b_w_ukv_2", "c_rpb_2", "w_out_2"]


class Count:

    def __init__(self, prog, name, step=1):
        self.prog, self.name, self.step, self.n = prog, name, step, 0
        self.sem = prog.ctx.enter_context(prog.nc.semaphore(name))

    def up(self, instruction):
        instruction.then_inc(self.sem, self.step)
        self.n += self.step
        return self.now()

    def now(self, back=0):
        return Mark(self, self.n - back * self.step, tuple(self.prog.loops))


class Mark:
    def __init__(self, count, n, loops):
        self.count, self.n, self.loops = count, n, loops


class Loop:
    def __init__(self, prog, key, index, trips):
        self.key, self.index, self.trips = key, index, trips
        self.gain = prog.gains.get(key, {})


class Prog:

    def __init__(self, nc, ctx, gains):
        self.nc, self.ctx, self.gains, self.found = nc, ctx, gains, {}
        self.loops, self.counts, self.held, self.seen = [], {}, {}, {}
        self.n_loops = 0
        self.boundary = lambda: None
        self.pe = self.count("pe")
        self.act = self.count("act")
        self.dve = self.count("dve")
        self.pool = self.count("pool")

    def count(self, name, step=1):
        self.counts[name] = Count(self, name, step)
        return self.counts[name]

    def wait(self, engine, *marks):
        for m in marks:
            if m is None:
                continue
            open_at = tuple(x for x in m.loops if x in self.loops)
            known = self.seen.get((engine, m.count.name))
            if m.loops == open_at and known and known[0] == m.loops and known[1] >= m.n:
                continue
            if m.loops == open_at:
                self.seen[engine, m.count.name] = (m.loops, m.n)
            value, index = m.n, None
            for loop in m.loops:
                gain = loop.gain.get(m.count.name, 0)
                if not gain:
                    continue
                if loop in self.loops:
                    term = loop.index * gain
                    index = term if index is None else index + term
                else:
                    value += (loop.trips - 1) * gain
            if index is None:
                if value > 0:
                    engine.wait_ge(m.count.sem, value)
            else:
                assert value > 0, m.count.name
                engine.wait_ge(m.count.sem, index + value)

    @contextmanager
    def loop(self, trips, apart=True):
        self.boundary()
        if apart:
            self.meet()
        key = self.n_loops
        self.n_loops += 1
        before = {k: c.n for k, c in self.counts.items()}
        self.seen = {}
        with self.nc.Fori(0, trips) as index:
            loop = Loop(self, key, index, trips)
            self.loops.append(loop)
            yield index
            self.boundary()
            if apart:
                self.meet()
            self.loops.pop()
        self.seen = {}
        self.found[key] = {}
        for k, c in self.counts.items():
            gain = c.n - before.get(k, 0)
            if gain:
                self.found[key][k] = gain
                c.n += (trips - 1) * gain
        if self.gains:
            assert self.found[key] == loop.gain, (key, self.found[key], loop.gain)

    def meet(self):
        nc = self.nc
        mine = [(nc.tensor, self.pe), (nc.scalar, self.act), (nc.vector, self.dve), (nc.gpsimd, self.pool)]
        for engine, _ in mine:
            for _, other in mine:
                self.wait(engine, other.now())
        self.held = {}

    def hold(self, what, *marks):
        self.held[what] = marks

    def free(self, engine, what):
        self.wait(engine, *self.held.get(what, ()))

    def T(self, f, *args, after=(), **kw):
        self.wait(self.nc.tensor, *after)
        return self.pe.up(f(*args, **kw))

    def A(self, f, *args, after=(), **kw):
        self.wait(self.nc.scalar, *after)
        return self.act.up(f(*args, **kw))

    def V(self, f, *args, after=(), **kw):
        self.wait(self.nc.vector, *after)
        return self.dve.up(f(*args, **kw))

    def G(self, f, *args, after=(), **kw):
        self.wait(self.nc.gpsimd, *after)
        return self.pool.up(f(*args, **kw))


def wide(ap, shape):
    return ap.to_broadcast(list(shape))


def emit(nc, ctx, gains, i, out, debug=None):
    pr = Prog(nc, ctx, gains)
    T, A, V, G, wait, hold, free = pr.T, pr.A, pr.V, pr.G, pr.wait, pr.hold, pr.free
    pe, act, dve, pool, sp = nc.tensor, nc.scalar, nc.vector, nc.gpsimd, nc.sync

    def sb(name, shape, dt=F32):
        return ctx.enter_context(nc.sbuf_tensor(name, shape, dt))

    def scratch(name, shape):
        kind = "ExternalOutput" if debug is not None and name in debug else "Internal"
        return nc.dram_tensor(name, shape, F32, kind=kind).ap()

    raw = sb("raw", [P, RAW_RING, QK, BLK])
    w_hi = sb("w_hi", [P, SPLIT_RING, QK, BLK], F32R)
    w_lo = sb("w_lo", [P, SPLIT_RING, QK, BLK], F32R)
    x_hi = sb("x_hi", [P, 2 * KT, S], F32R)
    x_lo = sb("x_lo", [P, 2 * KT, S], F32R)
    stage = sb("stage", [P, 2, NT, BLK])
    arena = sb("arena", [P, 14080])
    ident = sb("ident", [P, P])
    bank = [ctx.enter_context(nc.psum_tensor(f"bank{b}", [P, BLK], F32)) for b in range(8)]

    class Room:

        def __init__(self, at=0):
            self.at = at

        def __call__(self, *shape):
            n = int(np.prod(shape))
            a = arena[:, self.at:self.at + n]
            self.at += n
            assert self.at <= arena.shape[1], self.at
            if len(shape) == 2:
                a = a.rearrange("p (a b) -> p a b", a=shape[0])
            if len(shape) == 3:
                a = a.rearrange("p (a b c) -> p a b c", a=shape[0], b=shape[1])
            return a

    proj = scratch("proj", [S, N_IN])
    proj2 = scratch("proj2", [S, N_IN2])
    latent = scratch("latent", [S, 2048])
    residual = scratch("residual", [S, D])
    gated = scratch("gated", [S, D])
    heads_y = scratch("heads_y", [S, SSD_IN])
    heads_o = scratch("heads_o", [S, D])
    skew = scratch("skew", [C_H * (2 * ROWS - 1), GRID, P])

    def rows(ap):
        return ap.rearrange("(t p) n -> p t n", p=P)

    s_raw = [pr.count(f"s_raw{n}", 16) for n in range(RAW_RING)]
    s_hi = pr.count("s_hi")
    s_lo = pr.count("s_lo")
    s_mm = pr.count("s_mm")
    s_dra = pr.count("s_dra")
    s_drv = pr.count("s_drv")
    s_st = [pr.count(f"s_st{n}", 16) for n in range(2)]
    d_in = pr.count("d_in", 16)
    d_late = pr.count("d_late", 16)
    d_gate = pr.count("d_gate", 16)
    d_out = pr.count("d_out", 16)
    at = {"piece": 0, "block": 0, "drain": None, "save": None, "turn": 0, "since": 0, "beside": None,
          "waiting": []}

    def summed():
        return s_mm.now(at["since"])

    def load(to, source, *after, count=d_in):
        wait(act, *after)
        return count.up(act.dma_start(to, source))

    def store(to, source, *after):
        wait(act, *after)
        return d_out.up(act.dma_start(to, source))

    def piece(weight, x0, kts, n, banks, q, pieces):
        slot, half = at["piece"] % RAW_RING, at["piece"] % SPLIT_RING
        at["piece"] += 1
        source = weight()
        wait(sp, s_lo.now(RAW_RING - 1))
        landed = s_raw[slot].up(sp.dma_start(raw[:, slot, 0:kts, 0:n], source))
        wait(act, landed, s_mm.now(SPLIT_RING - 1 - len(at["waiting"])))
        hi = s_hi.up(act.activation(w_hi[:, half, 0:kts, 0:n], raw[:, slot, 0:kts, 0:n], ACT.Copy))
        wait(dve, hi)
        lo = s_lo.up(dve.tensor_tensor(w_lo[:, half, 0:kts, 0:n], raw[:, slot, 0:kts, 0:n],
                                       w_hi[:, half, 0:kts, 0:n].bitcast(F32), ALU.subtract))

        def products():
            first, last = q == 0, q == pieces - 1
            if first:
                wait(pe, s_drv.now())
            wait(pe, lo)
            for k in range(kts):
                for t in range(NT):
                    tok = slice(t * P, t * P + P)
                    a, b = first and k == 0, last and k == kts - 1
                    o = bank[banks + t][:, 0:n]
                    pe.matmul(o, x_hi[:, x0 + k, tok], w_lo[:, half, k, 0:n], start=a, stop=False)
                    pe.matmul(o, x_hi[:, x0 + k, tok], w_hi[:, half, k, 0:n], start=False, stop=False)
                    mm = pe.matmul(o, x_lo[:, x0 + k, tok], w_hi[:, half, k, 0:n], start=False, stop=b)
            s_mm.up(mm)
            at["since"] += 1
            if q % 2 or last:
                step()
        return products

    def caught_up(left=0):
        while len(at["waiting"]) > left:
            at["waiting"].pop(0)()

    def aligned():
        caught_up()
        at["piece"] = 0
        wait(sp, s_lo.now())
        wait(act, s_mm.now())

    pr.boundary = caught_up

    def beside(steps):
        at["beside"] = steps

    def step():
        if at["beside"] is not None:
            next(at["beside"], None)

    def ended():
        caught_up()
        if at["beside"] is not None:
            for _ in at["beside"]:
                pass
        at["beside"] = None

    def drained(late=False):
        if not late:
            caught_up()
        if at["drain"] is not None:
            at["save"] = at["drain"]()
            at["drain"] = None
        if not late:
            saved()

    def saved():
        if at["save"] is not None:
            at["save"]()
            at["save"] = None

    def block(weight, x0, kts, n, drain):
        half = at["block"] % 2
        at["block"] += 1
        pieces = max(1, kts // QK)

        def after(q, products):
            products()
            if q == min(AHEAD, pieces) - 1:
                drained(late=True)
            if q == min(AHEAD + 1, pieces) - 1:
                saved()
            if q == pieces - 1:
                at["since"] = 0
                at["drain"] = lambda: drain(half, n)
        for q in range(pieces):
            products = piece(lambda: weight(q), x0 + q * QK, min(QK, kts), n, 2 * half, q, pieces)
            at["waiting"].append(lambda q=q, products=products: after(q, products))
            caught_up(AHEAD)

    def weight_at(w, col, n):
        w = w.rearrange("(k p) n -> p k n", p=P)
        kts = min(QK, w.shape[1])

        def get(q):
            c = col
            if not isinstance(col, int):
                c = sp.snap(col)
            return w[:, q * kts:(q + 1) * kts, ds(c, n)]
        return get

    def segment(w, col, blocks, x0, drain, n=BLK):
        def one(j):
            block(weight_at(w, j * n + col, n), x0, KT, n, drain(j))

        def again(j):
            at["drain"] = lambda h=(at["block"] - 1) % 2: drain(j)(h, n)
        one(0)
        done = 1
        if blocks > 5:
            turns = (blocks - 1) // 2
            with pr.loop(turns, apart=False) as turn:
                again(turn * 2)
                one(turn * 2 + 1)
                one(turn * 2 + 2)
            again(2 * turns)
            done += 2 * turns
        for j in range(done, blocks):
            one(j)

    def to_dram(dest, col):
        def drain_of(j):
            def drain(half, n):
                wait(act, summed(), s_st[half].now())
                s_dra.up(act.activation(stage[:, half, 0, 0:n], bank[2 * half][:, 0:n], ACT.Copy))
                wait(dve, summed(), s_st[half].now(), s_dra.now())
                s_drv.up(dve.tensor_copy(stage[:, half, 1, 0:n], bank[2 * half + 1][:, 0:n]))
                full = s_drv.now()

                def save():
                    wait(act, full)
                    s_st[half].up(act.dma_start(rows(dest)[:, :, ds(j * BLK + col, n)], stage[:, half, :, 0:n]))
                return save
            return drain
        return drain_of

    def to_sum(total, add):
        def drain_of(j):
            def drain(half, n):
                wait(dve, summed())
                for t in range(NT):
                    to = total[:, t, j * BLK:j * BLK + n]
                    b = bank[2 * half + t][:, 0:n]
                    if add:
                        wait(dve, total_marks.get(j))
                        last = dve.tensor_tensor(to, b, to, ALU.add)
                    else:
                        last = dve.tensor_copy(to, b)
                total_marks[j] = s_drv.up(last)
            return drain
        return drain_of
    total_marks = {}

    TP = (6, 7)

    def transpose4(source, x0, t, *after, tiles=4):
        b = TP[at["turn"] % 2]
        at["turn"] += 1
        free(pe, b)
        wait(pe, *after)
        for k in range(tiles):
            last = pe.transpose(bank[b][:, k * P:(k + 1) * P], source[:, k * P:(k + 1) * P], ident[:, :])
        turned = pr.pe.up(last)
        full = bank[b][:, 0:tiles * P].rearrange("p (k n) -> p k n", k=tiles)
        hi, lo = x_hi[:, ds(x0, tiles), t * P:(t + 1) * P], x_lo[:, ds(x0, tiles), t * P:(t + 1) * P]
        free_set = s_mm.now()
        rounded = A(act.activation, hi, full, ACT.Copy, after=(turned, free_set))
        rest = V(dve.tensor_tensor, lo, full, hi.bitcast(F32), ALU.subtract, after=(rounded,))
        hold(b, rest)
        return rest

    def transpose_all(source, x0, *after):
        for t in range(NT):
            for k in range(0, KT, 4):
                last = transpose4(source[:, t, k * P:(k + 4) * P], x0 + k, t, *after)
        wait(pe, last)

    def row_of(w, n):
        return w.rearrange("(a n) -> a n", a=1).partition_broadcast(P) if len(w.shape) == 1 else w

    def inverse_root(to, sums, n, eps, *after):
        m = V(dve.tensor_scalar, to, sums, 1.0 / n, eps, ALU.mult, ALU.add, after=after)
        m = V(dve.reciprocal, to, to, after=(m,))
        return A(act.activation, to, to, ACT.Sqrt, after=(m,))

    def log1p_exp(to, x, e, u, *after):
        m = V(dve.scalar_tensor_tensor, e, x, -1.0, x, ALU.mult, ALU.max, after=after)
        m = A(act.activation, e, e, ACT.Exp, scale=-1.0, after=(m,))
        mu = V(dve.tensor_scalar, u, e, 1.0, None, ALU.add, after=(m,))
        ml = A(act.activation, to, u, ACT.Ln, after=(mu,))
        m = V(dve.scalar_tensor_tensor, e, u, -1.0, e, ALU.add, ALU.subtract, after=(mu,))
        m = V(dve.reciprocal, u, u, after=(m, ml))
        m = V(dve.tensor_tensor, e, e, u, ALU.mult, after=(m,))
        return V(dve.tensor_tensor, to, to, e, ALU.subtract, after=(m,))

    room = Room()
    xin = room(NT, D)
    loaded = load(ident[:, :], i["identity"])
    loaded = load(xin, rows(i["x"][0]))
    transpose_all(xin, 0, loaded)

    w_in = i["w_in"][0]

    def small(q):
        return w_in.rearrange("(k p) n -> p k n", p=P)[:, q * QK:(q + 1) * QK, ds(COL_DT, SSD_H)]

    block(small, 0, KT, SSD_H, to_dram(proj, COL_DT)(0))
    block(weight_at(w_in, COL_GK, GLA_R), 0, KT, GLA_R, to_dram(proj, COL_GK)(0))
    block(weight_at(w_in, COL_Z, BLK), 0, KT, BLK, to_dram(proj, COL_Z)(0))
    flat = lambda ap: ap.rearrange("p a b -> p (a b)")

    room = Room()
    TAB = 10
    tab = room(TAB, SSD_H)
    DT, AA, CS, EC, DW, DD = 0, 2, 4, 6, 8, 9
    tri = room(P)
    ones = room(P)
    t_a, t_b, t_c = room(NT, SSD_H), room(NT, SSD_H), room(NT, SSD_H)
    alog, bias = room(SSD_H), room(SSD_H)

    def ssd_shared():
        pr.meet()
        load(tri, i["causal"])
        load(t_a, rows(proj)[:, :, COL_DT:COL_DT + SSD_H], s_st[0].now(), s_st[1].now())
        load(bias, row_of(i["ssd_dt_bias"][0], SSD_H))
        load(alog, row_of(i["ssd_A_log"][0], SSD_H))
        loaded = load(tab[:, DD, :], row_of(i["ssd_D"][0], SSD_H))
        m_ones = G(pool.memset, ones, 1.0)
        yield
        for t in range(NT):
            m = V(dve.tensor_tensor, t_a[:, t, :], t_a[:, t, :], bias, ALU.add, after=(loaded,))
        m = log1p_exp(flat(tab[:, DT:DT + 2, :]), flat(t_a), flat(t_b), flat(t_c), m)
        m = V(dve.scalar_tensor_tensor, flat(tab[:, DT:DT + 2, :]), flat(t_a), 0.0, flat(tab[:, DT:DT + 2, :]),
              ALU.max, ALU.add, after=(m,))
        me = A(act.activation, alog, alog, ACT.Exp, after=(loaded,))
        for t in range(NT):
            m = V(dve.scalar_tensor_tensor, tab[:, AA + t, :], tab[:, DT + t, :], -1.0, alog, ALU.mult, ALU.mult,
                  after=(m, me))
        n2 = NT * SSD_H
        mt = T(pe.matmul, bank[4][:, 0:n2], tri, flat(tab[:, AA:AA + 2, :]), start=True, stop=True, after=(m,))
        m2 = T(pe.matmul, bank[5][:, 0:n2], ones, flat(tab[:, AA:AA + 2, :]), start=True, stop=True, after=(m_ones,))
        yield
        mc = V(dve.tensor_copy, flat(tab[:, CS:CS + 2, :]), bank[4][:, 0:n2], after=(mt, m2))
        A(act.activation, flat(tab[:, EC:EC + 2, :]), flat(tab[:, CS:CS + 2, :]), ACT.Exp, after=(mc,))
        m = V(dve.tensor_tensor, alog, bank[5][:, 0:SSD_H], tab[:, CS, :], ALU.subtract, after=(mc,))
        m = A(act.activation, alog, alog, ACT.Exp, after=(m,))
        V(dve.tensor_tensor, tab[:, DW, :], tab[:, DT, :], alog, ALU.mult, after=(m,))

    beside(ssd_shared())
    for j in (1, 2, 3):
        block(weight_at(w_in, COL_Z + j * BLK, BLK), 0, KT, BLK, to_dram(proj, COL_Z + j * BLK)(0))
    ended()
    segment(w_in, COL_Z + 4 * BLK, (COL_DT - COL_Z) // BLK - 4, 0, to_dram(proj, COL_Z + 4 * BLK))
    block(weight_at(w_in, COL_Q, BLK), 0, KT, BLK, to_dram(proj, COL_Q)(0))

    CH = SSD_HG * SSD_P
    pr.meet()
    wait(act, s_st[0].now(), s_st[1].now())
    gt = room(TAB, SSD_HG)
    xin = room(NT, CONV_T * P)
    z = room(NT, CH)
    cw = room(CONV_T, CONV_W + 1)
    nw = room(CH)
    ut = room(CONV_T, S + CONV_W - 1)
    cv = room(CONV_T, S)
    xt = room(NT, CH)
    xdt = room(NT, CH)
    xw = room(CH)
    yo = room(CH)
    btok = room(P)
    cbm = room(NT, P)
    dec = room(NT, SSD_HG, P)
    prev = room(CH)
    ysum = room(2, 1)
    HB = SSD_HG // 2
    by_head = lambda ap: ap.rearrange("p (h e) -> p h e", h=SSD_HG)
    V(dve.memset, ut[:, :, 0:CONV_W - 1], 0.0)
    DEC_BANK = {(0, 0): 7, (0, 1): 6, (1, 0): 5, (1, 1): 4}

    def ssd_group(g):
        pr.meet()
        pp = rows(proj)
        load(xin[:, :, 0:CH], pp[:, :, ds(g * CH + COL_XBC, CH)])
        load(xin[:, :, CH:CH + P], pp[:, :, ds(g * P + (COL_XBC + SSD_IN), P)])
        load(xin[:, :, CH + P:CH + 2 * P], pp[:, :, ds(g * P + (COL_XBC + SSD_IN + SSD_G * SSD_N), P)])
        m_in = load(flat(cw), i["conv"][ds(g, 1)].rearrange("a p n -> (a p) n"))
        load(z, pp[:, :, ds(g * CH + COL_Z, CH)], count=d_late)
        m_z = load(nw, row_of(i["ssd_norm_w"][0][ds(g * CH, CH)], CH), count=d_late)
        m_gt = V(dve.tensor_copy, gt, tab[:, :, ds(g * SSD_HG, SSD_HG)])
        m_cs = {}
        for (t, hb), b in DEC_BANK.items():
            for h in range(HB):
                m_cs[t, hb] = T(pe.matmul, bank[b][:, h * P:(h + 1) * P],
                                wide(gt[:, AA + t, hb * HB + h:hb * HB + h + 1], [P, P]), tri, start=True, stop=True,
                                after=(m_gt,))
        yield
        m_dec = {}
        for (t, hb), b in DEC_BANK.items():
            for h in range(HB):
                hh = hb * HB + h
                ms = V(dve.tensor_scalar, dec[:, t, hh, :], bank[b][:, h * P:(h + 1) * P],
                       gt[:, CS + t, hh:hh + 1], 0.0, ALU.subtract, ALU.min, after=(m_cs[t, hb],))
            some = dec[:, t, hb * HB:(hb + 1) * HB, :]
            m_dec[t, hb] = A(act.activation, some, some, ACT.Exp, after=(ms,))
        CB = (4, 5, 6)
        m_u = []
        for n in range(3):
            for c in (2 * n, 2 * n + 1):
                for t in range(NT):
                    m = T(pe.transpose, bank[CB[n]][:, (c % 2) * S + t * P:(c % 2) * S + (t + 1) * P],
                          xin[:, t, c * P:(c + 1) * P], ident[:, :], after=(m_in, ms))
            m_u.append(m)
        yield
        def conv(tiles):
            for w in range(1, CONV_W):
                for c in tiles:
                    m_cv[c] = V(dve.scalar_tensor_tensor, cv[:, c, :], ut[:, c, w:w + S], cw[:, c, w:w + 1],
                                cv[:, c, :], ALU.mult, ALU.add, after=(m_cv[c],))
            for c in tiles:
                m = A(act.activation, cv[:, c, :], cv[:, c, :], ACT.Silu, bias=cw[:, c, CONV_W:CONV_W + 1],
                      after=(m_cv[c],))
            return m

        m_cv = [None] * CONV_T
        for n in (2, 0, 1):
            mu = A(act.activation, ut[:, 2 * n:2 * n + 2, CONV_W - 1:],
                   bank[CB[n]][:, :].rearrange("p (a b) -> p a b", a=2), ACT.Copy, after=(m_u[n],))
            for c in (2 * n, 2 * n + 1):
                m_cv[c] = A(act.activation, cv[:, c, :], ut[:, c, 0:S], ACT.Copy, scale=cw[:, c, 0:1], after=(mu,))
            if n == 2:
                m_bc = conv((4, 5))
        for t in range(NT):
            tok = slice(t * P, t * P + P)
            T(pe.matmul, bank[4][:, tok], cv[:, 4, tok], cv[:, 5, tok], start=True, stop=True, after=(m_bc, mu))
        m_bt = T(pe.transpose, bank[4][:, S:S + P], cv[:, 4, 0:P], ident[:, :])
        yield
        m_s = conv((0, 1))
        for t in range(NT):
            m_cbm = V(dve.tensor_tensor, cbm[:, t, :], bank[4][:, t * P:(t + 1) * P], tri, ALU.mult, after=(m_bt,))
        m_bt = A(act.activation, btok, bank[4][:, S:S + P], ACT.Copy, after=(m_bt, m_cbm))
        for (t, hb), m in m_dec.items():
            some = dec[:, t, hb * HB:(hb + 1) * HB, :]
            m_dec[t, hb] = G(pool.tensor_tensor, some, some, wide(cbm[:, t, :].unsqueeze(1), [P, HB, P]), ALU.mult,
                             after=(m, m_cbm))
        yield
        m_s = conv((2, 3))
        for t in range(NT):
            m_sz = A(act.activation, z[:, t, :], z[:, t, :], ACT.Silu, after=(m_z,))
        for t in range(NT):
            for c in range(4):
                m_x = T(pe.transpose, bank[5 + t][:, c * P:(c + 1) * P], cv[:, c, t * P:(t + 1) * P], ident[:, :],
                        after=(m_s,))
        yield
        for t in range(NT):
            m_xt = A(act.activation, xt[:, t, :], bank[5 + t][:, :], ACT.Copy, after=(m_x,))
        for t in range(NT):
            m_xd = V(dve.tensor_tensor, by_head(xdt[:, t, :]), by_head(xt[:, t, :]),
                     wide(gt[:, DT + t, :].unsqueeze(2), [P, SSD_HG, SSD_P]), ALU.mult, after=(m_xt,))
        m_xw = V(dve.tensor_tensor, by_head(xw), by_head(xt[:, 0, :]),
                 wide(gt[:, DW, :].unsqueeze(2), [P, SSD_HG, SSD_P]), ALU.mult)
        m_st = T(pe.matmul, bank[4][:, :], btok, xw, start=True, stop=True, after=(m_bt, m_xw))
        m_y = []
        for t in range(NT):
            for h in range(SSD_HG):
                m = T(pe.matmul, bank[5 + t][:, h * SSD_P:(h + 1) * SSD_P], dec[:, t, h, :],
                      xdt[:, t, h * SSD_P:(h + 1) * SSD_P], start=True, stop=True, after=(m_dec[t, h // HB],))
            m_y.append(m)
        yield
        m_pv = A(act.activation, prev, bank[4][:, :], ACT.Copy, after=(m_st,))

        def skip(t):
            yt = xt[:, t, :]
            m = V(dve.tensor_tensor, by_head(yt), by_head(yt), wide(gt[:, DD, :].unsqueeze(2), [P, SSD_HG, SSD_P]),
                  ALU.mult, after=(m_xw,))
            return V(dve.tensor_tensor, yt, yt, bank[5 + t][:, :], ALU.add, after=(m, m_y[t]))

        def gated_squares(t, *after):
            yt = xt[:, t, :]
            m = V(dve.tensor_tensor, yt, yt, z[:, t, :], ALU.mult, after=(*after, m_sz))
            return V(dve.tensor_tensor_reduce, xdt[:, t, :], yt, yt, 1.0, 0.0, ALU.mult, ALU.add, ysum[:, t, :],
                     after=(m, m_y[1]))
        m_sq = gated_squares(0, skip(0))
        m_off = T(pe.matmul, bank[7][:, :], cv[:, 5, P:2 * P], prev, start=True, stop=True, after=(m_pv,))
        yield
        mx = skip(1)
        mo = V(dve.tensor_tensor, by_head(yo), by_head(bank[7][:, :]),
               wide(gt[:, EC + 1, :].unsqueeze(2), [P, SSD_HG, SSD_P]), ALU.mult, after=(m_off,))
        mx = V(dve.tensor_tensor, xt[:, 1, :], xt[:, 1, :], yo, ALU.add, after=(mx, mo))
        mx = gated_squares(1, mx)
        ms = inverse_root(flat(ysum), flat(ysum), CH, 1e-5, m_sq, mx)
        for t in range(NT):
            ms = V(dve.scalar_tensor_tensor, xt[:, t, :], xt[:, t, :], ysum[:, t, :], nw, ALU.mult, ALU.mult,
                   after=(ms, m_z))
        store(rows(heads_y)[:, :, ds(g * CH, CH)], xt, ms)

    def again(drain):
        at["drain"] = lambda h=(at["block"] - 1) % 2: drain(h, BLK)

    with pr.loop(SSD_G, apart=False) as g:
        again(to_dram(proj, COL_Q)(g))
        beside(ssd_group(g))
        block(weight_at(w_in, g * BLK + COL_GATE, BLK), 0, KT, BLK, to_dram(proj, COL_GATE)(g))
        block(weight_at(w_in, g * BLK + (COL_Q + BLK), BLK), 0, KT, BLK, to_dram(proj, COL_Q + BLK)(g))
        ended()
    again(to_dram(proj, COL_Q)(SSD_G))
    pr.meet()

    room = Room()
    halves = [room(NT, D), room(NT, D)]
    yloads = [load(halves[n], rows(heads_y)[:, :, n * D:(n + 1) * D], d_out.now()) for n in range(2)]

    def turned(source, x0, *after):
        for t in range(NT):
            for k in range(0, KT, 4):
                transpose4(source[:, t, k * P:(k + 4) * P], x0 + k, t, *after)
                yield

    beside(turned(halves[1], KT, *yloads))
    for j in range(SSD_G + 1, (COL_GK - COL_Q) // BLK):
        block(weight_at(w_in, COL_Q + j * BLK, BLK), 0, KT, BLK, to_dram(proj, COL_Q + j * BLK)(0))
    ended()
    drained()
    wait(act, s_st[0].now(), s_st[1].now())
    for _ in turned(halves[0], 0, *yloads):
        pass
    wait(pe, pr.dve.now())

    pr.meet()
    room = Room()
    low = room(NT, GLA_R)
    lowt = room(S)
    tri64, sum64, last64 = room(P), room(P), room(2)
    most, least = room(GLA_C), room(GLA_C)
    gnw = room(GLA_V)
    load(low, rows(proj)[:, :, COL_GK:COL_GK + GLA_R])
    load(tri64, i["causal64"])
    load(most, i["most64"])
    load(least, i["least64"])
    load(sum64, i["blocks64"])
    load(last64, i["columns64"])
    loaded = load(gnw, row_of(i["gla_norm_w"][0], GLA_V))
    m1 = V(dve.memset, lowt[0:GLA_R + 1, :], 1.0)
    for t in range(NT):
        m = T(pe.transpose, bank[4][0:GLA_R, t * P:(t + 1) * P], low[:, t, :], ident[:, :], after=(loaded,))
    V(dve.tensor_copy, lowt[0:GLA_R, :], bank[4][0:GLA_R, 0:S], after=(m, m1))
    q, k, v, gg = room(NT, GLA_K), room(NT, GLA_K), room(NT, GLA_V), room(NT, GLA_V)
    gkw = room(GLA_K)
    gk, e1, e2, e3 = room(NT, GLA_K), room(NT, GLA_K), room(NT, GLA_K), room(NT, GLA_K)
    qt, kt = room(2, S), room(2, S)
    dk = room(2, NT * 2)
    state = [room(2, GLA_V), room(2, GLA_V)]
    att = room(NT, P)
    osum = room(2, 1)
    o = room(NT, GLA_V)
    gate, grow = room(NT, BLK), room(BLK)
    V(dve.memset, att, 0.0)
    tok_of = lambda c: slice(c * GLA_C, (c + 1) * GLA_C)
    part_of = lambda c: slice((c % 2) * GLA_C, (c % 2 + 1) * GLA_C)

    def gla_head(h):
        pr.meet()
        pp = rows(proj)
        load(gkw[0:GLA_R, :], i["gla_gk_w"][0][:, ds(h * GLA_K, GLA_K)])
        load(gkw[GLA_R:GLA_R + 1, :], i["gla_gk_b"][:, ds(h * GLA_K, GLA_K)])
        load(q, pp[:, :, ds(h * GLA_K + COL_Q, GLA_K)])
        load(k, pp[:, :, ds(h * GLA_K + COL_K, GLA_K)])
        m_in = load(v, pp[:, :, ds(h * GLA_V + COL_V, GLA_V)])
        m_g = load(gg, pp[:, :, ds(h * GLA_V + COL_G, GLA_V)], count=d_late)
        yield
        for t in range(NT):
            m = T(pe.matmul, bank[4][:, t * GLA_K:(t + 1) * GLA_K], lowt[0:GLA_R + 1, t * P:(t + 1) * P],
                  gkw[0:GLA_R + 1, :], start=True, stop=True, after=(m_in,))
        yield
        m = V(dve.tensor_copy, flat(e1), bank[4][:, :], after=(m,))
        m = log1p_exp(flat(gk), flat(e1), flat(e2), flat(e3), m)
        m = V(dve.scalar_tensor_tensor, flat(gk), flat(e1), 0.0, flat(gk), ALU.min, ALU.subtract, after=(m,))
        m_gk = V(dve.tensor_scalar, flat(gk), flat(gk), 1.0 / 16.0, None, ALU.mult, after=(m,))
        T(pe.matmul, bank[5][:, :], tri64, flat(gk), start=True, stop=True, after=(m_gk,))
        T(pe.matmul, bank[6][:, :], sum64, flat(gk), start=True, stop=True)
        for kk in range(2):
            for t in range(NT):
                m = T(pe.matmul, bank[7][:, kk * 4 + 2 * t:kk * 4 + 2 * t + 2], gk[:, t, kk * P:(kk + 1) * P],
                      last64, start=True, stop=True)
        yield
        m_e1 = A(act.activation, flat(e1), bank[5][:, :], ACT.Copy, after=(m,))
        m_e2 = A(act.activation, flat(e2), bank[5][:, :], ACT.Exp)
        m_e3 = A(act.activation, flat(e3), bank[5][:, :], ACT.Exp, scale=-1.0)
        m_dk = A(act.activation, flat(dk), bank[7][:, 0:8], ACT.Exp)
        m = V(dve.tensor_tensor, flat(e1), bank[6][:, :], flat(e1), ALU.subtract, after=(m_e1,))
        m_e1 = A(act.activation, flat(e1), flat(e1), ACT.Exp, after=(m,))
        m_q = V(dve.scalar_tensor_tensor, flat(e2), flat(q), GLA_K ** -0.5, flat(e2), ALU.mult, ALU.mult,
                after=(m_e2, m_in))
        m_k = V(dve.tensor_tensor, flat(e3), flat(k), flat(e3), ALU.mult, after=(m_e3,))
        m_kd = V(dve.tensor_tensor, flat(e1), flat(k), flat(e1), ALU.mult, after=(m_e1,))
        m_t = []
        for src, b, ms in ((e2, 4, m_q), (e3, 7, m_k)):
            for kk in range(2):
                for t in range(NT):
                    m = T(pe.transpose, bank[b][:, kk * S + t * P:kk * S + (t + 1) * P],
                          src[:, t, kk * P:(kk + 1) * P], ident[:, :], after=(ms, m_dk))
            m_t.append(m)
        yield
        m_qt = A(act.activation, flat(qt), bank[4][:, :], ACT.Copy, after=(m_t[0],))
        m_kt = A(act.activation, flat(kt), bank[7][:, :], ACT.Copy, after=(m_t[1],))
        for c in range(2 * NT):
            t = c // 2
            for kk in range(2):
                m_a = T(pe.matmul, bank[5][part_of(c), t * GLA_C:(t + 1) * GLA_C], kt[:, kk, tok_of(c)],
                        qt[:, kk, tok_of(c)], start=(kk == 0), stop=(kk == 1), after=(m_kt, m_e1))

        def update(c, *after):
            for kk in range(2):
                m = T(pe.matmul, bank[6 + kk][:, :], e1[part_of(c), c // 2, kk * P:(kk + 1) * P],
                      v[part_of(c), c // 2, :], start=True, stop=True, after=after)
            return m

        def advance(c, m):
            now, nxt = state[c % 2], state[(c + 1) % 2]
            for kk in range(2):
                if c:
                    ms = V(dve.scalar_tensor_tensor, nxt[:, kk, :], now[:, kk, :], dk[:, kk, c:c + 1],
                           bank[6 + kk][:, :], ALU.mult, ALU.add, after=(m, m_state[c - 1]))
                else:
                    ms = V(dve.tensor_copy, nxt[:, kk, :], bank[6 + kk][:, :], after=(m,))
            m_state.append(ms)

        def carried(c):
            for kk in range(2):
                m = T(pe.matmul, bank[4 + c // 2][part_of(c), :], qt[:, kk, tok_of(c)], state[c % 2][:, kk, :],
                      start=False, stop=True, skip_group_check=True, after=(m_state[c - 1],))
            return m
        m_state = []
        m_up = update(0, m_kd, m_kt)
        yield
        for half in range(2):
            part = part_of(half)
            inner = att[part, :, part]
            ma = V(dve.tensor_tensor, inner, bank[5][part, 0:NT * GLA_C].rearrange("p (t n) -> p t n", t=NT),
                   wide(most[part, :].unsqueeze(1), [GLA_C, NT, GLA_C]), ALU.min, after=(m_a,))
            m_att = V(dve.tensor_tensor, inner, inner, wide(least[part, :].unsqueeze(1), [GLA_C, NT, GLA_C]),
                      ALU.max, after=(ma,))
        advance(0, m_up)
        for t in range(NT):
            T(pe.matmul, bank[4 + t][:, :], att[:, t, :], v[:, t, :], start=True, stop=True, after=(m_att, m_qt))
        m_o = [carried(1)]
        m_up = update(1, m_state[0])
        yield
        advance(1, m_up)
        for t in range(NT):
            m_sg = A(act.activation, gg[:, t, :], gg[:, t, :], ACT.Silu, after=(m_g,))
        carried(2)
        m_up = update(2, m_state[1])
        yield
        advance(2, m_up)
        m_o.append(carried(3))
        for t in range(NT):
            mo = A(act.activation, o[:, t, :], bank[4 + t][:, :], ACT.Copy, after=(m_o[t],))
            ms = V(dve.tensor_tensor_reduce, e2.rearrange("p t n -> p (t n)"), o[:, t, :], o[:, t, :], 1.0, 0.0,
                   ALU.mult, ALU.add, osum[:, t, :], after=(mo, m_t[1], pr.dve.now()))
        ms = inverse_root(flat(osum), flat(osum), GLA_V, 1e-5, ms)
        for t in range(NT):
            m = V(dve.scalar_tensor_tensor, o[:, t, :], o[:, t, :], osum[:, t, :], gnw, ALU.mult, ALU.mult,
                  after=(ms,))
            m = V(dve.tensor_tensor, o[:, t, :], o[:, t, :], gg[:, t, :], ALU.mult, after=(m, m_sg))
        store(rows(heads_o)[:, :, ds(h * GLA_V, GLA_V)], o, m)

    def gate_of(j, which, *after):
        load(gate, rows(proj)[:, :, ds(j * BLK + (COL_GATE + which * D), BLK)], *after, count=d_gate)
        return load(grow, row_of(i["gate_bias"][0, which][ds(j * BLK, BLK)], BLK), count=d_gate)

    def sigmoid_gate(loaded):
        for t in range(NT):
            m = V(dve.tensor_tensor, gate[:, t, :], gate[:, t, :], grow, ALU.add, after=(loaded,))
            m = A(act.activation, gate[:, t, :], gate[:, t, :], ACT.Sigmoid, after=(m,))
        return m

    def ssd_branch_drain(j):
        def drain(half, n):
            m = sigmoid_gate(d_gate.now())
            wait(dve, summed(), s_st[half].now(), m)
            for t in range(NT):
                last = dve.tensor_tensor(stage[:, half, t, 0:n], bank[2 * half + t][:, 0:n], gate[:, t, 0:n],
                                         ALU.mult)
            s_drv.up(last)
            full = s_drv.now()

            def save():
                wait(act, full)
                s_st[half].up(act.dma_start(rows(gated)[:, :, ds(j * BLK, n)], stage[:, half, :, 0:n]))
            return save
        return drain

    w_branch = i["w_ssd_branch"][0]
    with pr.loop(GLA_H, apart=False) as h:
        gate_of(h, 0, s_drv.now())
        beside(gla_head(h))
        block(weight_at(w_branch, h * BLK, BLK), 0, 2 * KT, BLK, ssd_branch_drain(h))
        ended()
        drained()
    pr.meet()
    wait(act, s_st[0].now(), s_st[1].now(), s_drv.now())

    room = Room()
    ov = room(NT, D)
    merged = room(2, NT, BLK)
    other = room(NT, BLK)
    gate, grow = room(NT, BLK), room(BLK)
    loaded = load(ov, rows(heads_o), d_out.now())
    transpose_all(ov, 0, loaded)

    def gla_branch_drain(j):
        def drain(half, n):
            free(dve, ("merged", half))
            m = sigmoid_gate(d_gate.now())
            wait(dve, summed(), m)
            for t in range(NT):
                last = dve.tensor_tensor(merged[:, half, t, :], bank[2 * half + t][:, 0:n], gate[:, t, :], ALU.mult)
            s_drv.up(last)
            for t in range(NT):
                m = V(dve.tensor_tensor, merged[:, half, t, :], merged[:, half, t, :], other[:, t, :], ALU.add,
                      after=(s_drv.now(),))
            for t in range(NT):
                transpose4(merged[:, half, t, :], KT + 4 * j, t, m)
            hold(("merged", half), pr.pe.now())
        return drain

    for j in range(D // BLK):
        load(other, rows(gated)[:, :, j * BLK:(j + 1) * BLK], pr.dve.now(), count=d_gate)
        gate_of(j, 1)
        block(weight_at(i["w_gla_branch"][0], j * BLK, BLK), 0, KT, BLK, gla_branch_drain(j))
        drained()
    wait(pe, pr.dve.now())

    room = Room()
    total = room(NT, D)
    wait(dve, pr.pe.now(), pr.act.now())
    segment(i["w_out"][0], 0, D // BLK, KT, to_sum(total, False))
    drained()

    def residual_norm(source, g_row, b_row, dest, *after):
        big = room_n(NT, D)
        grow, brow, mean, var = room_n(D), room_n(D), room_n(2, 1), room_n(2, 1)
        load(big, source, *after)
        load(grow, row_of(g_row, D))
        loaded = load(brow, row_of(b_row, D))
        for t in range(NT):
            m = V(dve.scalar_tensor_tensor, total[:, t, :], big[:, t, :], ALPHA, total[:, t, :], ALU.mult, ALU.add,
                  after=(loaded, s_drv.now()))
            m = V(dve.tensor_reduce, mean[:, t, :], total[:, t, :], AX, ALU.add, after=(m,))
            m = V(dve.tensor_scalar, mean[:, t, :], mean[:, t, :], 1.0 / D, None, ALU.mult, after=(m,))
            m = V(dve.tensor_scalar, total[:, t, :], total[:, t, :], mean[:, t, :], None, ALU.subtract, after=(m,))
            ma = A(act.activation, big[:, t, :], total[:, t, :], ACT.Square, accum_out=var[:, t, :], after=(m,))
            m = inverse_root(var[:, t, :], var[:, t, :], D, 1e-5, ma)
            m = V(dve.scalar_tensor_tensor, total[:, t, :], total[:, t, :], var[:, t, :], grow, ALU.mult, ALU.mult,
                  after=(m,))
            m = V(dve.tensor_tensor, total[:, t, :], total[:, t, :], brow, ALU.add, after=(m,))
        return m, store(rows(dest), total, m)

    room_n = Room(room.at)
    m, stored = residual_norm(rows(i["x"][0]), i["ln1_g"][0], i["ln1_b"][0], residual, pr.dve.now())
    transpose_all(total, 0, m)
    wait(dve, pr.pe.now(), stored)

    hid = Room(NT * D)(2, NT, BLK)
    m0 = V(dve.memset, total, 0.0)
    wait(dve, m0)
    with pr.loop(FF // D) as f:
        total_marks.clear()
        wait(dve, s_drv.now())

        def to_hidden(j):
            def drain(half, n):
                free(dve, ("hid", half))
                wait(dve, summed())
                for t in range(NT):
                    b = bank[2 * half + t][:, 0:n]
                    m1 = V(dve.tensor_scalar, hid[:, half, t, :], b, 0.0, None, ALU.max)
                    wait(dve, m1)
                    last = dve.tensor_tensor(hid[:, half, t, :], hid[:, half, t, :], b, ALU.mult)
                full = s_drv.up(last)
                for t in range(NT):
                    m = transpose4(hid[:, half, t, :], KT + 4 * j, t, full)
                hold(("hid", half), pr.pe.now())
            return drain
        for j in range(D // BLK):
            block(weight_at(i["w_up"][0], f * D + j * BLK, BLK), 0, KT, BLK, to_hidden(j))
        drained()

        def down(q, j):
            w = i["w_down"][0].rearrange("(f k p) n -> f p k n", p=P, k=KT)
            return w[ds(f_sp, 1), :, q * QK:(q + 1) * QK, j * BLK:(j + 1) * BLK].rearrange("a p k n -> (a p) k n")
        wait(pe, pr.dve.now())
        for j in range(D // BLK):
            f_sp = sp.snap(f)
            block(lambda q, j=j: down(q, j), KT, KT, BLK, to_sum(total, True)(j))
        drained()
        m_down = s_drv.now()
    room_n = Room(NT * D)
    m, stored = residual_norm(rows(residual), i["ln2_g"][0], i["ln2_b"][0], residual, m_down, stored)

    if debug and "stop1" in debug:
        return finish(pr, out, total, m)

    pr.meet()
    wait(act, stored)
    with pr.loop(LAYERS) as l:
        aligned()
        def row2(w, n):
            return w.rearrange("(a l) n -> a (l n)", a=1)[:, ds(l * n, n)].partition_broadcast(P)

        def weight2(w, row_tiles, col, n):
            w = w.rearrange("l (k p) n -> p (l k) n", p=P)
            kts = min(QK, row_tiles)

            def get(q):
                first = sp.snap(l * row_tiles + q * kts)
                c = col if isinstance(col, int) else sp.snap(col)
                return w[:, ds(first, kts), ds(c, n)]
            return get

        def segment2(w, blocks, drain):
            def one(j):
                block(weight2(w, KT, j * BLK, BLK), 0, KT, BLK, drain(j))
            for j in range(blocks):
                one(j)

        room = Room()
        xr, hn, grow, ssq = room(NT, D), room(NT, D), room(D), room(2, 1)
        load(xr, rows(residual))
        loaded = load(grow, row2(i["norm_pre_2"], D))
        for t in range(NT):
            m = A(act.activation, hn[:, t, :], xr[:, t, :], ACT.Square, accum_out=ssq[:, t, :], after=(loaded,))
            m = inverse_root(ssq[:, t, :], ssq[:, t, :], D, 1e-6, m)
            m = V(dve.scalar_tensor_tensor, hn[:, t, :], xr[:, t, :], ssq[:, t, :], grow, ALU.mult, ALU.mult,
                  after=(m,))
        transpose_all(hn, 0, m)
        segment2(i["w_in_2"], N_IN2 // BLK, to_dram(proj2, 0))
        rest = N_IN2 % BLK
        block(weight2(i["w_in_2"], KT, N_IN2 - rest, rest), 0, KT, rest, to_dram(proj2, N_IN2 - rest)(0))
        drained()

        pr.meet()
        room = Room()
        DR = 2 * ROWS - 1
        DC = 2 * WIN_C - 1
        osum = room(NT, D)
        edge = room(P)
        m = V(dve.memset, edge, 0.0)
        rpb = i["c_rpb_2"].rearrange("l h a b -> (l h) a b")
        for hh in range(C_H):
            loaded = load(edge[hh * DR:(hh + 1) * DR, GRID - WIN_C:GRID - WIN_C + DC],
                          rpb[ds(l * C_H + hh, 1), WIN_R - ROWS:WIN_R - ROWS + DR, :].rearrange("a r c -> (a r) c"), m)
        skewed = store(skew, wide(edge[0:C_H * DR, :].unsqueeze(1), [C_H * DR, GRID, P]), loaded)

        cq, ckv = room(NT, B_QL), room(NT, B_KVL)
        gq, gkv, sq = room(B_QL), room(B_KVL), room(4, 1)
        junk = room(B_QL)
        wait(act, s_st[0].now(), s_st[1].now())
        load(cq, rows(proj2)[:, :, C2_CQ:C2_CQ + B_QL])
        load(ckv, rows(proj2)[:, :, C2_CKV:C2_CKV + B_KVL])
        load(gq, row2(i["b_q_norm_2"], B_QL))
        loaded = load(gkv, row2(i["b_kv_norm_2"], B_KVL))
        ma = None
        for n, (x, g, w, tiles) in enumerate(((cq, gq, B_QL, 4), (ckv, gkv, B_KVL, 2))):
            for t in range(NT):
                s = sq[:, 2 * n + t, :]
                ma = A(act.activation, junk[:, 0:w], x[:, t, :], ACT.Square, accum_out=s, after=(loaded, ma))
                m = inverse_root(s, s, w, 1e-6, ma)
                m = V(dve.scalar_tensor_tensor, x[:, t, :], x[:, t, :], s, g, ALU.mult, ALU.mult, after=(m,))
                m = transpose4(x[:, t, :], KT + 4 * n, t, m, tiles=tiles)
        wait(pe, m)
        for col, n in ((0, BLK), (BLK, B_H * (HD + B_ROPE) - BLK)):
            block(weight2(i["b_w_uq_2"], B_QL // P, col, n), KT, B_QL // P, n, to_dram(latent, col)(0))
        for col in (0, BLK):
            block(weight2(i["b_w_ukv_2"], B_KVL // P, col, BLK), KT + 4, B_KVL // P, BLK,
                  to_dram(latent, 2 * BLK + col)(0))
        drained()
        wait(act, s_st[0].now(), s_st[1].now())

        UW = UNIT_H * HD
        pr.meet()
        room = Room(NT * D)
        small = room(6, 8)
        work_at = room.at

        def rope(x, heads, n, cos, sin, tmp, *after):
            q4 = n // 4
            split = lambda a: a.rearrange("p h (b s e) -> p h b s e", b=2, s=2)
            xs, ts = split(x), split(tmp)
            ss = sin.rearrange("p (b s e) -> p b s e", b=2, s=2)
            for s in range(2):
                for hh in range(heads):
                    m = V(dve.tensor_tensor, ts[:, hh, :, s, :], xs[:, hh, :, 1 - s, :], ss[:, :, s, :], ALU.mult,
                          after=after)
            m2 = V(dve.tensor_tensor, x, x, wide(cos.unsqueeze(1), [P, heads, n]), ALU.mult, after=(m,))
            return V(dve.tensor_tensor, x, x, tmp, ALU.add, after=(m2,))

        def head_norm(x, n, g, stat, tmp, *after):
            m = V(dve.tensor_tensor, tmp, x, x, ALU.mult, after=after)
            m = V(dve.tensor_reduce, stat, tmp, AX, ALU.add, after=(m,))
            m = inverse_root(stat, stat, HD, 1e-6, m)
            m = V(dve.tensor_tensor, x, x, wide(stat.unsqueeze(2), [P, n, HD]), ALU.mult, after=(m,))
            return V(dve.tensor_tensor, x, x, wide(g.unsqueeze(1), [P, n, HD]), ALU.mult, after=(m,))

        def turn_heads(to, source, banks, width, *after):
            heads = to.shape[1]
            for hh in range(heads):
                b = bank[banks[hh // 2 % len(banks)]]
                for t in range(NT):
                    m = T(pe.transpose, b[0:width, (hh % 2) * S + t * P:(hh % 2) * S + (t + 1) * P],
                          source(hh, t), ident[:, :], after=after)
                if hh % 2 or hh == heads - 1:
                    n = hh % 2 + 1
                    m = A(act.activation, to[0:width, hh - n + 1:hh + 1, :],
                          b[0:width, 0:n * S].rearrange("p (h n) -> p h n", h=n), ACT.Copy, after=(m,))
            return m

        def attend(parts, value, probs, pt, scale, bias, out_col, gate, m_gate, *after):
            m_p = []
            for t in range(NT):
                tok = slice(t * P, (t + 1) * P)
                for hh in range(UNIT_H):
                    o_ = bank[2 * t + hh // 2][:, (hh % 2) * S:(hh % 2 + 1) * S]
                    for n, (qf, kf) in enumerate(parts):
                        m = T(pe.matmul, o_, qf(hh)[:, tok], kf(hh), start=(n == 0), stop=(n == len(parts) - 1),
                              after=after)
                pb = probs[t]
                top, tot = small[:, t, 0:4], small[:, 2 + t, 0:4]
                mm = []
                for n in range(2):
                    sc = bank[2 * t + n][:, :].rearrange("p (h n) -> p h n", h=2)
                    if bias is not None:
                        ms = V(dve.scalar_tensor_tensor, pb[:, 2 * n:2 * n + 2, :], sc, scale,
                               bias[:, t, 2 * n:2 * n + 2, :], ALU.mult, ALU.add, after=(m,))
                        ms = V(dve.tensor_reduce, top[:, 2 * n:2 * n + 2], pb[:, 2 * n:2 * n + 2, :], AX, ALU.max,
                               after=(ms,))
                    else:
                        ms = V(dve.tensor_reduce, top[:, 2 * n:2 * n + 2], sc, AX, ALU.max, after=(m,))
                sf = 1.0 if bias is not None else scale
                ms = V(dve.tensor_scalar, top, top, -sf, None, ALU.mult, after=(ms,))
                for hh in range(UNIT_H):
                    src = pb[:, hh, :] if bias is not None else bank[2 * t + hh // 2][:, (hh % 2) * S:(hh % 2 + 1) * S]
                    me = A(act.activation, pb[:, hh, :], src, ACT.Exp, bias=top[:, hh:hh + 1], scale=sf,
                           accum_out=tot[:, hh:hh + 1], after=(ms,))
                V(dve.reciprocal, tot, tot, after=(me,))
                m_p.append(me)
            m_v = None
            for t in range(NT):
                for hh in range(UNIT_H):
                    b = bank[4 + hh // 2]
                    for kt in range(NT):
                        m = T(pe.transpose, b[:, ((hh % 2) * NT + kt) * P:((hh % 2) * NT + kt + 1) * P],
                              probs[t][:, hh, kt * P:(kt + 1) * P], ident[:, :], after=(m_p[t],))
                    if hh % 2:
                        m = A(act.activation, pt[:, hh - 1:hh + 1, :], b[:, :].rearrange("p (h n) -> p h n", h=2),
                              ACT.Copy, after=(m, m_v))
                o_ = bank[6 + t]
                for hh in range(UNIT_H):
                    for kt in range(NT):
                        m_v = T(pe.matmul, o_[:, hh * HD:(hh + 1) * HD], pt[:, hh, kt * P:(kt + 1) * P],
                                value(hh, kt), start=(kt == 0), stop=(kt == NT - 1), after=(m,))
                to = osum[:, t, out_col:out_col + UW]
                m = V(dve.tensor_tensor, to.rearrange("p (h n) -> p h n", h=UNIT_H),
                      o_[:, :].rearrange("p (h n) -> p h n", h=UNIT_H),
                      wide(small[:, 2 + t, 0:4].unsqueeze(2), [P, UNIT_H, HD]), ALU.mult, after=(m_v, pr.dve.now()))
                ms = A(act.activation, gate[:, t, :], gate[:, t, :], ACT.Silu, after=(m_gate,))
                V(dve.tensor_tensor, to, to, gate[:, t, :], ALU.mult, after=(m, ms))

        heads_of = lambda a: a.rearrange("p t (h n) -> p (t h) n", n=HD)
        p2 = rows(proj2)
        for unit in range(A_KV):
            pr.meet()
            room = Room(work_at)
            q, k, v, gt2 = room(NT, UW), room(NT, HD), room(NT, HD), room(NT, UW)
            qt, kt_, pt = room(UNIT_H, S), room(1, S), room(UNIT_H, S)
            tmp, tmp2 = room(NT, UW), room(NT, UW)
            gq, gk2, cos, sin = room(HD), room(HD), room(NT, HD), room(NT, HD)
            load(q, p2[:, :, C2_AQ + unit * UW:C2_AQ + (unit + 1) * UW])
            load(k, p2[:, :, C2_AK + unit * HD:C2_AK + (unit + 1) * HD])
            load(v, p2[:, :, C2_AV + unit * HD:C2_AV + (unit + 1) * HD])
            load(gq, row2(i["a_q_norm_2"], HD))
            load(gk2, row2(i["a_k_norm_2"], HD))
            load(cos, rows(i["cos128"]))
            m_in = load(sin, rows(i["sin128"]))
            m_gate = load(gt2, p2[:, :, C2_AG + unit * UW:C2_AG + (unit + 1) * UW], count=d_late)
            mq = head_norm(heads_of(q), NT * UNIT_H, gq, small[:, 4, :], heads_of(tmp), m_in)
            mk = head_norm(k, NT, gk2, small[:, 5, 0:2], tmp2[:, :, 0:HD], m_in)
            for t in range(NT):
                mq = rope(q[:, t, :].rearrange("p (h n) -> p h n", n=HD), UNIT_H, HD, cos[:, t, :], sin[:, t, :],
                          tmp[:, t, :].rearrange("p (h n) -> p h n", n=HD), mq)
                mk = rope(k[:, t:t + 1, :], 1, HD, cos[:, t, :], sin[:, t, :], tmp2[:, t:t + 1, 0:HD], mk)
            m1 = turn_heads(qt, lambda h, t: q[:, t, h * HD:(h + 1) * HD], (4, 5), HD, mq)
            m2 = turn_heads(kt_, lambda h, t: k[:, t, :], (6,), HD, mk)
            attend([(lambda h: qt[:, h, :], lambda h: kt_[:, 0, :])], lambda h, kt: v[:, kt, :],
                   [a.rearrange("p t n -> p (t n)").rearrange("p (h n) -> p h n", h=UNIT_H) for a in (tmp, tmp2)],
                   pt, HD ** -0.5, None, unit * UW, gt2, m_gate, m1, m2)

        pr.meet()
        room = Room(work_at)
        QW = HD + B_ROPE
        q, kv, kr = room(NT, B_H * QW), room(NT, B_H * 2 * HD), room(NT, B_ROPE)
        cos, sin = room(NT, B_ROPE), room(NT, B_ROPE)
        qt, kt_, pt = room(B_H, S), room(B_H, S), room(UNIT_H, S)
        qpe, kpe = room(B_H, S), room(1, S)
        tmp = room(B_H, B_ROPE)
        gt2 = room(NT, UW)
        lat = rows(latent)
        load(q, lat[:, :, 0:B_H * QW])
        load(kv, lat[:, :, 2 * BLK:4 * BLK])
        load(kr, p2[:, :, C2_KR:C2_KR + B_ROPE])
        load(cos, rows(i["cos64"]))
        m_in = load(sin, rows(i["sin64"]))
        m_gate = load(gt2, p2[:, :, C2_BG:C2_BG + UW], count=d_late)
        m = m_in
        for t in range(NT):
            m = rope(q[:, t, :].rearrange("p (h n) -> p h n", n=QW)[:, :, HD:QW], B_H, B_ROPE, cos[:, t, :],
                     sin[:, t, :], tmp, m)
            m = rope(kr[:, t:t + 1, :], 1, B_ROPE, cos[:, t, :], sin[:, t, :], tmp[:, 0:1, :], m)
        turn_heads(qt, lambda h, t: q[:, t, h * QW:h * QW + HD], (0, 1), HD, m)
        turn_heads(kt_, lambda h, t: kv[:, t, h * 2 * HD:h * 2 * HD + HD], (2, 3), HD, m)
        turn_heads(qpe, lambda h, t: q[:, t, h * QW + HD:(h + 1) * QW], (4, 5), B_ROPE, m)
        m = turn_heads(kpe, lambda h, t: kr[:, t, :], (6,), B_ROPE, m)
        flat_q = q.rearrange("p t n -> p (t n)")
        attend([(lambda h: qt[:, h, :], lambda h: kt_[:, h, :]),
                (lambda h: qpe[0:B_ROPE, h, :], lambda h: kpe[0:B_ROPE, 0, :])],
               lambda h, kt: kv[:, kt, h * 2 * HD + HD:(h + 1) * 2 * HD],
               [probs_b(stage, t) for t in range(NT)], pt, QW ** -0.5, None, A_H * HD, gt2, m_gate, m)

        pr.meet()
        room = Room(work_at)
        q, k, v, gt2 = room(NT, UW), room(NT, UW), room(NT, UW), room(NT, UW)
        qt, kt_, pt = room(C_H, S), room(C_H, S), room(UNIT_H, S)
        bias, mask = room(NT, C_H * S), room(NT, S)
        for to, c in ((q, C2_Q), (k, C2_K), (v, C2_V)):
            load(to, p2[:, :, c:c + UW])
        wait(act, skewed)
        load(mask, rows(i["window"]))
        for r in range(ROWS):
            part = slice((r % 2) * GRID, (r % 2 + 1) * GRID)
            for hh in range(C_H):
                m_in = load(bias[part, r // 2, hh * S:(hh + 1) * S].rearrange("p (a b) -> p a b", a=ROWS),
                            bass.AP(skew.tensor, (hh * DR + ROWS - 1 - r) * GRID * P + GRID - 1,
                                    [[P - 1, GRID], [GRID * P, ROWS], [1, GRID]]))
        m_gate = load(gt2, p2[:, :, C2_G:C2_G + UW], count=d_late)
        for t in range(NT):
            bt = bias[:, t, :].rearrange("p (h n) -> p h n", h=C_H)
            mb = V(dve.tensor_tensor, bt, bt, wide(mask[:, t, :].unsqueeze(1), [P, C_H, S]), ALU.add, after=(m_in,))
        turn_heads(qt, lambda h, t: q[:, t, h * HD:(h + 1) * HD], (0, 1), HD, m_in)
        m = turn_heads(kt_, lambda h, t: k[:, t, h * HD:(h + 1) * HD], (2, 3), HD, m_in)
        attend([(lambda h: qt[:, h, :], lambda h: kt_[:, h, :])], lambda h, kt: v[:, kt, h * HD:(h + 1) * HD],
               [a.rearrange("p t n -> p (t n)").rearrange("p (h n) -> p h n", h=UNIT_H) for a in (q, k)],
               pt, HD ** -0.5, bias.rearrange("p t (h n) -> p t h n", h=C_H), (A_H + B_H) * HD, gt2, m_gate, m, mb)

        pr.meet()
        transpose_all(osum, 0, pr.dve.now())
        total = osum
        total_marks.clear()
        wait(dve, pr.pe.now())
        segment2(i["w_out_2"], D // BLK, to_sum(total, False))
        drained()
        room = Room(NT * D)
        xr, grow, junk2, sq2 = room(NT, D), room(D), room(D), room(2, 1)
        load(xr, rows(residual), pr.pe.now(), pr.dve.now())
        loaded = load(grow, row2(i["norm_post_2"], D))
        wait(act, s_drv.now(), pr.dve.now())
        ma = None
        for t in range(NT):
            ma = A(act.activation, junk2, total[:, t, :], ACT.Square, accum_out=sq2[:, t, :], after=(ma,))
            m = inverse_root(sq2[:, t, :], sq2[:, t, :], D, 1e-6, ma)
            m = V(dve.scalar_tensor_tensor, total[:, t, :], total[:, t, :], sq2[:, t, :], grow, ALU.mult, ALU.mult,
                  after=(m, loaded))
            m = V(dve.tensor_tensor, total[:, t, :], total[:, t, :], xr[:, t, :], ALU.add, after=(m,))
        stored = store(rows(residual), total, m)
        wait(act, stored)

    return finish(pr, out, total, pr.dve.now())


def probs_b(stage, t):
    return stage[:, t, :, :].rearrange("p a n -> p (a n)").rearrange("p (h n) -> p h n", h=UNIT_H)


def finish(pr, out, value, *after):
    act = pr.nc.scalar
    pr.wait(act, *after)
    d_out = pr.counts["d_out"]
    d_out.up(act.dma_start(out[0].rearrange("(t p) n -> p t n", p=P), value))
    pr.wait(act, d_out.now(), pr.counts["s_st0"].now(), pr.counts["s_st1"].now())
    return pr.found


def constants():
    j, t = np.arange(P)[:, None], np.arange(P)[None, :]
    same = (j // GLA_C) == (t // GLA_C)
    most = np.where((j % GLA_C) <= np.arange(GLA_C)[None, :], np.finfo(np.float32).max, 0.0)
    c = {"most64": most, "least64": -most, "identity": j == t, "causal": j <= t, "causal64": (j <= t) & same, "blocks64": same,
         "columns64": (np.arange(P)[:, None] // GLA_C) == np.arange(2)[None, :]}
    tok = np.arange(S)
    for n, name in ((HD, "128"), (B_ROPE, "64")):
        half = n // 2
        freq = (np.float32(1.0) / (np.float32(10000.0) ** (np.arange(0, half, 2, dtype=np.float32) / np.float32(half)))).astype(np.float32)
        parts_c, parts_s = [], []
        for pos in (tok // GRID, tok % GRID):
            ang = pos.astype(np.float32)[:, None] * freq[None, :]
            parts_c += [np.cos(ang), np.cos(ang)]
            parts_s += [-np.sin(ang), np.sin(ang)]
        c["cos" + name], c["sin" + name] = np.concatenate(parts_c, 1), np.concatenate(parts_s, 1)
    col = tok % GRID
    first = np.clip(col - WIN_C // 2, 0, GRID - WIN_C)[:, None]
    c["window"] = np.where((col[None, :] >= first) & (col[None, :] < first + WIN_C), 0.0, MASKED)
    return {k: np.ascontiguousarray(v, dtype=np.float32) for k, v in c.items()}


def conv_layout(w, b):
    both = np.concatenate([w[0], b], axis=0)
    x, bc = both[:, :SSD_IN], both[:, SSD_IN:]
    x = x.reshape(CONV_W + 1, SSD_G, CONV_T - 2, P)
    bc = bc.reshape(CONV_W + 1, 2, SSD_G, P).transpose(0, 2, 1, 3)
    both = np.concatenate([x, bc], axis=2)
    return np.ascontiguousarray(both.transpose(1, 3, 2, 0).reshape(SSD_G, P, CONV_T * (CONV_W + 1)))


def build(nc, shapes, out_shape, debug=None):
    def one(nc, gains):
        i = {n: nc.dram_tensor(f"in_{n}", s, F32, kind="ExternalInput").ap() for n, s in shapes.items()}
        out = nc.dram_tensor("out", out_shape, F32, kind="ExternalOutput").ap()
        with ExitStack() as ctx:
            return emit(nc, ctx, gains, i, out, debug)
    return one


def kernel(**inputs):
    import concourse.bacc as bacc
    from concourse.bass_utils import run_bass_kernel_spmd

    arrays = {n: np.ascontiguousarray(a) for n, a in inputs.items() if n not in ("ssd_conv_w", "ssd_conv_b")}
    arrays["conv"] = conv_layout(np.asarray(inputs["ssd_conv_w"]), np.asarray(inputs["ssd_conv_b"]))
    arrays.update(constants())
    shapes = {n: a.shape for n, a in arrays.items()}
    one = build(None, shapes, (1, S, D))
    gains = one(bacc.Bacc("TRN2", target_bir_lowering=False, num_devices=1), {})
    nc = bacc.Bacc("TRN2", target_bir_lowering=False, num_devices=1)
    one(nc, gains)
    r = run_bass_kernel_spmd(nc, [{f"in_{n}": a for n, a in arrays.items()}], core_ids=[0])
    return r.results[0]["out"]
```

```python
from contextlib import ExitStack, contextmanager
from itertools import chain

import numpy as np

import concourse.bass as bass
import concourse.mybir as mybir

F32 = mybir.dt.float32
F32R = mybir.dt.float32r
ALU = mybir.AluOpType
ACT = mybir.ActivationFunctionType
AX = mybir.AxisListType.X
ds = bass.ds

P = 128
S = 256
NT = S // P
D = 2048
KT = D // P
QK = 2
BLK = 512
RAW_RING = 4
SPLIT_RING = 8
AHEAD = 4
PIECES = KT // QK

SSD_IN = 2 * D
SSD_G, SSD_HG, SSD_P, SSD_N = 8, 8, 64, 128
SSD_H = SSD_G * SSD_HG
CONV_W = 4
CONV_T = 6
GLA_H, GLA_K, GLA_V, GLA_C, GLA_R = 4, 256, 512, 64, 16
FF = 4 * D
ALPHA = 2.0 ** 0.25
COL_Z = 0
COL_XBC = SSD_IN
COL_DT = COL_XBC + SSD_IN + 2 * SSD_G * SSD_N
COL_Q = COL_DT + SSD_H
COL_K = COL_Q + GLA_H * GLA_K
COL_V = COL_K + GLA_H * GLA_K
COL_G = COL_V + D
COL_GK = COL_G + D
COL_GATE = COL_GK + GLA_R
N_IN = COL_GATE + 2 * D

LAYERS = 2
HD = 128
A_H, A_KV, B_H, C_H = 8, 2, 4, 4
B_QL, B_KVL, B_ROPE = 512, 256, 64
GRID = 64
ROWS = S // GRID
WIN_R, WIN_C = 8, 16
UNIT_H = 4
C2_AQ = 0
C2_AK = C2_AQ + A_H * HD
C2_AV = C2_AK + A_KV * HD
C2_AG = C2_AV + A_KV * HD
C2_CQ = C2_AG + A_H * HD
C2_CKV = C2_CQ + B_QL
C2_KR = C2_CKV + B_KVL
C2_BG = C2_KR + B_ROPE
C2_Q = C2_BG + B_H * HD
C2_K = C2_Q + C_H * HD
C2_V = C2_K + C_H * HD
C2_G = C2_V + C_H * HD
N_IN2 = C2_G + C_H * HD
MASKED = -1.0e30

INPUTS = ["x", "w_in", "conv", "ssd_dt_bias", "ssd_A_log", "ssd_D", "ssd_norm_w", "gla_gk_w", "gla_gk_b",
          "gla_norm_w", "w_ssd_branch", "w_gla_branch", "gate_bias", "w_out", "ln1_g", "ln1_b", "w_up",
          "w_down", "ln2_g", "ln2_b", "norm_pre_2", "norm_post_2", "w_in_2", "a_q_norm_2", "a_k_norm_2",
          "b_q_norm_2", "b_kv_norm_2", "b_w_uq_2", "b_w_ukv_2", "c_rpb_2", "w_out_2"]


class Count:

    def __init__(self, prog, name, step=1):
        self.prog, self.name, self.step, self.n = prog, name, step, 0
        self.sem = prog.ctx.enter_context(prog.nc.semaphore(name))

    def up(self, instruction):
        instruction.then_inc(self.sem, self.step)
        self.n += self.step
        return self.now()

    def now(self, back=0):
        return Mark(self, self.n - back * self.step, tuple(self.prog.loops))


class Mark:
    def __init__(self, count, n, loops):
        self.count, self.n, self.loops = count, n, loops


class Loop:
    def __init__(self, prog, key, index, trips):
        self.key, self.index, self.trips = key, index, trips
        self.gain = prog.gains.get(key, {})


class Prog:

    def __init__(self, nc, ctx, gains):
        self.nc, self.ctx, self.gains, self.found = nc, ctx, gains, {}
        self.loops, self.counts, self.held, self.seen = [], {}, {}, {}
        self.n_loops = 0
        self.boundary = lambda: None
        self.pe = self.count("pe")
        self.act = self.count("act")
        self.dve = self.count("dve")
        self.pool = self.count("pool")

    def count(self, name, step=1):
        self.counts[name] = Count(self, name, step)
        return self.counts[name]

    def wait(self, engine, *marks):
        for m in marks:
            if m is None:
                continue
            open_at = tuple(x for x in m.loops if x in self.loops)
            known = self.seen.get((engine, m.count.name))
            if m.loops == open_at and known and known[0] == m.loops and known[1] >= m.n:
                continue
            if m.loops == open_at:
                self.seen[engine, m.count.name] = (m.loops, m.n)
            value, index = m.n, None
            for loop in m.loops:
                gain = loop.gain.get(m.count.name, 0)
                if not gain:
                    continue
                if loop in self.loops:
                    term = loop.index * gain
                    index = term if index is None else index + term
                else:
                    value += (loop.trips - 1) * gain
            if index is None:
                if value > 0:
                    engine.wait_ge(m.count.sem, value)
            else:
                assert value > 0, m.count.name
                engine.wait_ge(m.count.sem, index + value)

    @contextmanager
    def loop(self, trips, apart=True, carry=False):
        if not carry:
            self.boundary()
        if apart:
            self.meet()
        key = self.n_loops
        self.n_loops += 1
        before = {k: c.n for k, c in self.counts.items()}
        self.seen = {}
        with self.nc.Fori(0, trips) as index:
            loop = Loop(self, key, index, trips)
            self.loops.append(loop)
            yield index
            if not carry:
                self.boundary()
            if apart:
                self.meet()
            self.loops.pop()
        self.seen = {}
        self.found[key] = {}
        for k, c in self.counts.items():
            gain = c.n - before.get(k, 0)
            if gain:
                self.found[key][k] = gain
                c.n += (trips - 1) * gain
        if self.gains:
            assert self.found[key] == loop.gain, (key, self.found[key], loop.gain)

    def meet(self):
        nc = self.nc
        mine = [(nc.tensor, self.pe), (nc.scalar, self.act), (nc.vector, self.dve), (nc.gpsimd, self.pool)]
        for engine, _ in mine:
            for _, other in mine:
                self.wait(engine, other.now())
        self.held = {}

    def hold(self, what, *marks):
        self.held[what] = marks

    def free(self, engine, what):
        self.wait(engine, *self.held.get(what, ()))

    def T(self, f, *args, after=(), **kw):
        self.wait(self.nc.tensor, *after)
        return self.pe.up(f(*args, **kw))

    def A(self, f, *args, after=(), **kw):
        self.wait(self.nc.scalar, *after)
        return self.act.up(f(*args, **kw))

    def V(self, f, *args, after=(), **kw):
        self.wait(self.nc.vector, *after)
        return self.dve.up(f(*args, **kw))

    def G(self, f, *args, after=(), **kw):
        self.wait(self.nc.gpsimd, *after)
        return self.pool.up(f(*args, **kw))


def wide(ap, shape):
    return ap.to_broadcast(list(shape))


def emit(nc, ctx, gains, i, out, debug=None):
    pr = Prog(nc, ctx, gains)
    T, A, V, G, wait, hold, free = pr.T, pr.A, pr.V, pr.G, pr.wait, pr.hold, pr.free
    pe, act, dve, pool, sp = nc.tensor, nc.scalar, nc.vector, nc.gpsimd, nc.sync

    def sb(name, shape, dt=F32):
        return ctx.enter_context(nc.sbuf_tensor(name, shape, dt))

    def scratch(name, shape):
        kind = "ExternalOutput" if debug is not None and name in debug else "Internal"
        return nc.dram_tensor(name, shape, F32, kind=kind).ap()

    raw = sb("raw", [P, RAW_RING, QK, BLK])
    w_hi = sb("w_hi", [P, SPLIT_RING, QK, BLK], F32R)
    w_lo = sb("w_lo", [P, SPLIT_RING, QK, BLK], F32R)
    x_hi = sb("x_hi", [P, 2 * KT, S], F32R)
    x_lo = sb("x_lo", [P, 2 * KT, S], F32R)
    stage = sb("stage", [P, 2, NT, BLK])
    arena = sb("arena", [P, 14080])
    ident = sb("ident", [P, P])
    bank = [ctx.enter_context(nc.psum_tensor(f"bank{b}", [P, BLK], F32)) for b in range(8)]

    class Room:

        def __init__(self, at=0):
            self.at = at

        def __call__(self, *shape):
            n = int(np.prod(shape))
            a = arena[:, self.at:self.at + n]
            self.at += n
            assert self.at <= arena.shape[1], self.at
            if len(shape) == 2:
                a = a.rearrange("p (a b) -> p a b", a=shape[0])
            if len(shape) == 3:
                a = a.rearrange("p (a b c) -> p a b c", a=shape[0], b=shape[1])
            return a

    proj = scratch("proj", [S, N_IN])
    shared = scratch("shared", [S, SSD_H + GLA_R])
    proj2 = scratch("proj2", [S, N_IN2])
    latent = scratch("latent", [S, 2048])
    gated = scratch("gated", [S, D])
    heads_y = scratch("heads_y", [S, SSD_IN])
    heads_o = scratch("heads_o", [S, D])
    skew = scratch("skew", [C_H * (2 * ROWS - 1), GRID, P])

    def rows(ap):
        return ap.rearrange("(t p) n -> p t n", p=P)

    s_raw = [pr.count(f"s_raw{n}", 16) for n in range(RAW_RING)]
    s_hi = pr.count("s_hi")
    s_lo = pr.count("s_lo")
    s_mm = pr.count("s_mm")
    s_dra = pr.count("s_dra")
    s_drv = pr.count("s_drv")
    s_st = [pr.count(f"s_st{n}", 16) for n in range(2)]
    d_in = pr.count("d_in", 16)
    d_late = pr.count("d_late", 16)
    d_gate = pr.count("d_gate", 16)
    d_part = pr.count("d_part", 16)
    d_out = pr.count("d_out", 16)
    at = {"piece": 0, "block": 0, "drain": None, "save": None, "turn": 0, "since": 0, "beside": None,
          "waiting": [], "every": 2}

    def summed():
        return s_mm.now(at["since"])

    def load(to, source, *after, count=d_in):
        wait(act, *after)
        return count.up(act.dma_start(to, source))

    def store(to, source, *after):
        wait(act, *after)
        return d_out.up(act.dma_start(to, source))

    def piece(weight, x0, kts, n, banks, q, pieces):
        slot, half = at["piece"] % RAW_RING, at["piece"] % SPLIT_RING
        at["piece"] += 1
        source = weight()
        wait(sp, s_lo.now(RAW_RING - 1 if at["piece"] > 1 else 0))
        col = 0
        for part in source if isinstance(source, list) else [source]:
            width = part.shape[-1]
            landed = s_raw[slot].up(sp.dma_start(raw[:, slot, 0:kts, col:col + width], part))
            col += width
        wait(act, landed, s_mm.now(SPLIT_RING - 1 - len(at["waiting"])))
        hi = s_hi.up(act.activation(w_hi[:, half, 0:kts, 0:n], raw[:, slot, 0:kts, 0:n], ACT.Copy))
        wait(dve, hi)
        s_lo.up(dve.tensor_tensor(w_lo[:, half, 0:kts, 0:n], raw[:, slot, 0:kts, 0:n],
                                  w_hi[:, half, 0:kts, 0:n].bitcast(F32), ALU.subtract))

        def products():
            first, last = q == 0, q == pieces - 1
            if first:
                wait(pe, s_drv.now())
            wait(pe, s_lo.now(len(at["waiting"])))
            for k in range(kts):
                for t in range(NT):
                    tok = slice(t * P, t * P + P)
                    a, b = first and k == 0, last and k == kts - 1
                    o = bank[banks + t][:, 0:n]
                    pe.matmul(o, x_hi[:, x0 + k, tok], w_lo[:, half, k, 0:n], start=a, stop=False)
                    pe.matmul(o, x_hi[:, x0 + k, tok], w_hi[:, half, k, 0:n], start=False, stop=False)
                    mm = pe.matmul(o, x_lo[:, x0 + k, tok], w_hi[:, half, k, 0:n], start=False, stop=b)
            s_mm.up(mm)
            at["since"] += 1
            if q % at["every"] == at["every"] - 1 or last:
                step()
        return products

    def caught_up(left=0):
        while len(at["waiting"]) > left:
            at["waiting"].pop(0)()

    def aligned():
        caught_up()
        at["piece"] = 0
        wait(act, s_mm.now())

    pr.boundary = caught_up

    def beside(steps, every=2):
        at["beside"], at["every"] = steps, every

    def step():
        if at["beside"] is not None:
            next(at["beside"], None)

    def stepped():
        assert next(at["beside"], None) is None
        at["beside"] = None

    def ended():
        caught_up()
        if at["beside"] is not None:
            for _ in at["beside"]:
                pass
        at["beside"] = None

    def drained(late=False):
        if not late:
            caught_up()
        if at["drain"] is not None:
            at["save"] = at["drain"]()
            at["drain"] = None
        if not late:
            saved()

    def saved():
        if at["save"] is not None:
            at["save"]()
            at["save"] = None

    def block(weight, x0, kts, n, drain):
        half = at["block"] % 2
        at["block"] += 1
        pieces = max(1, kts // QK)
        own = at["own"] = {"drain": drain}

        def after(q, products):
            products()
            if q == min(AHEAD - 1, pieces) - 1:
                drained(late=True)
            if q == min(AHEAD, pieces) - 1:
                saved()
            if q == pieces - 1:
                at["since"] = 0
                at["drain"] = lambda: own["drain"](half, n)
        for q in range(pieces):
            products = piece(lambda: weight(q), x0 + q * QK, min(QK, kts), n, 2 * half, q, pieces)
            at["waiting"].append(lambda q=q, products=products: after(q, products))
            caught_up(AHEAD)

    def again(drain):
        at["own"]["drain"] = drain

    def weight_at(w, col, n):
        w = w.rearrange("(k p) n -> p k n", p=P)
        kts = min(QK, w.shape[1])

        def get(q):
            c = col
            if not isinstance(col, int):
                c = sp.snap(col)
            return w[:, q * kts:(q + 1) * kts, ds(c, n)]
        return get

    def segment(w, col, blocks, x0, drain, n=BLK):
        def one(j):
            block(weight_at(w, j * n + col, n), x0, KT, n, drain(j))

        one(0)
        done = 1
        if blocks > 5:
            turns = (blocks - 1) // 2
            with pr.loop(turns, apart=False, carry=True) as turn:
                again(drain(turn * 2))
                one(turn * 2 + 1)
                one(turn * 2 + 2)
            again(drain(2 * turns))
            done += 2 * turns
        for j in range(done, blocks):
            one(j)

    def to_dram(dest, col):
        def drain_of(j):
            def drain(half, n):
                wait(act, summed(), s_st[half].now())
                s_dra.up(act.activation(stage[:, half, 0, 0:n], bank[2 * half][:, 0:n], ACT.Copy))
                wait(dve, summed(), s_st[half].now(), s_dra.now())
                s_drv.up(dve.tensor_copy(stage[:, half, 1, 0:n], bank[2 * half + 1][:, 0:n]))
                full = s_drv.now()

                def save():
                    wait(act, full)
                    s_st[half].up(act.dma_start(rows(dest)[:, :, ds(j * BLK + col, n)], stage[:, half, :, 0:n]))
                return save
            return drain
        return drain_of

    def to_sum(total, add, then=None):
        def drain_of(j):
            def drain(half, n):
                before = s_drv.now()
                wait(dve, summed())
                for t in range(NT):
                    to = total[:, t, j * BLK:j * BLK + n]
                    b = bank[2 * half + t][:, 0:n]
                    if add:
                        wait(dve, before)
                        last = dve.tensor_tensor(to, b, to, ALU.add)
                    else:
                        last = dve.tensor_copy(to, b)
                added = s_drv.up(last)
                return then and (lambda: then(j, added))
            return drain
        return drain_of

    TP = (6, 7)

    def turn4(source, x0, t, *after, tiles=4, unread=None, banks=TP):
        b = banks[at["turn"] % len(banks)]
        at["turn"] += 1
        free(pe, b)
        wait(pe, *after)
        for k in range(tiles):
            last = pe.transpose(bank[b][:, k * P:(k + 1) * P], source[:, k * P:(k + 1) * P], ident[:, :])
        turned = pr.pe.up(last)

        def split():
            full = bank[b][:, 0:tiles * P].rearrange("p (k n) -> p k n", k=tiles)
            hi, lo = x_hi[:, ds(x0, tiles), t * P:(t + 1) * P], x_lo[:, ds(x0, tiles), t * P:(t + 1) * P]
            rounded = A(act.activation, hi, full, ACT.Copy, after=(turned, unread or s_mm.now()))
            rest = V(dve.tensor_tensor, lo, full, hi.bitcast(F32), ALU.subtract, after=(rounded,))
            hold(b, rest)
            return rest
        return split

    def transpose4(*args, **kw):
        return turn4(*args, **kw)()

    def transpose_all(source, x0, after):
        for t in range(NT):
            for k in range(0, KT, 4):
                last = transpose4(source[:, t, k * P:(k + 4) * P], x0 + k, t, after(t, k), banks=(4, 5, 6, 7))
        wait(pe, last)

    def by_columns(source, x0, arrived):
        for n, m in enumerate(arrived):
            for t in range(NT):
                last = transpose4(source[:, t, n * BLK:(n + 1) * BLK], x0 + 4 * n, t, m, banks=(4, 5, 6, 7))
        wait(pe, last)

    def row_of(w, n):
        return w.rearrange("(a n) -> a n", a=1).partition_broadcast(P) if len(w.shape) == 1 else w

    def inverse_root(to, sums, n, eps, *after):
        m = V(dve.tensor_scalar, to, sums, 1.0 / n, eps, ALU.mult, ALU.add, after=after)
        m = V(dve.reciprocal, to, to, after=(m,))
        return A(act.activation, to, to, ACT.Sqrt, after=(m,))

    def log1p_exp(to, x, e, u, *after):
        m = V(dve.scalar_tensor_tensor, e, x, -1.0, x, ALU.mult, ALU.max, after=after)
        m = A(act.activation, e, e, ACT.Exp, scale=-1.0, after=(m,))
        mu = V(dve.tensor_scalar, u, e, 1.0, None, ALU.add, after=(m,))
        ml = A(act.activation, to, u, ACT.Ln, after=(mu,))
        m = V(dve.scalar_tensor_tensor, e, u, -1.0, e, ALU.add, ALU.subtract, after=(mu,))
        m = V(dve.reciprocal, u, u, after=(m, ml))
        m = V(dve.tensor_tensor, e, e, u, ALU.mult, after=(m,))
        return V(dve.tensor_tensor, to, to, e, ALU.subtract, after=(m,))

    room = Room()
    xin = room(NT, D)
    load(ident[:, :], i["identity"])
    arrived = [load(xin[:, :, n * BLK:(n + 1) * BLK], rows(i["x"][0])[:, :, n * BLK:(n + 1) * BLK], count=count)
               for n, count in enumerate((d_in, d_late, d_gate, d_part))]
    by_columns(xin, 0, arrived)

    w_in = i["w_in"][0]

    def small(q):
        return [weight_at(w_in, c, n)(q) for c, n in ((COL_DT, SSD_H), (COL_GK, GLA_R))]

    block(small, 0, KT, SSD_H + GLA_R, to_dram(shared, 0)(0))
    flat = lambda ap: ap.rearrange("p a b -> p (a b)")

    room = Room()
    TAB = 10
    tab = room(TAB, SSD_H)
    DT, AA, CS, EC, DW, DD = 0, 2, 4, 6, 8, 9
    tri = room(P)
    ones = room(P)
    t_a, t_b, t_c = room(NT, SSD_H), room(NT, SSD_H), room(NT, SSD_H)
    alog, bias = room(SSD_H), room(SSD_H)

    def ssd_shared():
        for _ in range(AHEAD):
            yield
        pr.meet()
        load(tri, i["causal"])
        load(t_a, rows(shared)[:, :, 0:SSD_H], s_st[0].now(), s_st[1].now())
        load(bias, row_of(i["ssd_dt_bias"][0], SSD_H))
        load(alog, row_of(i["ssd_A_log"][0], SSD_H))
        loaded = load(tab[:, DD, :], row_of(i["ssd_D"][0], SSD_H))
        m_ones = G(pool.memset, ones, 1.0)
        yield
        for t in range(NT):
            m = V(dve.tensor_tensor, t_a[:, t, :], t_a[:, t, :], bias, ALU.add, after=(loaded,))
        m = log1p_exp(flat(tab[:, DT:DT + 2, :]), flat(t_a), flat(t_b), flat(t_c), m)
        m = V(dve.scalar_tensor_tensor, flat(tab[:, DT:DT + 2, :]), flat(t_a), 0.0, flat(tab[:, DT:DT + 2, :]),
              ALU.max, ALU.add, after=(m,))
        me = A(act.activation, alog, alog, ACT.Exp, after=(loaded,))
        for t in range(NT):
            m = V(dve.scalar_tensor_tensor, tab[:, AA + t, :], tab[:, DT + t, :], -1.0, alog, ALU.mult, ALU.mult,
                  after=(m, me))
        n2 = NT * SSD_H
        mt = T(pe.matmul, bank[4][:, 0:n2], tri, flat(tab[:, AA:AA + 2, :]), start=True, stop=True, after=(m,))
        m2 = T(pe.matmul, bank[5][:, 0:n2], ones, flat(tab[:, AA:AA + 2, :]), start=True, stop=True, after=(m_ones,))
        yield
        mc = V(dve.tensor_copy, flat(tab[:, CS:CS + 2, :]), bank[4][:, 0:n2], after=(mt, m2))
        A(act.activation, flat(tab[:, EC:EC + 2, :]), flat(tab[:, CS:CS + 2, :]), ACT.Exp, after=(mc,))
        m = V(dve.tensor_tensor, alog, bank[5][:, 0:SSD_H], tab[:, CS, :], ALU.subtract, after=(mc,))
        m = A(act.activation, alog, alog, ACT.Exp, after=(m,))
        V(dve.tensor_tensor, tab[:, DW, :], tab[:, DT, :], alog, ALU.mult, after=(m,))

    beside(ssd_shared())
    for j in range(3):
        block(weight_at(w_in, COL_Z + j * BLK, BLK), 0, KT, BLK, to_dram(proj, COL_Z + j * BLK)(0))
    ended()
    segment(w_in, COL_Z + 3 * BLK, (COL_DT - COL_Z) // BLK - 3, 0, to_dram(proj, COL_Z + 3 * BLK))
    block(weight_at(w_in, COL_Q, BLK), 0, KT, BLK, to_dram(proj, COL_Q)(0))

    CH = SSD_HG * SSD_P
    pr.meet()
    wait(act, s_st[0].now(), s_st[1].now())
    gt = room(TAB, SSD_HG)
    xin = room(NT, CONV_T * P)
    z = room(NT, CH)
    cw = room(CONV_T, CONV_W + 1)
    nw = room(CH)
    ut = room(CONV_T, S + CONV_W - 1)
    cv = room(CONV_T, S)
    xt = room(NT, CH)
    xdt = room(NT, CH)
    xw = room(CH)
    yo = room(CH)
    btok = room(P)
    cbm = room(NT, P)
    dec = room(NT, SSD_HG, P)
    prev = room(CH)
    ysum = room(2, 1)
    HB = SSD_HG // 2
    by_head = lambda ap: ap.rearrange("p (h e) -> p h e", h=SSD_HG)
    V(dve.memset, ut[:, :, 0:CONV_W - 1], 0.0)
    DEC_BANK = {(0, 0): 7, (0, 1): 6, (1, 0): 5, (1, 1): 4}

    def ssd_group(g):
        pr.meet()
        pp = rows(proj)
        load(xin[:, :, 0:CH], pp[:, :, ds(g * CH + COL_XBC, CH)])
        load(xin[:, :, CH:CH + P], pp[:, :, ds(g * P + (COL_XBC + SSD_IN), P)])
        load(xin[:, :, CH + P:CH + 2 * P], pp[:, :, ds(g * P + (COL_XBC + SSD_IN + SSD_G * SSD_N), P)])
        m_in = load(flat(cw), i["conv"][ds(g, 1)].rearrange("a p n -> (a p) n"))
        load(z, pp[:, :, ds(g * CH + COL_Z, CH)], count=d_late)
        m_z = load(nw, row_of(i["ssd_norm_w"][0][ds(g * CH, CH)], CH), count=d_late)
        m_gt = V(dve.tensor_copy, gt, tab[:, :, ds(g * SSD_HG, SSD_HG)])
        m_cs = {}
        for (t, hb), b in DEC_BANK.items():
            for h in range(HB):
                m_cs[t, hb] = T(pe.matmul, bank[b][:, h * P:(h + 1) * P],
                                wide(gt[:, AA + t, hb * HB + h:hb * HB + h + 1], [P, P]), tri, start=True, stop=True,
                                after=(m_gt,))
        yield
        m_dec = {}
        for (t, hb), b in DEC_BANK.items():
            for h in range(HB):
                hh = hb * HB + h
                ms = V(dve.tensor_scalar, dec[:, t, hh, :], bank[b][:, h * P:(h + 1) * P],
                       gt[:, CS + t, hh:hh + 1], 0.0, ALU.subtract, ALU.min, after=(m_cs[t, hb],))
            some = dec[:, t, hb * HB:(hb + 1) * HB, :]
            m_dec[t, hb] = A(act.activation, some, some, ACT.Exp, after=(ms,))
        CB = (4, 5, 6)
        m_u = []
        for n in range(3):
            for c in (2 * n, 2 * n + 1):
                for t in range(NT):
                    m = T(pe.transpose, bank[CB[n]][:, (c % 2) * S + t * P:(c % 2) * S + (t + 1) * P],
                          xin[:, t, c * P:(c + 1) * P], ident[:, :], after=(m_in, ms))
            m_u.append(m)
        yield
        def conv(tiles):
            for w in range(1, CONV_W):
                for c in tiles:
                    m_cv[c] = V(dve.scalar_tensor_tensor, cv[:, c, :], ut[:, c, w:w + S], cw[:, c, w:w + 1],
                                cv[:, c, :], ALU.mult, ALU.add, after=(m_cv[c],))
            for c in tiles:
                m = A(act.activation, cv[:, c, :], cv[:, c, :], ACT.Silu, bias=cw[:, c, CONV_W:CONV_W + 1],
                      after=(m_cv[c],))
            return m

        m_cv = [None] * CONV_T
        for n in (2, 0, 1):
            mu = A(act.activation, ut[:, 2 * n:2 * n + 2, CONV_W - 1:],
                   bank[CB[n]][:, :].rearrange("p (a b) -> p a b", a=2), ACT.Copy, after=(m_u[n],))
            for c in (2 * n, 2 * n + 1):
                m_cv[c] = A(act.activation, cv[:, c, :], ut[:, c, 0:S], ACT.Copy, scale=cw[:, c, 0:1], after=(mu,))
            if n == 2:
                m_bc = conv((4, 5))
        for t in range(NT):
            tok = slice(t * P, t * P + P)
            T(pe.matmul, bank[4][:, tok], cv[:, 4, tok], cv[:, 5, tok], start=True, stop=True, after=(m_bc, mu))
        m_bt = T(pe.transpose, bank[4][:, S:S + P], cv[:, 4, 0:P], ident[:, :])
        yield
        m_s = conv((0, 1))
        for t in range(NT):
            m_cbm = V(dve.tensor_tensor, cbm[:, t, :], bank[4][:, t * P:(t + 1) * P], tri, ALU.mult, after=(m_bt,))
        m_bt = A(act.activation, btok, bank[4][:, S:S + P], ACT.Copy, after=(m_bt, m_cbm))
        for (t, hb), m in m_dec.items():
            some = dec[:, t, hb * HB:(hb + 1) * HB, :]
            m_dec[t, hb] = G(pool.tensor_tensor, some, some, wide(cbm[:, t, :].unsqueeze(1), [P, HB, P]), ALU.mult,
                             after=(m, m_cbm))
        yield
        m_s = conv((2, 3))
        for t in range(NT):
            m_sz = A(act.activation, z[:, t, :], z[:, t, :], ACT.Silu, after=(m_z,))
        for t in range(NT):
            for c in range(4):
                m_x = T(pe.transpose, bank[5 + t][:, c * P:(c + 1) * P], cv[:, c, t * P:(t + 1) * P], ident[:, :],
                        after=(m_s,))
        yield
        for t in range(NT):
            m_xt = A(act.activation, xt[:, t, :], bank[5 + t][:, :], ACT.Copy, after=(m_x,))
        for t in range(NT):
            m_xd = V(dve.tensor_tensor, by_head(xdt[:, t, :]), by_head(xt[:, t, :]),
                     wide(gt[:, DT + t, :].unsqueeze(2), [P, SSD_HG, SSD_P]), ALU.mult, after=(m_xt,))
        m_xw = V(dve.tensor_tensor, by_head(xw), by_head(xt[:, 0, :]),
                 wide(gt[:, DW, :].unsqueeze(2), [P, SSD_HG, SSD_P]), ALU.mult)
        m_st = T(pe.matmul, bank[4][:, :], btok, xw, start=True, stop=True, after=(m_bt, m_xw))
        m_y = []
        for t in range(NT):
            for h in range(SSD_HG):
                m = T(pe.matmul, bank[5 + t][:, h * SSD_P:(h + 1) * SSD_P], dec[:, t, h, :],
                      xdt[:, t, h * SSD_P:(h + 1) * SSD_P], start=True, stop=True, after=(m_dec[t, h // HB],))
            m_y.append(m)
        yield
        m_pv = A(act.activation, prev, bank[4][:, :], ACT.Copy, after=(m_st,))

        def skip(t):
            yt = xt[:, t, :]
            m = V(dve.tensor_tensor, by_head(yt), by_head(yt), wide(gt[:, DD, :].unsqueeze(2), [P, SSD_HG, SSD_P]),
                  ALU.mult, after=(m_xw,))
            return V(dve.tensor_tensor, yt, yt, bank[5 + t][:, :], ALU.add, after=(m, m_y[t]))

        def gated_squares(t, *after):
            yt = xt[:, t, :]
            m = V(dve.tensor_tensor, yt, yt, z[:, t, :], ALU.mult, after=(*after, m_sz))
            return V(dve.tensor_tensor_reduce, xdt[:, t, :], yt, yt, 1.0, 0.0, ALU.mult, ALU.add, ysum[:, t, :],
                     after=(m, m_y[1]))
        m_sq = gated_squares(0, skip(0))
        m_off = T(pe.matmul, bank[7][:, :], cv[:, 5, P:2 * P], prev, start=True, stop=True, after=(m_pv,))
        yield
        mx = skip(1)
        mo = V(dve.tensor_tensor, by_head(yo), by_head(bank[7][:, :]),
               wide(gt[:, EC + 1, :].unsqueeze(2), [P, SSD_HG, SSD_P]), ALU.mult, after=(m_off,))
        mx = V(dve.tensor_tensor, xt[:, 1, :], xt[:, 1, :], yo, ALU.add, after=(mx, mo))
        mx = gated_squares(1, mx)
        ms = inverse_root(flat(ysum), flat(ysum), CH, 1e-5, m_sq, mx)
        for t in range(NT):
            ms = V(dve.scalar_tensor_tensor, xt[:, t, :], xt[:, t, :], ysum[:, t, :], nw, ALU.mult, ALU.mult,
                   after=(ms, m_z))
        store(rows(heads_y)[:, :, ds(g * CH, CH)], xt, ms)

    with pr.loop(SSD_G, apart=False, carry=True) as g:
        again(to_dram(proj, COL_Q)(g))
        beside(ssd_group(g))
        block(weight_at(w_in, g * BLK + COL_GATE, BLK), 0, KT, BLK, to_dram(proj, COL_GATE)(g))
        block(weight_at(w_in, g * BLK + (COL_Q + BLK), BLK), 0, KT, BLK, to_dram(proj, COL_Q + BLK)(g))
        stepped()
    again(to_dram(proj, COL_Q)(SSD_G))

    room = Room()
    halves = [room(NT, D), room(NT, D)]
    yloads = []

    def turned():
        for _ in range(AHEAD):
            yield
        pr.meet()
        yloads.extend(load(halves[n], rows(heads_y)[:, :, n * D:(n + 1) * D], d_out.now(), count=count)
                      for n, count in ((1, d_in), (0, d_late)))
        yield
        yield
        for t in range(NT):
            for k in range(0, KT, 4):
                split = turn4(halves[1][:, t, k * P:(k + 4) * P], KT + k, t, yloads[0])
                yield
                split()

    beside(turned(), 1)
    for j in range(SSD_G + 1, (COL_GK - COL_Q) // BLK):
        block(weight_at(w_in, COL_Q + j * BLK, BLK), 0, KT, BLK, to_dram(proj, COL_Q + j * BLK)(0))
    ended()
    drained()
    wait(act, s_st[0].now(), s_st[1].now())
    transpose_all(halves[0], 0, lambda t, k: yloads[1])
    pr.meet()

    room = Room()
    low = room(NT, GLA_R)
    lowt = room(S)
    tri64, sum64, last64 = room(P), room(P), room(2)
    most, least = room(GLA_C), room(GLA_C)
    gnw = room(GLA_V)
    load(low, rows(shared)[:, :, SSD_H:SSD_H + GLA_R])
    load(tri64, i["causal64"])
    load(most, i["most64"])
    load(least, i["least64"])
    load(sum64, i["blocks64"])
    load(last64, i["columns64"])
    loaded = load(gnw, row_of(i["gla_norm_w"][0], GLA_V))
    m1 = V(dve.memset, lowt[0:GLA_R + 1, :], 1.0)
    for t in range(NT):
        m = T(pe.transpose, bank[4][0:GLA_R, t * P:(t + 1) * P], low[:, t, :], ident[:, :], after=(loaded,))
    V(dve.tensor_copy, lowt[0:GLA_R, :], bank[4][0:GLA_R, 0:S], after=(m, m1))
    q, k, v, gg = room(NT, GLA_K), room(NT, GLA_K), room(NT, GLA_V), room(NT, GLA_V)
    gkw = room(GLA_K)
    gk, e1, e2, e3 = room(NT, GLA_K), room(NT, GLA_K), room(NT, GLA_K), room(NT, GLA_K)
    qt, kt = room(2, S), room(2, S)
    dk = room(2, NT * 2)
    state = [room(2, GLA_V), room(2, GLA_V)]
    att = room(NT, P)
    osum = room(2, 1)
    o = room(NT, GLA_V)
    gate, grow = room(NT, BLK), room(BLK)
    V(dve.memset, att, 0.0)
    tok_of = lambda c: slice(c * GLA_C, (c + 1) * GLA_C)
    part_of = lambda c: slice((c % 2) * GLA_C, (c % 2 + 1) * GLA_C)

    def gla_head(h):
        pr.meet()
        pp = rows(proj)
        load(gkw[0:GLA_R, :], i["gla_gk_w"][0][:, ds(h * GLA_K, GLA_K)])
        load(gkw[GLA_R:GLA_R + 1, :], i["gla_gk_b"][:, ds(h * GLA_K, GLA_K)])
        load(q, pp[:, :, ds(h * GLA_K + COL_Q, GLA_K)])
        load(k, pp[:, :, ds(h * GLA_K + COL_K, GLA_K)])
        m_in = load(v, pp[:, :, ds(h * GLA_V + COL_V, GLA_V)])
        m_g = load(gg, pp[:, :, ds(h * GLA_V + COL_G, GLA_V)], count=d_late)
        yield
        for t in range(NT):
            m = T(pe.matmul, bank[4][:, t * GLA_K:(t + 1) * GLA_K], lowt[0:GLA_R + 1, t * P:(t + 1) * P],
                  gkw[0:GLA_R + 1, :], start=True, stop=True, after=(m_in,))
        yield
        m = V(dve.tensor_copy, flat(e1), bank[4][:, :], after=(m,))
        m = log1p_exp(flat(gk), flat(e1), flat(e2), flat(e3), m)
        m = V(dve.scalar_tensor_tensor, flat(gk), flat(e1), 0.0, flat(gk), ALU.min, ALU.subtract, after=(m,))
        m_gk = V(dve.tensor_scalar, flat(gk), flat(gk), 1.0 / 16.0, None, ALU.mult, after=(m,))
        T(pe.matmul, bank[5][:, :], tri64, flat(gk), start=True, stop=True, after=(m_gk,))
        T(pe.matmul, bank[6][:, :], sum64, flat(gk), start=True, stop=True)
        for kk in range(2):
            for t in range(NT):
                m = T(pe.matmul, bank[7][:, kk * 4 + 2 * t:kk * 4 + 2 * t + 2], gk[:, t, kk * P:(kk + 1) * P],
                      last64, start=True, stop=True)
        yield
        m_e1 = A(act.activation, flat(e1), bank[5][:, :], ACT.Copy, after=(m,))
        m_e2 = A(act.activation, flat(e2), bank[5][:, :], ACT.Exp)
        m_e3 = A(act.activation, flat(e3), bank[5][:, :], ACT.Exp, scale=-1.0)
        m_dk = A(act.activation, flat(dk), bank[7][:, 0:8], ACT.Exp)
        m = V(dve.tensor_tensor, flat(e1), bank[6][:, :], flat(e1), ALU.subtract, after=(m_e1,))
        m_e1 = A(act.activation, flat(e1), flat(e1), ACT.Exp, after=(m,))
        m_q = V(dve.scalar_tensor_tensor, flat(e2), flat(q), GLA_K ** -0.5, flat(e2), ALU.mult, ALU.mult,
                after=(m_e2, m_in))
        m_k = V(dve.tensor_tensor, flat(e3), flat(k), flat(e3), ALU.mult, after=(m_e3,))
        m_kd = V(dve.tensor_tensor, flat(e1), flat(k), flat(e1), ALU.mult, after=(m_e1,))
        m_t = []
        for src, b, ms in ((e2, 4, m_q), (e3, 7, m_k)):
            for kk in range(2):
                for t in range(NT):
                    m = T(pe.transpose, bank[b][:, kk * S + t * P:kk * S + (t + 1) * P],
                          src[:, t, kk * P:(kk + 1) * P], ident[:, :], after=(ms, m_dk))
            m_t.append(m)
        yield
        m_qt = A(act.activation, flat(qt), bank[4][:, :], ACT.Copy, after=(m_t[0],))
        m_kt = A(act.activation, flat(kt), bank[7][:, :], ACT.Copy, after=(m_t[1],))
        for c in range(2 * NT):
            t = c // 2
            for kk in range(2):
                m_a = T(pe.matmul, bank[5][part_of(c), t * GLA_C:(t + 1) * GLA_C], kt[:, kk, tok_of(c)],
                        qt[:, kk, tok_of(c)], start=(kk == 0), stop=(kk == 1), after=(m_kt, m_e1))

        def update(c, *after):
            for kk in range(2):
                m = T(pe.matmul, bank[6 + kk][:, :], e1[part_of(c), c // 2, kk * P:(kk + 1) * P],
                      v[part_of(c), c // 2, :], start=True, stop=True, after=after)
            return m

        def advance(c, m):
            now, nxt = state[c % 2], state[(c + 1) % 2]
            for kk in range(2):
                if c:
                    ms = V(dve.scalar_tensor_tensor, nxt[:, kk, :], now[:, kk, :], dk[:, kk, c:c + 1],
                           bank[6 + kk][:, :], ALU.mult, ALU.add, after=(m, m_state[c - 1]))
                else:
                    ms = V(dve.tensor_copy, nxt[:, kk, :], bank[6 + kk][:, :], after=(m,))
            m_state.append(ms)

        def carried(c):
            for kk in range(2):
                m = T(pe.matmul, bank[4 + c // 2][part_of(c), :], qt[:, kk, tok_of(c)], state[c % 2][:, kk, :],
                      start=False, stop=True, skip_group_check=True, after=(m_state[c - 1],))
            return m
        m_state = []
        m_up = update(0, m_kd, m_kt)
        yield
        for half in range(2):
            part = part_of(half)
            inner = att[part, :, part]
            ma = V(dve.tensor_tensor, inner, bank[5][part, 0:NT * GLA_C].rearrange("p (t n) -> p t n", t=NT),
                   wide(most[part, :].unsqueeze(1), [GLA_C, NT, GLA_C]), ALU.min, after=(m_a,))
            m_att = V(dve.tensor_tensor, inner, inner, wide(least[part, :].unsqueeze(1), [GLA_C, NT, GLA_C]),
                      ALU.max, after=(ma,))
        advance(0, m_up)
        for t in range(NT):
            T(pe.matmul, bank[4 + t][:, :], att[:, t, :], v[:, t, :], start=True, stop=True, after=(m_att, m_qt))
        m_o = [carried(1)]
        m_up = update(1, m_state[0])
        yield
        advance(1, m_up)
        for t in range(NT):
            m_sg = A(act.activation, gg[:, t, :], gg[:, t, :], ACT.Silu, after=(m_g,))
        carried(2)
        m_up = update(2, m_state[1])
        yield
        advance(2, m_up)
        m_o.append(carried(3))
        for t in range(NT):
            mo = A(act.activation, o[:, t, :], bank[4 + t][:, :], ACT.Copy, after=(m_o[t],))
            ms = V(dve.tensor_tensor_reduce, e2.rearrange("p t n -> p (t n)"), o[:, t, :], o[:, t, :], 1.0, 0.0,
                   ALU.mult, ALU.add, osum[:, t, :], after=(mo, m_t[1], pr.dve.now()))
        ms = inverse_root(flat(osum), flat(osum), GLA_V, 1e-5, ms)
        for t in range(NT):
            m = V(dve.scalar_tensor_tensor, o[:, t, :], o[:, t, :], osum[:, t, :], gnw, ALU.mult, ALU.mult,
                  after=(ms,))
            m = V(dve.tensor_tensor, o[:, t, :], o[:, t, :], gg[:, t, :], ALU.mult, after=(m, m_sg))
        store(rows(heads_o)[:, :, ds(h * GLA_V, GLA_V)], o, m)

    def gate_of(j, which, *after):
        load(gate, rows(proj)[:, :, ds(j * BLK + (COL_GATE + which * D), BLK)], *after, count=d_gate)
        return load(grow, row_of(i["gate_bias"][0, which][ds(j * BLK, BLK)], BLK), count=d_gate)

    def sigmoid_gate(loaded):
        for t in range(NT):
            m = V(dve.tensor_tensor, gate[:, t, :], gate[:, t, :], grow, ALU.add, after=(loaded,))
            m = A(act.activation, gate[:, t, :], gate[:, t, :], ACT.Sigmoid, after=(m,))
        return m

    def ssd_branch_drain(j):
        def drain(half, n):
            m = sigmoid_gate(d_gate.now())
            wait(dve, summed(), s_st[half].now(), m)
            for t in range(NT):
                last = dve.tensor_tensor(stage[:, half, t, 0:n], bank[2 * half + t][:, 0:n], gate[:, t, 0:n],
                                         ALU.mult)
            s_drv.up(last)
            full = s_drv.now()

            def save():
                wait(act, full)
                s_st[half].up(act.dma_start(rows(gated)[:, :, ds(j * BLK, n)], stage[:, half, :, 0:n]))
            return save
        return drain

    w_branch = i["w_ssd_branch"][0]
    def heads(h, count):
        for n in range(count):
            gate_of(h + n, 0, s_drv.now())
            beside(gla_head(h + n), 1)
            block(weight_at(w_branch, (h + n) * BLK, BLK), 0, 2 * KT, BLK, ssd_branch_drain(h + n))
            ended()
            drained()

    with pr.loop(GLA_H, apart=False) as h:
        heads(h, 1)
    pr.meet()
    wait(act, s_st[0].now(), s_st[1].now(), s_drv.now())

    room = Room()
    total = ov = room(NT, D)
    ln_g, ln_b = room(D), room(D)
    parts, shift, spread = room(NT, D // BLK), room(2, 1), room(2, 1)
    work_at = room.at
    merged = room(2, NT, BLK)
    other = room(NT, BLK)
    gate, grow = room(NT, BLK), room(BLK)
    arrived = [load(ov[:, :, n * BLK:(n + 1) * BLK], rows(heads_o)[:, :, n * BLK:(n + 1) * BLK], d_out.now(),
                    count=count) for n, count in enumerate((d_in, d_late, d_gate, d_part))]
    by_columns(ov, 0, arrived)

    def sum_begins(source, g_row, b_row, *after):
        if source is not None:
            load(total, source, *after, count=d_late)
        load(ln_g, row_of(g_row, D), *after, count=d_late)
        m = load(ln_b, row_of(b_row, D), count=d_late)
        yield
        yield
        for t in range(NT):
            yield
            m = A(act.activation, total[:, t, :], total[:, t, :], ACT.Copy, scale=ALPHA, after=(m, *after))
        wait(dve, m)

    beside(sum_begins(rows(i["x"][0]), i["ln1_g"][0], i["ln1_b"][0], pr.pe.now()))

    def others(j):
        load(other, rows(gated)[:, :, j * BLK:(j + 1) * BLK], pr.dve.now(), count=d_gate)
        gate_of(j, 1)

    def gla_branch_drain(j):
        def drain(half, n):
            free(dve, ("merged", half))
            m = sigmoid_gate(d_gate.now())
            wait(dve, summed(), m)
            for t in range(NT):
                last = dve.tensor_tensor(merged[:, half, t, :], bank[2 * half + t][:, 0:n], gate[:, t, :], ALU.mult)
            s_drv.up(last)
            for t in range(NT):
                m = V(dve.tensor_tensor, merged[:, half, t, :], merged[:, half, t, :], other[:, t, :], ALU.add,
                      after=(s_drv.now(),))
            splits = [turn4(merged[:, half, t, :], KT + 4 * j, t, m, unread=summed()) for t in range(NT)]
            hold(("merged", half), pr.pe.now())

            def save():
                for split in splits:
                    split()
                if (j + 1) * BLK < D:
                    others(j + 1)
            return save
        return drain

    others(0)
    for j in range(D // BLK):
        block(weight_at(i["w_gla_branch"][0], j * BLK, BLK), 0, KT, BLK, gla_branch_drain(j))
    stepped()

    junk = stage[:, :, :, :].rearrange("p a t n -> p (a t n)")

    def sum_up(j, added):
        for t in range(NT):
            A(act.activation, junk[:, t * BLK:(t + 1) * BLK], total[:, t, j * BLK:(j + 1) * BLK], ACT.Copy,
              accum_out=parts[:, t, j:j + 1], after=(added, pr.act.now()))

    for j in range(D // BLK):
        if j == 1:
            wait(pe, pr.dve.now())
        block(weight_at(i["w_out"][0], j * BLK, BLK), KT, KT, BLK, to_sum(total, True, sum_up)(j))
    drained()

    def layer_norm():
        y = Room(work_at)(NT, D)
        m = V(dve.tensor_reduce, flat(shift), parts, AX, ALU.add, after=(pr.act.now(), pr.pe.now()))
        m = V(dve.tensor_scalar, flat(shift), flat(shift), -1.0 / D, None, ALU.mult, after=(m,))
        m_sq, m_y = [], []
        for t in range(NT):
            m_sq.append(A(act.activation, junk, total[:, t, :], ACT.Square, bias=shift[:, t, :],
                          accum_out=spread[:, t, :], after=(m, pr.act.now())))
            m_y.append(V(dve.scalar_tensor_tensor, y[:, t, :], total[:, t, :], shift[:, t, :], ln_g, ALU.add,
                         ALU.mult, after=(m,)))
        marks = {}
        for t in range(NT):
            m = inverse_root(spread[:, t, :], spread[:, t, :], D, 1e-5, m_sq[t])
            for k in range(0, KT, 4):
                some = slice(k * P, (k + 4) * P)
                marks[t, k] = V(dve.scalar_tensor_tensor, total[:, t, some], y[:, t, some], spread[:, t, :],
                                ln_b[:, some], ALU.mult, ALU.add, after=(m, m_y[t]))
        return marks

    marks = layer_norm()
    transpose_all(total, 0, lambda t, k: marks[t, k])

    hid = Room(work_at)(2, NT, BLK)

    def to_hidden(j):
        def drain(half, n):
            free(dve, ("hid", half))
            wait(dve, summed())
            for t in range(NT):
                b = bank[2 * half + t][:, 0:n]
                m1 = V(dve.tensor_scalar, hid[:, half, t, :], b, 0.0, None, ALU.max)
                wait(dve, m1)
                last = dve.tensor_tensor(hid[:, half, t, :], hid[:, half, t, :], b, ALU.mult)
            full = s_drv.up(last)
            splits = [turn4(hid[:, half, t, :], KT + 4 * j, t, full, unread=summed()) for t in range(NT)]
            hold(("hid", half), pr.pe.now())
            return lambda: [split() for split in splits]
        return drain

    def down(f, j):
        w = i["w_down"][0].rearrange("(f k p) n -> p f k n", p=P, k=KT)

        def get(q):
            if (j, q) == (1, 0):
                wait(pe, pr.dve.now())
            if isinstance(f, int):
                return w[:, f, q * QK:(q + 1) * QK, j * BLK:(j + 1) * BLK]
            return w[:, ds(sp.snap(f), 1), q * QK:(q + 1) * QK, j * BLK:(j + 1) * BLK].rearrange("p a k n -> p (a k) n")
        return get

    def mlp_turn(f, then=None):
        for j in range(D // BLK):
            block(weight_at(i["w_up"][0], f * D + j * BLK, BLK), 0, KT, BLK, to_hidden(j))
        for j in range(D // BLK):
            block(down(f, j), KT, KT, BLK, to_sum(total, True, then)(j))

    beside(sum_begins(None, i["ln2_g"][0], i["ln2_b"][0], pr.pe.now(), pr.dve.now()))
    mlp_turn(0)
    stepped()
    last_sum = to_sum(total, True)(D // BLK - 1)
    with pr.loop(FF // D - 2, apart=False, carry=True) as f:
        again(last_sum)
        mlp_turn(f + 1)
    again(last_sum)
    mlp_turn(FF // D - 1, sum_up)
    drained()
    marks = layer_norm()
    for t in range(NT):
        stored = store(rows(out[0])[:, t, :], total[:, t, :], *[marks[t, k] for k in range(0, KT, 4)])

    with pr.loop(LAYERS) as l:
        aligned()
        def row2(w, n):
            return w.rearrange("(a l) n -> a (l n)", a=1)[:, ds(l * n, n)].partition_broadcast(P)

        def weight2(w, row_tiles, col, n, start=0):
            w = w.rearrange("l (k p) n -> p (l k) n", p=P)
            kts = min(QK, row_tiles)

            def get(q):
                first = sp.snap(l * row_tiles + (start + q * kts))
                c = col if isinstance(col, int) else sp.snap(col)
                return w[:, ds(first, kts), ds(c, n)]
            return get

        room = Room(NT * D)
        hn, grow, ssq = room(NT, D), room(D), room(2, 1)
        loaded = load(grow, row2(i["norm_pre_2"], D))
        m_sq = [A(act.activation, hn[:, t, :], total[:, t, :], ACT.Square, accum_out=ssq[:, t, :]) for t in range(NT)]
        marks = {}
        for t in range(NT):
            m = inverse_root(ssq[:, t, :], ssq[:, t, :], D, 1e-6, m_sq[t])
            for k in range(0, KT, 4):
                some = slice(k * P, (k + 4) * P)
                marks[t, k] = V(dve.scalar_tensor_tensor, hn[:, t, some], total[:, t, some], ssq[:, t, :],
                                grow[:, some], ALU.mult, ALU.mult, after=(m, loaded))
        transpose_all(hn, 0, lambda t, k: marks[t, k])

        def into(col, n=BLK):
            block(weight2(i["w_in_2"], KT, col, n), 0, KT, n, to_dram(proj2, col)(0))

        into(0)
        into(C2_CKV, B_KVL + B_ROPE)
        into(C2_CQ)
        for j in (1, 2):
            into(j * BLK)

        pr.meet()
        room = Room(NT * D)
        small = room(6, 8)
        work_at = room.at
        DR = 2 * ROWS - 1
        DC = 2 * WIN_C - 1
        edge = room(P)
        m = V(dve.memset, edge, 0.0)
        rpb = i["c_rpb_2"].rearrange("l h a b -> (l h) a b")
        for hh in range(C_H):
            loaded = load(edge[hh * DR:(hh + 1) * DR, GRID - WIN_C:GRID - WIN_C + DC],
                          rpb[ds(l * C_H + hh, 1), WIN_R - ROWS:WIN_R - ROWS + DR, :].rearrange("a r c -> (a r) c"), m)
        skewed = store(skew, wide(edge[0:C_H * DR, :].unsqueeze(1), [C_H * DR, GRID, P]), loaded)
        wait(act, skewed)

        def idle(pieces):
            for _ in range(pieces):
                yield

        UW = UNIT_H * HD

        def rope(x, heads, n, cos, sin, tmp, *after):
            q4 = n // 4
            split = lambda a: a.rearrange("p h (b s e) -> p h b s e", b=2, s=2)
            xs, ts = split(x), split(tmp)
            ss = sin.rearrange("p (b s e) -> p b s e", b=2, s=2)
            for s in range(2):
                for hh in range(heads):
                    m = V(dve.tensor_tensor, ts[:, hh, :, s, :], xs[:, hh, :, 1 - s, :], ss[:, :, s, :], ALU.mult,
                          after=after)
            m2 = V(dve.tensor_tensor, x, x, wide(cos.unsqueeze(1), [P, heads, n]), ALU.mult, after=(m,))
            return V(dve.tensor_tensor, x, x, tmp, ALU.add, after=(m2,))

        def head_norm(x, n, g, stat, tmp, *after):
            m = V(dve.tensor_tensor, tmp, x, x, ALU.mult, after=after)
            m = V(dve.tensor_reduce, stat, tmp, AX, ALU.add, after=(m,))
            m = inverse_root(stat, stat, HD, 1e-6, m)
            m = V(dve.tensor_tensor, x, x, wide(stat.unsqueeze(2), [P, n, HD]), ALU.mult, after=(m,))
            return V(dve.tensor_tensor, x, x, wide(g.unsqueeze(1), [P, n, HD]), ALU.mult, after=(m,))

        def turn_heads(to, source, banks, width, *after):
            heads = to.shape[1]
            copies = []
            for hh in range(heads):
                b = bank[banks[hh // 2]]
                for t in range(NT):
                    m = T(pe.transpose, b[0:width, (hh % 2) * S + t * P:(hh % 2) * S + (t + 1) * P],
                          source(hh, t), ident[:, :], after=after)
                if hh % 2 or hh == heads - 1:
                    n = hh % 2 + 1
                    copies.append((to[0:width, hh - n + 1:hh + 1, :],
                                   b[0:width, 0:n * S].rearrange("p (h n) -> p h n", h=n), m))

            def out_of_banks():
                for dst, src, m in copies:
                    m = A(act.activation, dst, src, ACT.Copy, after=(m,))
                return m
            return out_of_banks

        def attend(parts, value, probs, pt, scale, bias, gate, load_gate, x0, *after, unread=None):
            m_sc = []
            for t in range(NT):
                tok = slice(t * P, (t + 1) * P)
                for hh in range(UNIT_H):
                    o_ = bank[4 + 2 * t + hh // 2][:, (hh % 2) * S:(hh % 2 + 1) * S]
                    for n, (qf, kf) in enumerate(parts):
                        m = T(pe.matmul, o_, qf(hh)[:, tok], kf(hh), start=(n == 0), stop=(n == len(parts) - 1),
                              after=after)
                m_sc.append(m)
            m_gate = load_gate()
            yield

            def softmax(t):
                m, pb = m_sc[t], probs[t]
                top, tot = small[:, t, 0:4], small[:, 2 + t, 0:4]
                for n in range(2):
                    sc = bank[4 + 2 * t + n][:, :].rearrange("p (h n) -> p h n", h=2)
                    if bias is not None:
                        ms = V(dve.scalar_tensor_tensor, pb[:, 2 * n:2 * n + 2, :], sc, scale,
                               bias[:, t, 2 * n:2 * n + 2, :], ALU.mult, ALU.add, after=(m_sc[1],))
                        ms = V(dve.tensor_reduce, top[:, 2 * n:2 * n + 2], pb[:, 2 * n:2 * n + 2, :], AX, ALU.max,
                               after=(ms,))
                    else:
                        ms = V(dve.tensor_reduce, top[:, 2 * n:2 * n + 2], sc, AX, ALU.max, after=(m,))
                sf = 1.0 if bias is not None else scale
                ms = V(dve.tensor_scalar, top, top, -sf, None, ALU.mult, after=(ms,))
                for hh in range(UNIT_H):
                    src = (pb[:, hh, :] if bias is not None
                           else bank[4 + 2 * t + hh // 2][:, (hh % 2) * S:(hh % 2 + 1) * S])
                    me = A(act.activation, pb[:, hh, :], src, ACT.Exp, bias=top[:, hh:hh + 1], scale=sf,
                           accum_out=tot[:, hh:hh + 1], after=(ms, m_sc[1]))
                return me, V(dve.reciprocal, tot, tot, after=(me,))

            def turn_probs(t, *after):
                for hh in range(UNIT_H):
                    for kt in range(NT):
                        m = T(pe.transpose, bank[4 + hh // 2][:, ((hh % 2) * NT + kt) * P:((hh % 2) * NT + kt + 1) * P],
                              probs[t][:, hh, kt * P:(kt + 1) * P], ident[:, :], after=after)
                return m

            def take_probs(*after):
                for n in range(2):
                    m = A(act.activation, pt[:, 2 * n:2 * n + 2, :],
                          bank[4 + n][:, :].rearrange("p (h n) -> p h n", h=2), ACT.Copy, after=after)
                return m

            def times_values(t, *after):
                for hh in range(UNIT_H):
                    for kt in range(NT):
                        m = T(pe.matmul, bank[6 + t][:, hh * HD:(hh + 1) * HD], pt[:, hh, kt * P:(kt + 1) * P],
                              value(hh, kt), start=(kt == 0), stop=(kt == NT - 1), after=after)
                return m

            def gates(t, *after):
                m = A(act.activation, gate[:, t, :], gate[:, t, :], ACT.Silu, after=(m_gate,))
                g = gate[:, t, :].rearrange("p (h n) -> p h n", h=UNIT_H)
                return V(dve.tensor_tensor, g, g, wide(small[:, 2 + t, 0:4].unsqueeze(2), [P, UNIT_H, HD]), ALU.mult,
                         after=(m, *after))

            me, mr = softmax(0)
            yield
            me1, mr1 = softmax(1)
            m_tp = turn_probs(0, me)
            mg = gates(0, mr)
            yield
            m_pt = take_probs(m_tp)
            m_v = times_values(0, m_pt, me1)
            m_tp = turn_probs(1, m_pt, me1)
            mg1 = gates(1, mr1)
            yield
            m_pt = take_probs(m_tp, m_v)
            m_v1 = times_values(1, m_pt)
            m0 = V(dve.tensor_tensor, gate[:, 0, :], gate[:, 0, :], bank[6][:, :], ALU.mult, after=(m_v, mg))
            yield
            m1 = V(dve.tensor_tensor, gate[:, 1, :], gate[:, 1, :], bank[7][:, :], ALU.mult, after=(m_v1, mg1))
            splits = [turn4(gate[:, t, :], x0, t, m0, m1, unread=unread) for t in range(NT)]
            yield
            for split in splits:
                split()

        heads_of = lambda a: a.rearrange("p t (h n) -> p (t h) n", n=HD)
        four = lambda a: a.rearrange("p a n -> p (a n)")[:, 0:UNIT_H * S].rearrange("p (h n) -> p h n", h=UNIT_H)
        p2 = rows(proj2)
        old = s_mm.now()

        def grouped_unit(unit):
            pr.meet()
            wait(act, s_st[0].now(), s_st[1].now())
            room = Room(work_at)
            q, k, v, gt2 = room(NT, UW), room(NT, HD), room(NT, HD), room(NT, UW)
            qt, kt_, pt = room(UNIT_H, S), room(1, S), room(UNIT_H, S)
            tmp, tmp2 = room(NT, UW), room(NT, UW)
            gq, gk2, cos, sin = room(HD), room(HD), room(NT, HD), room(NT, HD)
            load(q, p2[:, :, C2_AQ + unit * UW:C2_AQ + (unit + 1) * UW])
            load(k, p2[:, :, C2_AK + unit * HD:C2_AK + (unit + 1) * HD])
            load(v, p2[:, :, C2_AV + unit * HD:C2_AV + (unit + 1) * HD])
            load(gq, row2(i["a_q_norm_2"], HD))
            load(gk2, row2(i["a_k_norm_2"], HD))
            load(cos, rows(i["cos128"]))
            m_in = load(sin, rows(i["sin128"]))
            yield
            mq = head_norm(heads_of(q), NT * UNIT_H, gq, small[:, 4, :], heads_of(tmp), m_in)
            mk = head_norm(k, NT, gk2, small[:, 5, 0:2], tmp2[:, :, 0:HD], m_in)
            yield
            for t in range(NT):
                mq = rope(q[:, t, :].rearrange("p (h n) -> p h n", n=HD), UNIT_H, HD, cos[:, t, :], sin[:, t, :],
                          tmp[:, t, :].rearrange("p (h n) -> p h n", n=HD), mq)
                mk = rope(k[:, t:t + 1, :], 1, HD, cos[:, t, :], sin[:, t, :], tmp2[:, t:t + 1, 0:HD], mk)
            yield
            q_out = turn_heads(qt, lambda h, t: q[:, t, h * HD:(h + 1) * HD], (4, 5), HD, mq)
            k_out = turn_heads(kt_, lambda h, t: k[:, t, :], (6,), HD, mk)
            yield
            m1, m2 = q_out(), k_out()
            yield from attend([(lambda h: qt[:, h, :], lambda h: kt_[:, 0, :])], lambda h, kt: v[:, kt, :],
                              [four(tmp), four(tmp2)], pt, HD ** -0.5, None, gt2,
                              lambda: load(gt2, p2[:, :, C2_AG + unit * UW:C2_AG + (unit + 1) * UW],
                                           s_st[0].now(), s_st[1].now(), count=d_gate),
                              KT + 4 * unit, m1, m2, unread=old)

        def latents():
            yield from idle(AHEAD)
            pr.meet()
            room = Room(work_at)
            cq, ckv = room(NT, B_QL), room(NT, B_KVL)
            gq, gkv, sq = room(B_QL), room(B_KVL), room(4, 1)
            junk = room(B_QL)
            wait(act, s_st[0].now(), s_st[1].now())
            load(cq, p2[:, :, C2_CQ:C2_CQ + B_QL])
            load(ckv, p2[:, :, C2_CKV:C2_CKV + B_KVL])
            load(gq, row2(i["b_q_norm_2"], B_QL))
            loaded = load(gkv, row2(i["b_kv_norm_2"], B_KVL))
            yield
            ma = None
            for n, (x, g, w, tiles) in enumerate(((cq, gq, B_QL, 4), (ckv, gkv, B_KVL, 2))):
                splits = []
                for t in range(NT):
                    s = sq[:, 2 * n + t, :]
                    ma = A(act.activation, junk[:, 0:w], x[:, t, :], ACT.Square, accum_out=s, after=(loaded, ma))
                    m = inverse_root(s, s, w, 1e-6, ma)
                    m = V(dve.scalar_tensor_tensor, x[:, t, :], x[:, t, :], s, g, ALU.mult, ALU.mult, after=(m,))
                    splits.append(turn4(x[:, t, :], KT + 8 + 4 * n, t, m, tiles=tiles, unread=old))
                yield
                for split in splits:
                    m = split()
            wait(pe, m)
            at["latents"] = True
            yield from idle(2 * AHEAD)

        def latent_unit():
            yield from idle(2 * AHEAD)
            pr.meet()
            wait(act, s_st[0].now(), s_st[1].now())
            unread = s_mm.now()
            room = Room(work_at)
            QW = HD + B_ROPE
            q, kv, kr = room(NT, B_H * QW), room(NT, B_H * 2 * HD), room(NT, B_ROPE)
            cos, sin = room(NT, B_ROPE), room(NT, B_ROPE)
            qt, kt_, pt = room(B_H, S), room(B_H, S), room(UNIT_H, S)
            qpe, kpe = room(B_H, S), room(1, S)
            tmp = room(B_H, B_ROPE)
            gt2 = room(NT, UW)
            lat = rows(latent)
            load(q, lat[:, :, 0:B_H * QW])
            load(kv, lat[:, :, 2 * BLK:4 * BLK])
            load(kr, p2[:, :, C2_KR:C2_KR + B_ROPE])
            load(cos, rows(i["cos64"]))
            m_in = load(sin, rows(i["sin64"]))
            yield
            m = m_in
            for t in range(NT):
                m = rope(q[:, t, :].rearrange("p (h n) -> p h n", n=QW)[:, :, HD:QW], B_H, B_ROPE, cos[:, t, :],
                         sin[:, t, :], tmp, m)
                m = rope(kr[:, t:t + 1, :], 1, B_ROPE, cos[:, t, :], sin[:, t, :], tmp[:, 0:1, :], m)
            yield
            q_out = turn_heads(qt, lambda h, t: q[:, t, h * QW:h * QW + HD], (4, 5), HD, m)
            k_out = turn_heads(kpe, lambda h, t: kr[:, t, :], (6,), B_ROPE)
            yield
            mq, mk = q_out(), k_out()
            k_out = turn_heads(kt_, lambda h, t: kv[:, t, h * 2 * HD:h * 2 * HD + HD], (6, 7), HD, mq, mk)
            q_out = turn_heads(qpe, lambda h, t: q[:, t, h * QW + HD:(h + 1) * QW], (4, 5), B_ROPE)
            yield
            m1, m2 = q_out(), k_out()
            yield from attend([(lambda h: qt[:, h, :], lambda h: kt_[:, h, :]),
                               (lambda h: qpe[0:B_ROPE, h, :], lambda h: kpe[0:B_ROPE, 0, :])],
                              lambda h, kt: kv[:, kt, h * 2 * HD + HD:(h + 1) * 2 * HD],
                              [four(qt), four(kt_)], pt, QW ** -0.5, None, gt2,
                              lambda: load(gt2, p2[:, :, C2_BG:C2_BG + UW], s_st[0].now(), s_st[1].now(),
                                           count=d_gate),
                              KT + A_H, m1, m2, unread=unread)

        def neighbour_unit():
            yield from idle(2 * AHEAD)
            pr.meet()
            wait(act, s_st[0].now(), s_st[1].now())
            unread = s_mm.now()
            room = Room(work_at)
            q, k, v, gt2 = room(NT, UW), room(NT, UW), room(NT, UW), room(NT, UW)
            qt, kt_, pt = room(C_H, S), room(C_H, S), room(UNIT_H, S)
            bias, mask = room(NT, C_H * S), room(NT, S)
            load(q, p2[:, :, C2_Q:C2_Q + UW])
            load(k, p2[:, :, C2_K:C2_K + UW])
            m_in = load(v, p2[:, :, C2_V:C2_V + UW])
            load(mask, rows(i["window"]), count=d_late)
            for r in range(ROWS):
                part = slice((r % 2) * GRID, (r % 2 + 1) * GRID)
                for hh in range(C_H):
                    m_bias = load(bias[part, r // 2, hh * S:(hh + 1) * S].rearrange("p (a b) -> p a b", a=ROWS),
                                  bass.AP(skew.tensor, (hh * DR + ROWS - 1 - r) * GRID * P + GRID - 1,
                                          [[P - 1, GRID], [GRID * P, ROWS], [1, GRID]]), count=d_late)
            yield
            q_out = turn_heads(qt, lambda h, t: q[:, t, h * HD:(h + 1) * HD], (4, 5), HD, m_in)
            k_out = turn_heads(kt_, lambda h, t: k[:, t, h * HD:(h + 1) * HD], (6, 7), HD, m_in)
            yield
            for t in range(NT):
                bt = bias[:, t, :].rearrange("p (h n) -> p h n", h=C_H)
                mb = V(dve.tensor_tensor, bt, bt, wide(mask[:, t, :].unsqueeze(1), [P, C_H, S]), ALU.add,
                       after=(m_bias,))
            m1, m2 = q_out(), k_out()
            yield from attend([(lambda h: qt[:, h, :], lambda h: kt_[:, h, :])],
                              lambda h, kt: v[:, kt, h * HD:(h + 1) * HD], [four(q), four(k)],
                              pt, HD ** -0.5, bias.rearrange("p t (h n) -> p t h n", h=C_H), gt2,
                              lambda: load(gt2, p2[:, :, C2_G:C2_G + UW], count=d_gate),
                              KT + A_H + B_H, m1, m2, mb, unread=unread)

        at["latents"] = False
        beside(chain(latents(), *[grouped_unit(unit) for unit in range(A_KV)]), 1)
        into(3 * BLK)
        into(4 * BLK)
        assert at["latents"]
        for col, n in ((0, BLK), (BLK, B_H * (HD + B_ROPE) - BLK)):
            block(weight2(i["b_w_uq_2"], B_QL // P, col, n), KT + 8, B_QL // P, n, to_dram(latent, col)(0))
        for col in (0, BLK):
            block(weight2(i["b_w_ukv_2"], B_KVL // P, col, BLK), KT + 12, B_KVL // P, BLK,
                  to_dram(latent, 2 * BLK + col)(0))
        later = [C2_BG + j * BLK for j in range((N_IN2 - C2_BG) // BLK)]
        for col in later[:2]:
            into(col)
        ended()
        beside(latent_unit(), 1)
        for col in later[2:]:
            into(col)
        ended()

        beside(neighbour_unit(), 1)
        first = A_H + B_H
        for j in range(D // BLK):
            block(weight2(i["w_out_2"], KT, j * BLK, BLK), KT, first, BLK, to_sum(total, False)(j))
        ended()
        pr.meet()
        room = Room(NT * D)
        xr, grow, sq2 = room(NT, D), room(D), room(NT, D // BLK)
        root = room(2, 1)
        load(xr, rows(out[0]), d_out.now())
        loaded = load(grow, row2(i["norm_post_2"], D))
        squared = {}

        def times_gain(j):
            for t in range(NT):
                part = total[:, t, j * BLK:(j + 1) * BLK]
                m = V(dve.tensor_tensor, part, part, grow[:, j * BLK:(j + 1) * BLK], ALU.mult, after=squared[j])
            return m

        def squares(j, added):
            squared[j] = [A(act.activation, junk[:, t * BLK:(t + 1) * BLK], total[:, t, j * BLK:(j + 1) * BLK],
                            ACT.Square, accum_out=sq2[:, t, j:j + 1], after=(added, pr.act.now()))
                          for t in range(NT)] + [loaded]
            if j:
                times_gain(j - 1)

        wait(act, s_st[0].now(), s_st[1].now())
        for j in range(D // BLK):
            block(weight2(i["w_out_2"], KT, j * BLK, BLK, first), KT + first, KT - first, BLK,
                  to_sum(total, True, squares)(j))
        drained()

        m = V(dve.tensor_reduce, flat(root), sq2, AX, ALU.add, after=squared[D // BLK - 1])
        m = inverse_root(flat(root), flat(root), D, 1e-6, m)
        mg = times_gain(D // BLK - 1)
        for t in range(NT):
            mt = V(dve.scalar_tensor_tensor, total[:, t, :], total[:, t, :], root[:, t, :], xr[:, t, :], ALU.mult,
                   ALU.add, after=(m, mg))
            store(rows(out[0])[:, t, :], total[:, t, :], mt)

    return finish(pr)


def finish(pr):
    pr.wait(pr.nc.scalar, pr.counts["d_out"].now(), pr.counts["s_st0"].now(), pr.counts["s_st1"].now())
    return pr.found


def constants():
    j, t = np.arange(P)[:, None], np.arange(P)[None, :]
    same = (j // GLA_C) == (t // GLA_C)
    most = np.where((j % GLA_C) <= np.arange(GLA_C)[None, :], np.finfo(np.float32).max, 0.0)
    c = {"most64": most, "least64": -most, "identity": j == t, "causal": j <= t, "causal64": (j <= t) & same, "blocks64": same,
         "columns64": (np.arange(P)[:, None] // GLA_C) == np.arange(2)[None, :]}
    tok = np.arange(S)
    for n, name in ((HD, "128"), (B_ROPE, "64")):
        half = n // 2
        freq = (np.float32(1.0) / (np.float32(10000.0) ** (np.arange(0, half, 2, dtype=np.float32) / np.float32(half)))).astype(np.float32)
        parts_c, parts_s = [], []
        for pos in (tok // GRID, tok % GRID):
            ang = pos.astype(np.float32)[:, None] * freq[None, :]
            parts_c += [np.cos(ang), np.cos(ang)]
            parts_s += [-np.sin(ang), np.sin(ang)]
        c["cos" + name], c["sin" + name] = np.concatenate(parts_c, 1), np.concatenate(parts_s, 1)
    col = tok % GRID
    first = np.clip(col - WIN_C // 2, 0, GRID - WIN_C)[:, None]
    c["window"] = np.where((col[None, :] >= first) & (col[None, :] < first + WIN_C), 0.0, MASKED)
    return {k: np.ascontiguousarray(v, dtype=np.float32) for k, v in c.items()}


def conv_layout(w, b):
    both = np.concatenate([w[0], b], axis=0)
    x, bc = both[:, :SSD_IN], both[:, SSD_IN:]
    x = x.reshape(CONV_W + 1, SSD_G, CONV_T - 2, P)
    bc = bc.reshape(CONV_W + 1, 2, SSD_G, P).transpose(0, 2, 1, 3)
    both = np.concatenate([x, bc], axis=2)
    return np.ascontiguousarray(both.transpose(1, 3, 2, 0).reshape(SSD_G, P, CONV_T * (CONV_W + 1)))


def build(nc, shapes, out_shape, debug=None):
    def one(nc, gains):
        i = {n: nc.dram_tensor(f"in_{n}", s, F32, kind="ExternalInput").ap() for n, s in shapes.items()}
        out = nc.dram_tensor("out", out_shape, F32, kind="ExternalOutput").ap()
        with ExitStack() as ctx:
            return emit(nc, ctx, gains, i, out, debug)
    return one


def kernel(**inputs):
    import concourse.bacc as bacc
    from concourse.bass_utils import run_bass_kernel_spmd

    arrays = {n: np.ascontiguousarray(a) for n, a in inputs.items() if n not in ("ssd_conv_w", "ssd_conv_b")}
    arrays["conv"] = conv_layout(np.asarray(inputs["ssd_conv_w"]), np.asarray(inputs["ssd_conv_b"]))
    arrays.update(constants())
    shapes = {n: a.shape for n, a in arrays.items()}
    one = build(None, shapes, (1, S, D))
    gains = one(bacc.Bacc("TRN2", target_bir_lowering=False, num_devices=1), {})
    nc = bacc.Bacc("TRN2", target_bir_lowering=False, num_devices=1)
    one(nc, gains)
    r = run_bass_kernel_spmd(nc, [{f"in_{n}": a for n, a in arrays.items()}], core_ids=[0])
    return r.results[0]["out"]
```
